# Optimizing a Trainium2 kernel written in Bass

```python
import math
import jax, jax.numpy as jnp
from jax import lax
import numpy as np
import jax
import jax.numpy as jnp

D_MODEL = 1024
BATCH = 1
SEQ = 256
DEPTH = 2

N_MIXERS = 2
N_SSD_LAYERS = (DEPTH + N_MIXERS - 1) // N_MIXERS
N_LRU_LAYERS = DEPTH // N_MIXERS
SSD_EXPAND = 2
SSD_D_INNER = SSD_EXPAND * D_MODEL
SSD_HEADDIM = 64
SSD_HEADS = SSD_D_INNER // SSD_HEADDIM
SSD_GROUPS = 4
SSD_HPG = SSD_HEADS // SSD_GROUPS
SSD_D_STATE = 128
SSD_CONV = 4
SSD_CHUNK = 128
SSD_CONV_DIM = SSD_D_INNER + 2 * SSD_GROUPS * SSD_D_STATE
SSD_IN_DIM = SSD_D_INNER + SSD_CONV_DIM + SSD_HEADS
LRU_WIDTH = 1280
LRU_HEADS = 10
LRU_BLOCK = LRU_WIDTH // LRU_HEADS
LRU_CONV = 4
LRU_C = 8.0
D_FF = 4 * D_MODEL
FFN_CONV = 3
EPS = 1e-6


def rmsnorm(x, w):
    xf = x.astype(jnp.float32)
    y = xf * lax.rsqrt(jnp.mean(xf * xf, axis=-1, keepdims=True) + EPS)
    return (y * w.astype(jnp.float32)).astype(x.dtype)

def causal_dwconv(x, w, b):
    k = w.shape[0]
    s = x.shape[1]
    xp = jnp.pad(x, ((0, 0), (k - 1, 0), (0, 0)))
    y = b
    for j in range(k):
        y = y + xp[:, j:j + s, :] * w[j]
    return y

def ssd_chunked_scan(xh, dt, a, bm, cm):
    bsz, s, h, p = xh.shape
    nc = s // SSD_CHUNK
    xdt = (xh * dt[..., None]).reshape(bsz, nc, SSD_CHUNK, SSD_GROUPS, SSD_HPG, p)
    da = (dt * a).reshape(bsz, nc, SSD_CHUNK, SSD_GROUPS, SSD_HPG)
    bc = bm.reshape(bsz, nc, SSD_CHUNK, SSD_GROUPS, SSD_D_STATE)
    cc = cm.reshape(bsz, nc, SSD_CHUNK, SSD_GROUPS, SSD_D_STATE)
    cs = jnp.moveaxis(jnp.cumsum(da, axis=2), 2, -1)
    tri = jnp.tril(jnp.ones((SSD_CHUNK, SSD_CHUNK), dtype=bool))
    decay_in = jnp.exp(jnp.where(tri, cs[..., :, None] - cs[..., None, :], -jnp.inf))
    cb = jnp.einsum('bclgn,bcsgn->bcgls', cc, bc)
    scores = cb[:, :, :, None] * decay_in
    y_diag = jnp.einsum('bcgels,bcsgep->bclgep', scores, xdt)
    decay_out = jnp.moveaxis(jnp.exp(cs[..., -1:] - cs), -1, 2)
    states = jnp.einsum('bclgn,bclgep->bcgepn', bc, xdt * decay_out[..., None])
    tot = cs[..., -1]
    inc = jnp.moveaxis(jnp.cumsum(tot, axis=1), 1, -1)
    exc = inc - jnp.moveaxis(tot, 1, -1)
    stri = jnp.tril(jnp.ones((nc, nc), dtype=bool), -1)
    decay_chunk = jnp.exp(jnp.where(stri, exc[..., :, None] - inc[..., None, :], -jnp.inf))
    entering = jnp.einsum('bgezc,bcgepn->bzgepn', decay_chunk, states)
    state_decay = jnp.moveaxis(jnp.exp(cs), -1, 2)
    y_off = jnp.einsum('bclgn,bcgepn->bclgep', cc, entering) * state_decay[..., None]
    return (y_diag + y_off).reshape(bsz, s, h, p)

def gated_group_rmsnorm(y, z, w):
    bsz, s, d = y.shape
    g = (y * jax.nn.silu(z.astype(jnp.float32))).reshape(bsz, s, SSD_GROUPS, d // SSD_GROUPS)
    g = g * lax.rsqrt(jnp.mean(g * g, axis=-1, keepdims=True) + EPS)
    return g.reshape(bsz, s, d) * w.astype(jnp.float32)

def ssd_mixer(u, w_in, conv_w, conv_b, dt_bias, a_log, d_skip, norm_w, w_out):
    bsz, s, _ = u.shape
    proj = u @ w_in
    z = proj[..., :SSD_D_INNER]
    xbc = proj[..., SSD_D_INNER:SSD_D_INNER + SSD_CONV_DIM]
    dt_raw = proj[..., SSD_D_INNER + SSD_CONV_DIM:]
    xbc = jax.nn.silu(causal_dwconv(xbc, conv_w, conv_b)).astype(jnp.float32)
    xs = xbc[..., :SSD_D_INNER].reshape(bsz, s, SSD_HEADS, SSD_HEADDIM)
    bm = xbc[..., SSD_D_INNER:SSD_D_INNER + SSD_GROUPS * SSD_D_STATE].reshape(bsz, s, SSD_GROUPS, SSD_D_STATE)
    cm = xbc[..., SSD_D_INNER + SSD_GROUPS * SSD_D_STATE:].reshape(bsz, s, SSD_GROUPS, SSD_D_STATE)
    dt = jax.nn.softplus(dt_raw.astype(jnp.float32) + dt_bias.astype(jnp.float32))
    a = -jnp.exp(a_log.astype(jnp.float32))
    y = ssd_chunked_scan(xs, dt, a, bm, cm)
    y = y + d_skip.astype(jnp.float32)[:, None] * xs
    y = gated_group_rmsnorm(y.reshape(bsz, s, SSD_D_INNER), z, norm_w)
    return (y.astype(u.dtype) @ w_out).astype(u.dtype)

def _linear_combine(c1, c2):
    a1, b1 = c1
    a2, b2 = c2
    return a1 * a2, a2 * b1 + b2

def rglru_mixer(u, w_in, b_in, conv_w, conv_b, w_gx, b_gx, w_ga, b_ga, lam, w_out, b_out):
    bsz, s, _ = u.shape
    proj = u @ w_in + b_in
    ybr = jax.nn.gelu(proj[..., :LRU_WIDTH].astype(jnp.float32))
    xbr = causal_dwconv(proj[..., LRU_WIDTH:], conv_w, conv_b)
    xh = xbr.reshape(bsz, s, LRU_HEADS, LRU_BLOCK)
    gx = jax.nn.sigmoid((jnp.einsum('bshi,hij->bshj', xh, w_gx).reshape(bsz, s, LRU_WIDTH) + b_gx).astype(jnp.float32))
    ga = jax.nn.sigmoid((jnp.einsum('bshi,hij->bshj', xh, w_ga).reshape(bsz, s, LRU_WIDTH) + b_ga).astype(jnp.float32))
    log_a = LRU_C * ga * jax.nn.log_sigmoid(lam.astype(jnp.float32))
    a_t = jnp.exp(log_a)
    mult = jnp.sqrt(-jnp.expm1(2.0 * log_a))
    b_t = mult * gx * xbr.astype(jnp.float32)
    _, h = lax.associative_scan(_linear_combine, (a_t, b_t), axis=1)
    out = (h * ybr).astype(u.dtype) @ w_out + b_out
    return out.astype(u.dtype)

def conv_ffn(u, w_up, conv_w, conv_b, w_down):
    hcv = causal_dwconv(u @ w_up, conv_w, conv_b)
    g = hcv[..., :D_FF]
    v = hcv[..., D_FF:]
    return ((jax.nn.gelu(g.astype(jnp.float32)) * v.astype(jnp.float32)).astype(u.dtype) @ w_down).astype(u.dtype)

def first_inputs(seed: int = 0) -> dict:
    key = jax.random.key(seed)
    ks = jax.random.split(key, 32)
    f32 = jnp.float32

    def nrm(k, shape, scale):
        return scale * jax.random.normal(k, shape, f32)

    def gain(k, shape):
        return 1.0 + 0.1 * jax.random.normal(k, shape, f32)

    na, nb = N_SSD_LAYERS, N_LRU_LAYERS
    dt0 = jnp.exp(jax.random.uniform(ks[9], (na, SSD_HEADS), f32, math.log(1e-3), math.log(1e-1)))
    lam_u = jax.random.uniform(ks[20], (nb, LRU_WIDTH), f32, 0.9, 0.999)
    return {
        'x': jax.random.normal(ks[0], (BATCH, SEQ, D_MODEL), f32),
        'norm_mix_pre': gain(ks[1], (DEPTH, D_MODEL)),
        'norm_mix_post': gain(ks[2], (DEPTH, D_MODEL)),
        'norm_ffn_pre': gain(ks[3], (DEPTH, D_MODEL)),
        'norm_ffn_post': gain(ks[4], (DEPTH, D_MODEL)),
        'ssd_w_in': nrm(ks[5], (na, D_MODEL, SSD_IN_DIM), D_MODEL ** -0.5),
        'ssd_conv_w': nrm(ks[6], (na, SSD_CONV, SSD_CONV_DIM), SSD_CONV ** -0.5),
        'ssd_conv_b': nrm(ks[7], (na, SSD_CONV_DIM), 0.01),
        'ssd_dt_bias': dt0 + jnp.log(-jnp.expm1(-dt0)),
        'ssd_a_log': jnp.log(jax.random.uniform(ks[10], (na, SSD_HEADS), f32, 1.0, 16.0)),
        'ssd_d': gain(ks[11], (na, SSD_HEADS)),
        'ssd_norm': gain(ks[12], (na, SSD_D_INNER)),
        'ssd_w_out': nrm(ks[13], (na, SSD_D_INNER, D_MODEL), SSD_D_INNER ** -0.5),
        'lru_w_in': nrm(ks[14], (nb, D_MODEL, 2 * LRU_WIDTH), D_MODEL ** -0.5),
        'lru_b_in': nrm(ks[15], (nb, 2 * LRU_WIDTH), 0.01),
        'lru_conv_w': nrm(ks[16], (nb, LRU_CONV, LRU_WIDTH), LRU_CONV ** -0.5),
        'lru_conv_b': nrm(ks[17], (nb, LRU_WIDTH), 0.01),
        'lru_w_gx': nrm(ks[18], (nb, LRU_HEADS, LRU_BLOCK, LRU_BLOCK), LRU_BLOCK ** -0.5),
        'lru_b_gx': nrm(ks[19], (nb, LRU_WIDTH), 0.01),
        'lru_w_ga': nrm(ks[21], (nb, LRU_HEADS, LRU_BLOCK, LRU_BLOCK), LRU_BLOCK ** -0.5),
        'lru_b_ga': nrm(ks[22], (nb, LRU_WIDTH), 0.01),
        'lru_lambda': jnp.log(lam_u) - jnp.log1p(-lam_u),
        'lru_w_out': nrm(ks[23], (nb, LRU_WIDTH, D_MODEL), LRU_WIDTH ** -0.5),
        'lru_b_out': nrm(ks[24], (nb, D_MODEL), 0.01),
        'ffn_w_up': nrm(ks[25], (DEPTH, D_MODEL, 2 * D_FF), D_MODEL ** -0.5),
        'ffn_conv_w': nrm(ks[26], (DEPTH, FFN_CONV, 2 * D_FF), FFN_CONV ** -0.5),
        'ffn_conv_b': nrm(ks[27], (DEPTH, 2 * D_FF), 0.01),
        'ffn_w_down': nrm(ks[28], (DEPTH, D_FF, D_MODEL), D_FF ** -0.5),
    }

def first_block(x, norm_mix_pre, norm_mix_post, norm_ffn_pre, norm_ffn_post,
              ssd_w_in, ssd_conv_w, ssd_conv_b, ssd_dt_bias, ssd_a_log, ssd_d, ssd_norm, ssd_w_out,
              lru_w_in, lru_b_in, lru_conv_w, lru_conv_b, lru_w_gx, lru_b_gx, lru_w_ga, lru_b_ga,
              lru_lambda, lru_w_out, lru_b_out,
              ffn_w_up, ffn_conv_w, ffn_conv_b, ffn_w_down):
    for i in range(DEPTH):
        h = rmsnorm(x, norm_mix_pre[i])
        j = i // N_MIXERS
        if i % N_MIXERS == 0:
            m = ssd_mixer(h, ssd_w_in[j], ssd_conv_w[j], ssd_conv_b[j], ssd_dt_bias[j],
                          ssd_a_log[j], ssd_d[j], ssd_norm[j], ssd_w_out[j])
        else:
            m = rglru_mixer(h, lru_w_in[j], lru_b_in[j], lru_conv_w[j], lru_conv_b[j],
                            lru_w_gx[j], lru_b_gx[j], lru_w_ga[j], lru_b_ga[j],
                            lru_lambda[j], lru_w_out[j], lru_b_out[j])
        x = x + rmsnorm(m, norm_mix_post[i])
        h = rmsnorm(x, norm_ffn_pre[i])
        f = conv_ffn(h, ffn_w_up[i], ffn_conv_w[i], ffn_conv_b[i], ffn_w_down[i])
        x = x + rmsnorm(f, norm_ffn_post[i])
    return x


DA_HEADS = 4
DA_HEAD_DIM = 64
DA_WIDTH = DA_HEADS * 2 * DA_HEAD_DIM
Q_BLOCK = 128
ROPE_THETA = 10000.0
DN_HEADS = 4
DN_HEAD_DIM = 128
DN_WIDTH = DN_HEADS * DN_HEAD_DIM
CONV_K = 5
CHUNK = 64
D_FF_2 = 4 * D_MODEL
IN_SPLITS = (DA_WIDTH, DA_WIDTH, DA_WIDTH, DN_WIDTH, DN_WIDTH, DN_WIDTH, DN_WIDTH,
             2 * DN_HEADS, 2 * DN_HEADS, 2 * D_MODEL)
IN_COLS = sum(IN_SPLITS)


def rms_norm(x, gain):
    x32 = x.astype(jnp.float32)
    y = x32 * lax.rsqrt(jnp.mean(x32 * x32, axis=-1, keepdims=True) + EPS)
    return (y * gain.astype(jnp.float32)).astype(x.dtype)

def l2_norm(x):
    x32 = x.astype(jnp.float32)
    return (x32 * lax.rsqrt(jnp.sum(x32 * x32, axis=-1, keepdims=True) + EPS)).astype(x.dtype)

def rope_tables(seq, dim, dtype):
    pos = jnp.arange(seq, dtype=jnp.float32)
    inv = 1.0 / (ROPE_THETA ** (jnp.arange(0, dim, 2, dtype=jnp.float32) / dim))
    ang = pos[:, None] * inv[None, :]
    ang = jnp.concatenate([ang, ang], axis=-1)
    return jnp.cos(ang).astype(dtype), jnp.sin(ang).astype(dtype)

def apply_rope(x, cos, sin):
    half = x.shape[-1] // 2
    rot = jnp.concatenate([-x[..., half:], x[..., :half]], axis=-1)
    return x * cos + rot * sin

def diff_attention(q, k, v, lam, lambda_init, cos, sin, qn_gain, kn_gain, subln_gain):
    B, S, H, _, d = q.shape
    q = apply_rope(rms_norm(q, qn_gain).transpose(0, 2, 3, 1, 4), cos, sin)
    k = apply_rope(rms_norm(k, kn_gain).transpose(0, 2, 3, 1, 4), cos, sin)
    v = v.transpose(0, 2, 1, 3)
    nb = S // Q_BLOCK
    qb = q.reshape(B, H, 2, nb, Q_BLOCK, d).transpose(3, 0, 1, 2, 4, 5)
    scale = d ** -0.5

    def block(qi):
        s = jnp.einsum('bhtqd,bhtkd->bhtqk', qi, k).astype(jnp.float32) * scale
        p = jax.nn.softmax(s, axis=-1)
        a = p[:, :, 0] - lam * p[:, :, 1]
        return jnp.einsum('bhqk,bhkd->bhqd', a.astype(v.dtype), v)

    o = lax.map(block, qb)
    o = o.transpose(1, 0, 3, 2, 4).reshape(B, S, H, 2 * d)
    o = rms_norm(o, subln_gain) * (1.0 - lambda_init)
    return o.reshape(B, S, H * 2 * d)

def gated_delta_rule_chunked(q, k, v, g, beta):
    out_dtype = v.dtype
    q, k, v, g, beta = [t.astype(jnp.float32) for t in (q, k, v, g, beta)]
    B, H, S, Dk = q.shape
    Dv = v.shape[-1]
    n = S // CHUNK
    q = q.reshape(B, H, n, CHUNK, Dk)
    k = k.reshape(B, H, n, CHUNK, Dk)
    v = v.reshape(B, H, n, CHUNK, Dv)
    beta = beta.reshape(B, H, n, CHUNK)
    g = jnp.cumsum(g.reshape(B, H, n, CHUNK), axis=-1)
    idx = jnp.arange(CHUNK)
    incl = idx[:, None] >= idx[None, :]
    strict = idx[:, None] > idx[None, :]
    gdiff = g[..., :, None] - g[..., None, :]
    decay = jnp.where(incl, jnp.exp(jnp.where(incl, gdiff, 0.0)), 0.0)
    kb = k * beta[..., None]
    L = jnp.where(strict, jnp.einsum('bhncd,bhnmd->bhncm', kb, k) * decay, 0.0)
    eye = jnp.eye(CHUNK, dtype=jnp.float32)
    T = lax.linalg.triangular_solve(eye + L, jnp.broadcast_to(eye, L.shape), left_side=True,
                                    lower=True, unit_diagonal=True)
    u = jnp.einsum('bhncm,bhnme->bhnce', T, v * beta[..., None])
    w = jnp.einsum('bhncm,bhnmd->bhncd', T, kb * jnp.exp(g)[..., None])
    qk = jnp.einsum('bhncd,bhnmd->bhncm', q, k) * decay
    q_dec = q * jnp.exp(g)[..., None]
    k_dec = k * jnp.exp(g[..., -1:] - g)[..., None]
    g_last = jnp.exp(g[..., -1])

    def step(state, inp):
        qd_i, kd_i, u_i, w_i, qk_i, gl_i = inp
        v_new = u_i - jnp.einsum('bhcd,bhde->bhce', w_i, state)
        o_i = jnp.einsum('bhcd,bhde->bhce', qd_i, state) + jnp.einsum('bhcm,bhme->bhce', qk_i, v_new)
        state = state * gl_i[..., None, None] + jnp.einsum('bhcd,bhce->bhde', kd_i, v_new)
        return state, o_i

    xs = (jnp.moveaxis(q_dec, 2, 0), jnp.moveaxis(k_dec, 2, 0), jnp.moveaxis(u, 2, 0),
          jnp.moveaxis(w, 2, 0), jnp.moveaxis(qk, 2, 0), jnp.moveaxis(g_last, 2, 0))
    state0 = jnp.zeros((B, H, Dk, Dv), jnp.float32)
    _, o = lax.scan(step, state0, xs)
    return jnp.moveaxis(o, 0, 2).reshape(B, H, S, Dv).astype(out_dtype)

def gated_deltanet(q, k, v, z, b, a, conv_w, A_log, dt_bias, out_gain):
    B, S, _ = q.shape
    qkv = jnp.concatenate([q, k, v], axis=-1)
    qkv = lax.conv_general_dilated(qkv, conv_w[:, None, :].astype(qkv.dtype), window_strides=(1,),
                                   padding=[(CONV_K // 2, CONV_K // 2)],
                                   dimension_numbers=('NWC', 'WIO', 'NWC'),
                                   feature_group_count=qkv.shape[-1])
    q, k, v = jnp.split(jax.nn.silu(qkv), 3, axis=-1)

    def heads(t):
        return t.reshape(B, S, DN_HEADS, DN_HEAD_DIM).transpose(0, 2, 1, 3)

    q = l2_norm(heads(q)) * (DN_HEAD_DIM ** -0.5)
    k = l2_norm(heads(k))
    v = heads(v)
    beta = jax.nn.sigmoid(b.astype(jnp.float32)).reshape(B, S, 2, DN_HEADS).transpose(2, 0, 3, 1)
    a_in = a.astype(jnp.float32).reshape(B, S, 2, DN_HEADS).transpose(2, 0, 3, 1)
    g = -jnp.exp(A_log.astype(jnp.float32))[:, None, :, None] * jax.nn.softplus(
        a_in + dt_bias.astype(jnp.float32)[:, None, :, None])
    o_fwd = gated_delta_rule_chunked(q, k, v, g[0], beta[0])
    o_bwd = jnp.flip(gated_delta_rule_chunked(jnp.flip(q, 2), jnp.flip(k, 2), jnp.flip(v, 2),
                                              jnp.flip(g[1], 2), jnp.flip(beta[1], 2)), 2)
    o = (o_fwd + o_bwd).transpose(0, 2, 1, 3)
    o = rms_norm(o, out_gain) * jax.nn.silu(z.reshape(B, S, DN_HEADS, DN_HEAD_DIM))
    return o.reshape(B, S, DN_WIDTH)

def second_inputs(seed: int = 0) -> dict:
    key = jax.random.key(seed)
    ks = jax.random.split(key, 20)
    f32 = jnp.float32

    def nrm(k, shape, scale):
        return jax.random.normal(k, shape, f32) * scale

    x = nrm(ks[0], (BATCH, SEQ, D_MODEL), 1.0)
    c = nrm(ks[1], (BATCH, D_MODEL), 1.0)
    ada_w = nrm(ks[2], (DEPTH, D_MODEL, 6 * D_MODEL), D_MODEL ** -0.5)
    ada_b = nrm(ks[3], (DEPTH, 6 * D_MODEL), 0.02)
    norm1_g = 1.0 + nrm(ks[4], (DEPTH, D_MODEL), 0.05)
    norm2_g = 1.0 + nrm(ks[5], (DEPTH, D_MODEL), 0.05)
    w_in = nrm(ks[6], (DEPTH, D_MODEL, IN_COLS), D_MODEL ** -0.5)
    dn_conv = nrm(ks[7], (DEPTH, CONV_K, 3 * DN_WIDTH), CONV_K ** -0.5)
    dn_A_log = jnp.log(jax.random.uniform(ks[8], (DEPTH, 2, DN_HEADS), f32, 1.0, 16.0))
    dt = jnp.exp(jax.random.uniform(ks[9], (DEPTH, 2, DN_HEADS), f32, math.log(1e-3), math.log(1e-1)))
    dn_dt_bias = dt + jnp.log(-jnp.expm1(-dt))
    dn_out_gain = 1.0 + nrm(ks[10], (DEPTH, DN_HEAD_DIM), 0.05)
    qk_norm_gain = 1.0 + nrm(ks[11], (DEPTH, 2, DA_HEAD_DIM), 0.05)
    diff_lambda = nrm(ks[12], (DEPTH, 4, DA_HEAD_DIM), 0.1)
    diff_subln_gain = 1.0 + nrm(ks[13], (DEPTH, 2 * DA_HEAD_DIM), 0.05)
    w_branch_a = nrm(ks[14], (DEPTH, DA_WIDTH, D_MODEL), DA_WIDTH ** -0.5)
    w_branch_b = nrm(ks[15], (DEPTH, DN_WIDTH, D_MODEL), DN_WIDTH ** -0.5)
    w_out = nrm(ks[16], (DEPTH, D_MODEL, D_MODEL), D_MODEL ** -0.5)
    w_mlp1 = nrm(ks[17], (DEPTH, D_MODEL, D_FF_2), D_MODEL ** -0.5)
    w_mlp2 = nrm(ks[18], (DEPTH, D_FF_2, D_MODEL), D_FF_2 ** -0.5)
    return {'x': x, 'c': c, 'ada_w': ada_w, 'ada_b': ada_b, 'norm1_g': norm1_g, 'norm2_g': norm2_g,
            'w_in': w_in, 'dn_conv': dn_conv, 'dn_A_log': dn_A_log, 'dn_dt_bias': dn_dt_bias,
            'dn_out_gain': dn_out_gain, 'qk_norm_gain': qk_norm_gain, 'diff_lambda': diff_lambda,
            'diff_subln_gain': diff_subln_gain, 'w_branch_a': w_branch_a, 'w_branch_b': w_branch_b,
            'w_out': w_out, 'w_mlp1': w_mlp1, 'w_mlp2': w_mlp2}

def second_block(x, c, ada_w, ada_b, norm1_g, norm2_g, w_in, dn_conv, dn_A_log, dn_dt_bias, dn_out_gain,
              qk_norm_gain, diff_lambda, diff_subln_gain, w_branch_a, w_branch_b, w_out, w_mlp1, w_mlp2):
    B, S, D = x.shape
    cos, sin = rope_tables(S, DA_HEAD_DIM, x.dtype)
    split_points = [int(p) for p in np.cumsum(IN_SPLITS)[:-1]]
    c_act = jax.nn.silu(c)
    for l in range(DEPTH):
        mod = c_act @ ada_w[l] + ada_b[l]
        sh1, sc1, gt1, sh2, sc2, gt2 = [m[:, None, :] for m in jnp.split(mod, 6, axis=-1)]
        h = rms_norm(x, norm1_g[l]) * (1.0 + sc1) + sh1
        proj = h @ w_in[l]
        da_q, da_k, da_v, dn_q, dn_k, dn_v, dn_z, dn_b, dn_a, gates = jnp.split(proj, split_points, axis=-1)
        lambda_init = 0.8 - 0.6 * math.exp(-0.3 * l)
        lq = diff_lambda[l].astype(jnp.float32)
        lam = jnp.exp(jnp.sum(lq[0] * lq[1])) - jnp.exp(jnp.sum(lq[2] * lq[3])) + lambda_init
        y_a = diff_attention(da_q.reshape(B, S, DA_HEADS, 2, DA_HEAD_DIM),
                             da_k.reshape(B, S, DA_HEADS, 2, DA_HEAD_DIM),
                             da_v.reshape(B, S, DA_HEADS, 2 * DA_HEAD_DIM),
                             lam, lambda_init, cos, sin, qk_norm_gain[l, 0], qk_norm_gain[l, 1],
                             diff_subln_gain[l])
        y_b = gated_deltanet(dn_q, dn_k, dn_v, dn_z, dn_b, dn_a, dn_conv[l], dn_A_log[l], dn_dt_bias[l],
                             dn_out_gain[l])
        g_a, g_b = jnp.split(jax.nn.sigmoid(gates), 2, axis=-1)
        merged = g_a * (y_a @ w_branch_a[l]) + g_b * (y_b @ w_branch_b[l])
        x = x + gt1 * (merged @ w_out[l])
        h = rms_norm(x, norm2_g[l]) * (1.0 + sc2) + sh2
        x = x + gt2 * (jnp.square(jax.nn.relu(h @ w_mlp1[l])) @ w_mlp2[l])
    return x


def setup_inputs(seed=0):
    out = dict(first_inputs(seed))
    for name, value in second_inputs(seed + 1).items():
        if name != "x":
            out[name + "_2"] = value
    return out


def reference(
    x, norm_mix_pre, norm_mix_post, norm_ffn_pre, norm_ffn_post, ssd_w_in, ssd_conv_w,
    ssd_conv_b, ssd_dt_bias, ssd_a_log, ssd_d, ssd_norm, ssd_w_out, lru_w_in, lru_b_in,
    lru_conv_w, lru_conv_b, lru_w_gx, lru_b_gx, lru_w_ga, lru_b_ga, lru_lambda, lru_w_out,
    lru_b_out, ffn_w_up, ffn_conv_w, ffn_conv_b, ffn_w_down, c_2, ada_w_2, ada_b_2, norm1_g_2,
    norm2_g_2, w_in_2, dn_conv_2, dn_A_log_2, dn_dt_bias_2, dn_out_gain_2, qk_norm_gain_2,
    diff_lambda_2, diff_subln_gain_2, w_branch_a_2, w_branch_b_2, w_out_2, w_mlp1_2, w_mlp2_2,
):
    x = first_block(
        x, norm_mix_pre, norm_mix_post, norm_ffn_pre, norm_ffn_post, ssd_w_in, ssd_conv_w,
        ssd_conv_b, ssd_dt_bias, ssd_a_log, ssd_d, ssd_norm, ssd_w_out, lru_w_in, lru_b_in,
        lru_conv_w, lru_conv_b, lru_w_gx, lru_b_gx, lru_w_ga, lru_b_ga, lru_lambda, lru_w_out,
        lru_b_out, ffn_w_up, ffn_conv_w, ffn_conv_b, ffn_w_down,
    )
    return second_block(
        x, c_2, ada_w_2, ada_b_2, norm1_g_2, norm2_g_2, w_in_2, dn_conv_2, dn_A_log_2,
        dn_dt_bias_2, dn_out_gain_2, qk_norm_gain_2, diff_lambda_2, diff_subln_gain_2,
        w_branch_a_2, w_branch_b_2, w_out_2, w_mlp1_2, w_mlp2_2,
    )


_drawn_inputs = setup_inputs


def setup_inputs(seed=0):
    import zlib

    import numpy as np

    out = dict(_drawn_inputs(seed))
    spreads = {}
    factors = {'ssd_conv_b': 3.664,
     'lru_conv_b': 2.91,
     'lru_b_gx': 8.0,
     'lru_b_ga': 8.0,
     'lru_b_out': 3.588,
     'ffn_conv_b': 4.199,
     'norm1_g_2': 4.626,
     'dn_out_gain_2': 6.471,
     'qk_norm_gain_2': 8.0,
     'diff_lambda_2': 8.0,
     'diff_subln_gain_2': 7.745,
     'norm2_g_2': 3.731}
    for name, (base, spread) in spreads.items():
        noise = np.random.default_rng([zlib.crc32(name.encode()), seed]).standard_normal(out[name].shape)
        drawn = base * np.exp(spread * noise) if base else spread * noise
        out[name] = jnp.asarray(drawn.astype(out[name].dtype))
    for name, factor in factors.items():
        out[name] = (out[name] * factor).astype(out[name].dtype)
    return out
```

```python
import math

import numpy as np

import concourse.bass as bass
from concourse import mybir
from concourse.alu_op_type import AluOpType as ALU

P = 128
T = 256
D = 1024
DT_ = D // P
NCHK = T // P
RING = 6
CW = 2048
H_SSD, G_SSD = 32, 4
XT = 16
BCT = 8
LT = 10
FT = 32
NH = 4
AW = 128
ADA_N = 6 * D // AW
EPS = 1e-6
NEG = -1e30

STAGES = [("ssd_in", 20, 0), ("ssd_out", 0, 8), ("ffn0", 32, 16), ("lru_in", 10, 0), ("lru_gates", 0, 0),
          ("lru_out", 0, 5), ("ffn1", 32, 16)]
for _l in range(2):
    STAGES += [(f"in2_{_l}", 22, 0), (f"bra_{_l}", 0, 2), (f"brb_{_l}", 0, 2), (f"out2_{_l}", 0, 4),
               (f"mlp_{_l}", 16, 16)]
EXTRA = {"lru_gates": 2}
CH0, U0, B0 = {}, {}, {}
_c = _u = _b = 0
for _n, _a, _bb in STAGES:
    CH0[_n], U0[_n], B0[_n] = _c, _u, _b
    _c += _a + _bb + EXTRA.get(_n, 0)
    _u += _a
    _b += _bb
NCHUNK = _c


def _columns(sizes):
    at, out = 0, {}
    for name, n in sizes:
        out[name] = at
        at += n
    return out, at


PAR, NPAR = _columns([
    ("mix_pre", 16), ("mix_post", 16), ("ffn_pre", 16), ("ffn_post", 16),
    ("ssd_conv", 24 * 5), ("dt_w", 8 * 32), ("dt_bias", 1), ("a_log", 1), ("ssd_d", 16), ("ssd_norm", 16),
    ("lru_b_in", 20), ("lru_conv", LT * 5), ("b_gx", LT), ("b_ga", LT), ("lam", LT), ("b_out", 8),
    ("ffn_conv", 2 * FT * 8), ("c", 8), ("ada_b", 96), ("n1", 16), ("n2", 16), ("dn_conv", 2 * 12 * 5),
    ("ba_w", 2 * 8 * 72), ("A_log", 2), ("dn_dt", 2), ("dn_gain", 2), ("qk_gain", 4), ("dlam", 8), ("subln", 2)])
CON, NCON = _columns([
    ("ident", P), ("ones", P), ("half_ones", P), ("neg_up", P), ("neg_lo", P), ("rope", P), ("level", 14 * P),
    ("cos", T), ("sin", T), ("eps", 1), ("one", 1), ("tiny", 1), ("zero", 1)])


def constants():
    c = np.zeros((P, NCON), np.float32)
    i = np.arange(P)
    def put(name, m, k=0):
        c[:, CON[name] + k:CON[name] + k + m.shape[1]] = m
    put("ident", np.eye(P))
    put("ones", np.ones((P, P)))
    put("half_ones", (i[:, None] // 64 == i[None, :] // 64))
    put("neg_up", np.where(i[:, None] <= i[None, :], 0, NEG))
    put("neg_lo", np.where(i[:, None] >= i[None, :], 0, NEG))
    rope = np.zeros((P, P))
    for b in (0, 64):
        for j in range(32):
            rope[b + j + 32, b + j] = -1.0
            rope[b + j, b + j + 32] = 1.0
    put("rope", rope)
    for n in range(7):
        m = 1 << n
        low = ((i[:, None] // m) % 2 == 1) & ((i[None, :] // m) == (i[:, None] // m) - 1)
        put("level", low, 2 * n * P)
        put("level", low.T, (2 * n + 1) * P)
    inv = 1.0 / (10000.0 ** (np.arange(0, 64, 2, dtype=np.float32) / 64))
    ang = np.arange(T, dtype=np.float32)[:, None] * inv.astype(np.float32)[None, :]
    ang = np.concatenate([ang, ang, ang, ang], axis=-1).T
    put("cos", np.cos(ang))
    put("sin", np.sin(ang))
    put("eps", np.full((P, 1), EPS))
    put("one", np.ones((P, 1)))
    put("tiny", np.full((P, 1), 1e-30))
    return c


def tiled(v):
    return np.reshape(v, (-1, P)).T


def parameters(a):
    p = np.zeros((P, NPAR), np.float32)
    def put(name, m, k=0):
        p[0:m.shape[0], PAR[name] + k:PAR[name] + k + m.shape[1]] = m
    for l in range(2):
        for name, src in (("mix_pre", "norm_mix_pre"), ("mix_post", "norm_mix_post"), ("ffn_pre", "norm_ffn_pre"),
                          ("ffn_post", "norm_ffn_post"), ("n1", "norm1_g_2"), ("n2", "norm2_g_2")):
            put(name, tiled(a[src][l]), 8 * l)
        w, b = a["ffn_conv_w"][l], a["ffn_conv_b"][l]
        for half in range(2):
            for j in range(3):
                m = tiled(w[j])[:, FT * half:FT * (half + 1)]
                p[:, PAR["ffn_conv"] + l * FT * 8 + 4 * half + j:PAR["ffn_conv"] + (l + 1) * FT * 8:8] = m
            p[:, PAR["ffn_conv"] + l * FT * 8 + 4 * half + 3:PAR["ffn_conv"] + (l + 1) * FT * 8:8] = \
                tiled(b)[:, FT * half:FT * (half + 1)]
        put("ada_b", tiled(a["ada_b_2"][l]), 48 * l)
        for j in range(5):
            p[:, PAR["dn_conv"] + 60 * l + j:PAR["dn_conv"] + 60 * (l + 1):5] = tiled(a["dn_conv_2"][l, j])
        ba = a["w_in_2"][l][:, 3584:3600]
        for k in range(8):
            rows = ba[k * P:(k + 1) * P]
            for d in range(2):
                at = (l * 8 + k) * 72 + 32 * d
                put("ba_w", rows[:, 4 * d:4 * d + 4], at)
                put("ba_w", rows[:, 8 + 4 * d:12 + 4 * d], at + 36)
        for d in range(2):
            r = slice(32 * d, 32 * d + 4)
            p[r, PAR["A_log"] + l] = a["dn_A_log_2"][l, d]
            p[r, PAR["dn_dt"] + l] = a["dn_dt_bias_2"][l, d]
        put("dn_gain", a["dn_out_gain_2"][l][:, None], l)
        for t in range(2):
            put("qk_gain", np.concatenate([a["qk_norm_gain_2"][l, t]] * 2)[:, None], 2 * l + t)
        put("dlam", a["diff_lambda_2"][l].T, 4 * l)
        put("subln", a["diff_subln_gain_2"][l][:, None], l)
    for j in range(4):
        p[:, PAR["ssd_conv"] + j:PAR["ssd_conv"] + 120:5] = tiled(a["ssd_conv_w"][0, j])
        p[:, PAR["lru_conv"] + j:PAR["lru_conv"] + 50:5] = tiled(a["lru_conv_w"][0, j])
    p[:, PAR["ssd_conv"] + 4:PAR["ssd_conv"] + 120:5] = tiled(a["ssd_conv_b"][0])
    p[:, PAR["lru_conv"] + 4:PAR["lru_conv"] + 50:5] = tiled(a["lru_conv_b"][0])
    put("dt_w", a["ssd_w_in"][0][:, 5120:].reshape(8, P, 32).transpose(1, 0, 2).reshape(P, 256))
    put("dt_bias", a["ssd_dt_bias"][0][:, None])
    put("a_log", a["ssd_a_log"][0][:, None])
    put("ssd_d", tiled(np.repeat(a["ssd_d"][0], 64)))
    put("ssd_norm", tiled(a["ssd_norm"][0]))
    put("lru_b_in", tiled(a["lru_b_in"][0]))
    put("b_gx", tiled(a["lru_b_gx"][0]))
    put("b_ga", tiled(a["lru_b_ga"][0]))
    put("lam", tiled(a["lru_lambda"][0]))
    put("b_out", tiled(a["lru_b_out"][0]))
    put("c", tiled(a["c_2"][0]))
    return p


def stream(a):
    w = np.zeros((NCHUNK, P, CW), np.float32)

    def kind_a(at, m):
        n = m.shape[1] // 256
        w[at:at + n] = m.reshape(8, P, n, 256).transpose(2, 1, 0, 3).reshape(n, P, CW)

    def kind_b(at, m):
        n = m.shape[0] // 256
        w[at:at + n] = m.reshape(n, 2, P, D).transpose(0, 2, 1, 3).reshape(n, P, CW)

    s = a["ssd_w_in"][0]
    kind_a(CH0["ssd_in"], s[:, 2048:5120])
    kind_a(CH0["ssd_in"] + 12, s[:, 0:2048])
    kind_b(CH0["ssd_out"], a["ssd_w_out"][0])
    kind_a(CH0["lru_in"], np.concatenate([a["lru_w_in"][0][:, 1280:], a["lru_w_in"][0][:, :1280]], axis=1))
    for half in range(2):
        for g, name in enumerate(("lru_w_gx", "lru_w_ga")):
            m = a[name][0][5 * half:5 * half + 5].transpose(1, 0, 2).reshape(P, 640)
            w[CH0["lru_gates"] + half][:, 640 * g:640 * (g + 1)] = m
    kind_b(CH0["lru_out"], a["lru_w_out"][0])
    for l in range(2):
        up, down = a["ffn_w_up"][l], a["ffn_w_down"][l]
        ups = np.stack([up[:, :FT * P].reshape(D, FT, P), up[:, FT * P:].reshape(D, FT, P)], axis=2).reshape(D, -1)
        spread(w, CH0[f"ffn{l}"], ups, down, kind_a, kind_b)
        m = a["w_in_2"][l]
        at = CH0[f"in2_{l}"]
        kind_a(at, m[:, 1536:3072])
        kind_a(at + 6, m[:, 0:1536])
        kind_a(at + 12, m[:, 3072:3584])
        kind_a(at + 14, m[:, 3600:5648])
        kind_b(CH0[f"bra_{l}"], a["w_branch_a_2"][l])
        kind_b(CH0[f"brb_{l}"], a["w_branch_b_2"][l])
        kind_b(CH0[f"out2_{l}"], a["w_out_2"][l])
        mlp_chunks(w, CH0[f"mlp_{l}"], a["w_mlp1_2"][l], a["w_mlp2_2"][l], kind_a, kind_b)
    return w


def spread(w, at, up, down, kind_a, kind_b):
    for p in range(16):
        a0 = at + (0 if p == 0 else 3 * p - 1)
        kind_a(a0, up[:, 512 * p:512 * (p + 1)])
        b0 = at + 3 * p + 4 if p < 15 else at + 47
        kind_b(b0, down[256 * p:256 * (p + 1)])


def mlp_chunks(w, at, up, down, kind_a, kind_b):
    for p in range(16):
        kind_a(at + (0 if p == 0 else 2 * p - 1), up[:, 256 * p:256 * (p + 1)])
        kind_b(at + (2 * p + 2 if p < 15 else 31), down[256 * p:256 * (p + 1)])


class Chain:

    def __init__(self, engine, sem):
        self.engine, self.sem, self.n, self.at = engine, sem, 0, None

    def __call__(self, ins):
        ins.then_inc(self.sem, 1)
        self.n += 1
        value = self.n if self.at is None else self.at[0] * self.at[1] + self.n
        self.engine.wait_ge(self.sem, value)

    def enter(self, i, per):
        self.at, self.start = (i, per), self.n

    def leave(self, turns):
        per = self.at[1]
        assert self.n - self.start == per, (self.n - self.start, per)
        self.n, self.at = self.start + per * turns, None


def build(nc, x_in, w_in, ada_in, par_in, con_in, out):
    f32 = mybir.dt.float32
    ACT = mybir.ActivationFunctionType
    AX = mybir.AxisListType
    sems = {}
    from contextlib import ExitStack
    ctx = ExitStack()
    with ctx:
        def sb(name, shape):
            return ctx.enter_context(nc.sbuf_tensor(name, shape, f32))

        def S(name):
            if name not in sems:
                sems[name] = ctx.enter_context(nc.semaphore(name))
            return sems[name]

        ring = [sb(f"ring{i}", [P, CW]) for i in range(RING)]
        x = sb("x", [P, DT_, T])
        h = sb("h", [P, DT_, T])
        par = sb("par", [P, NPAR])
        con = sb("con", [P, NCON])
        ada_ring = [sb(f"ada_ring{i}", [P, 8, AW]) for i in range(2)]
        ada_acc = sb("ada_acc", [P, 6 * D])
        rstd = sb("rstd", [P, T])
        lnv = sb("lnv", [P, T])
        tmp = sb("tmp", [P, 4, T])
        cact = sb("cact", [P, 8])
        mod = sb("mod", [P, 48])
        gsc = sb("gsc", [P, 16])
        arena_cols = 21100
        arena = sb("arena", [P, arena_cols])

        unit = [ctx.enter_context(nc.psum_tensor(f"unit{i}", [P, 512], f32)) for i in range(2)]
        misc = [ctx.enter_context(nc.psum_tensor(f"misc{i}", [P, 512], f32)) for i in range(2)]
        acc = ctx.enter_context(nc.psum_tensor("acc", [P, 4 * 512], f32))
        acc8 = acc[:, :].rearrange("p (t n) -> p t n", n=T)

        def carve(sizes):
            at, views = 0, {}
            for name, shape in sizes:
                n = int(np.prod(shape))
                v = arena[:, at:at + n]
                if len(shape) == 2:
                    v = v.rearrange("p (a b) -> p a b", b=shape[1])
                elif len(shape) == 3:
                    v = v.rearrange("p (a b c) -> p a b c", b=shape[1], c=shape[2])
                views[name] = v
                at += n
            assert at <= arena_cols, at
            return views

        def pr(name, k=0, rows=P):
            return par[0:rows, PAR[name] + k:PAR[name] + k + 1]

        def cn(name, k=0, n=P):
            return con[:, CON[name] + k:CON[name] + k + n]

        def one(name, rows=P):
            return con[0:rows, CON[name]:CON[name] + 1]

        ident, ones = cn("ident"), cn("ones")
        bank = lambda b, a, z: acc[:, 512 * b + a:512 * b + z]
        mm = nc.tensor.matmul
        act = nc.scalar.activation
        tt = nc.vector.tensor_tensor
        stt = nc.vector.scalar_tensor_tensor
        ts = nc.vector.tensor_scalar

        NORMS = ["mix_pre0", "mix_post0", "ffn_pre0", "ffn_post0", "mix_pre1", "mix_post1", "ffn_pre1",
                 "ffn_post1", "pre1_0", "pre2_0", "pre1_1", "pre2_1"]
        NI = {n: i for i, n in enumerate(NORMS)}
        XU = {"load": 0, "mix_post0": 1, "ffn_post0": 2, "mix_post1": 3, "ffn_post1": 4, "res1_0": 5,
              "res2_0": 6, "res1_1": 7, "res2_1": 8}
        HU = {"mix_pre0": 0, "ffn_pre0": 1, "mix_pre1": 2, "ffn_pre1": 3, "pre1_0": 4, "pre2_0": 5,
              "pre1_1": 6, "pre2_1": 7}

        def act_norm(ac, name, source, ready):
            n = NI[name]
            for q in range(4):
                ready(q)
                act(h[:, 2 * q:2 * q + 2, :], source[:, 2 * q:2 * q + 2, :], ACT.Square).then_inc(S("squares"), 1)
            ac.wait_ge(S("square_sums"), n + 1)
            act(lnv[:, :], misc[0][:, 0:T], ACT.Ln, bias=one("eps"), scale=1.0 / D).then_inc(S("log_var"), 1)
            ac.wait_ge(S("log_var"), n + 1)
            act(rstd[:, :], lnv[:, :], ACT.Exp, scale=-0.5).then_inc(S("rstd_ready"), 1)

        def pe_norm(pe, name):
            n = NI[name]
            for q in range(4):
                pe.wait_ge(S("squares"), 4 * n + q + 1)
                for t in (2 * q, 2 * q + 1):
                    last = mm(misc[0][:, 0:T], ones, h[:, t, :], start=(t == 0), stop=(t == 7))
            last.then_inc(S("square_sums"), 1)

        def x_ready(eng, name):
            return lambda q: eng.wait_ge(S("x_ready"), 4 * XU[name] + q + 1)

        def dve_pre(dve, name, weight, k0):
            dve.wait_ge(S("rstd_ready"), NI[name] + 1)
            for t in range(8):
                ins = stt(h[:, t, :], x[:, t, :], weight(t), rstd[:, :], ALU.mult, ALU.mult)
                if t % 2:
                    ins.then_inc(S("h_ready"), 1)

        def dve_post(dve, link, name, weight, source):
            dve.wait_ge(S("rstd_ready"), NI[name] + 1)
            for q in range(4):
                s = tmp[:, 2 * (q % 2):2 * (q % 2) + 2, :]
                for k in range(2):
                    ins = stt(s[:, k, :], source[:, 2 * q + k, :], weight(2 * q + k), rstd[:, :], ALU.mult, ALU.mult)
                link(ins)
                tt(x[:, 2 * q:2 * q + 2, :], x[:, 2 * q:2 * q + 2, :], s, ALU.add).then_inc(S("x_ready"), 1)

        def dve_residual(dve, name, gate, done):
            dve.wait_ge(S("down_done"), done)
            for t in range(8):
                ins = stt(x[:, t, :], acc8[:, t, :], gate(t), x[:, t, :], ALU.mult, ALU.add)
                if t % 2:
                    ins.then_inc(S("x_ready"), 1)

        loaded = [S(f"chunk_loaded{i}") for i in range(RING)]

        def slot(c):
            return ring[c % RING][:, :].rearrange("p (k n) -> p k n", k=8)

        def pe_chunk(pe, c, i=None, chunks=0):
            turn = c // RING + 1
            pe.wait_ge(loaded[c % RING], 16 * turn if i is None else i * (16 * chunks // RING) + 16 * turn)

        def begun(c, first, ins):
            if first and c > 0:
                ins.then_inc(S("chunk_begun"), 1)

        def pe_unit(pe, c, n, i=None, chunks=0, units=0, tokens_out=False):
            pe_chunk(pe, c, i, chunks)
            pe.wait_ge(S("unit_free"), n + 1 if i is None else i * units + n + 1)
            w, b = slot(c), unit[n % 2]
            for half in range(2):
                for k in range(8):
                    if tokens_out:
                        ins = mm(b[:, T * half:T * (half + 1)], h[:, k, P * half:P * (half + 1)], w[:, k, :],
                                 start=(k == 0), stop=(k == 7))
                    else:
                        ins = mm(b[:, T * half:T * (half + 1)], w[:, k, P * half:P * (half + 1)], h[:, k, :],
                                 start=(k == 0), stop=(k == 7))
                    begun(c, half == 0 and k == 0, ins)
            ins.then_inc(S("unit_ready"), 1)

        def pe_units(pe, c0, n0, count):
            turns = count // RING
            if turns >= 2:
                with pe.Fori(0, turns) as i:
                    for j in range(RING):
                        pe_unit(pe, c0 + j, n0 + j, i, RING, RING)
                done = turns * RING
            else:
                done = 0
            for j in range(done, count):
                pe_unit(pe, c0 + j, n0 + j)

        def pe_down(pe, c, b, moving, first, last, i=None, chunks=0):
            pe_chunk(pe, c, i, chunks)
            w = ring[c % RING][:, :].rearrange("p (k n) -> p k n", k=2)
            for k in range(2):
                for t in range(8):
                    ins = mm(acc8[:, t, :], w[:, k, P * t:P * (t + 1)], moving[:, k, :],
                             start=(first and k == 0 and t % 2 == 0), stop=(last and k == 1 and t % 2 == 1))
                    begun(c, k == 0 and t == 0, ins)
            ins.then_inc(S("down_done"), 1)

        A = carve([("zs", (16, T)), ("xbc", (24, T)), ("xdt", (32, 64)), ("xdtd", (32, 64)), ("btok", (4, P)),
                   ("cb", (4, P)), ("e", (8, P)), ("e2", (8, P)), ("st", (32, 64)), ("rows", (2, T)),
                   ("tok", (5, 32))])
        A["conv"] = tmp[:, :, :]
        A["rg"] = tmp[:, :, :]
        late = A["xdtd"].rearrange("p a b -> p (a b)")
        A["ecs"] = late[:, 0:512].rearrange("p (a b) -> p a b", b=P)
        A["yo"] = late[:, 512:1024].rearrange("p (a b) -> p a b", b=P)
        xbc, zs = A["xbc"], A["zs"]
        HR = 32
        r_cs, r_a = (A["rows"][0:HR, k, :] for k in range(2))
        early = [v.rearrange("p a b -> p (a b)") for v in (A["e"], A["e2"])]
        r_dt, r_da, r_b, r_ncs = (early[0][0:HR, T * k:T * (k + 1)] for k in range(4))
        r_dtd, r_one = (early[1][0:HR, T * k:T * (k + 1)] for k in range(2))
        tokv = A["tok"]
        E2 = [A["e"], A["e2"]]

        def pe_ssd(pe):
            pe.wait_ge(S("h_ready"), 4)
            for k in range(8):
                ins = mm(misc[1][0:HR, 0:T], par[:, PAR["dt_w"] + 32 * k:PAR["dt_w"] + 32 * (k + 1)], h[:, k, :],
                         start=(k == 0), stop=(k == 7))
            ins.then_inc(S("dt_raw"), 1)
            pe_units(pe, CH0["ssd_in"], U0["ssd_in"], 20)
            pe.wait_ge(S("ssd_rows"), 1)
            for n, (src, c) in enumerate(((r_dt, 0), (r_dt, 1), (r_ncs, 0), (r_ncs, 1), (r_dtd, 0))):
                ins = nc.tensor.transpose(misc[1][:, 32 * n:32 * (n + 1)], src[:, P * c:P * (c + 1)], ident[0:HR, 0:HR])
            ins.then_inc(S("ssd_tok_ps"), 1)
            pe.wait_ge(S("ssd_conv_done"), 24)
            for g in range(4):
                ins = nc.tensor.transpose(bank(0, P * g, P * (g + 1)), xbc[:, 16 + g, 0:P], ident)
            ins.then_inc(S("ssd_btok_ps"), 1)
            for c in range(2):
                for q in range(4):
                    m = 4 * c + q
                    if m >= 2:
                        pe.wait_ge(S("ssd_x_read"), m - 1)
                    if m == 0:
                        pe.wait_ge(S("ssd_btok"), 1)
                    for k in range(4):
                        ins = nc.tensor.transpose(bank(m % 2, P * k, P * (k + 1)), xbc[:, 4 * q + k, P * c:P * (c + 1)],
                                                  ident)
                    ins.then_inc(S("ssd_x_ps"), 1)
                if c == 1:
                    pe.wait_ge(S("ssd_cb"), 1)
                for g in range(4):
                    ins = mm(bank(2, P * g, P * (g + 1)), xbc[:, 16 + g, P * c:P * (c + 1)],
                             xbc[:, 20 + g, P * c:P * (c + 1)], start=True, stop=True)
                ins.then_inc(S("ssd_cb_ps"), 1)
                if c == 0:
                    for g in range(4):
                        pe.wait_ge(S("ssd_xdtd"), g + 1)
                        if g >= 1:
                            pe.wait_ge(S("ssd_state"), g)
                        mm(bank(3, 0, 512), A["btok"][:, g, :],
                           A["xdtd"].rearrange("p a b -> p (a b)")[:, 512 * g:512 * (g + 1)],
                           start=True, stop=True).then_inc(S("ssd_state_ps"), 1)
                    pe.wait_ge(S("ssd_state"), 4)
                if c == 1:
                    pe.wait_ge(S("ssd_x_read"), 8)
                for g in range(4):
                    n = 4 * c + g
                    for half in range(2):
                        m = 2 * n + half
                        if m >= 2:
                            pe.wait_ge(S("ssd_exp"), m - 1)
                        b = unit[m % 2]
                        if m < 2:
                            pe.wait_ge(S("unit_free"), 22)
                        for k in range(4):
                            hd = 8 * g + 4 * half + k
                            mm(b[:, P * k:P * (k + 1)], ident[0:HR, hd:hd + 1].to_broadcast([HR, P]),
                               r_cs[:, P * c:P * (c + 1)], start=(k == 0), stop=False, skip_group_check=True)
                        for k in range(4):
                            ins = mm(b[:, P * k:P * (k + 1)], ident, cn("neg_up"), start=False, stop=(k == 3),
                                     skip_group_check=True)
                        ins.then_inc(S("ssd_decay_ps"), 1)
                    pe.wait_ge(S("ssd_scores"), n + 1)
                    if n >= 1:
                        pe.wait_ge(S("ssd_y"), n)
                    if n == 0:
                        pe.wait_ge(S("ssd_tok"), 1)
                    for hd in range(8):
                        lo = 64 * (hd % 2)
                        ins = mm(misc[0][lo:lo + 64, P * (hd // 2):P * (hd // 2) + P], A["xdt"][:, 8 * g + hd, :],
                                 E2[n % 2][:, hd, :], start=True, stop=True, skip_group_check=True)
                    if c == 1:
                        for k in range(4):
                            st = A["st"].rearrange("p a b -> p (a b)")[:, 512 * g + P * k:512 * g + P * (k + 1)]
                            mm(misc[1][:, P * k:P * (k + 1)], st, xbc[:, 20 + g, P:T], start=True, stop=True)
                        for k in range(4):
                            for e in range(2):
                                hd = 8 * g + 2 * k + e
                                ins = mm(bank(3, P * k, P * (k + 1))[64 * e:64 * (e + 1), :],
                                         ident[0:HR, hd:hd + 1].to_broadcast([HR, 64]), r_a[:, P:T],
                                         start=True, stop=True, skip_group_check=True)
                    ins.then_inc(S("ssd_y_ps"), 1)
            pe.wait_ge(S("ssd_y"), 8)
            for g in range(4):
                pe.wait_ge(S("ssd_sq"), g + 1)
                if g >= 2:
                    pe.wait_ge(S("ssd_glog"), g - 1)
                for k in range(4):
                    ins = mm(misc[g % 2][:, 0:T], ones, E2[0 if g % 2 == 0 else 1].rearrange("p a b -> p (a b)")
                             .rearrange("p (a b) -> p a b", b=T)[:, k, :], start=(k == 0), stop=(k == 3))
                ins.then_inc(S("ssd_gsum"), 1)
            for j in range(8):
                pe.wait_ge(S("ssd_yn"), j + 1)
                pe_down(pe, CH0["ssd_out"] + j, B0["ssd_out"] + j, xbc[:, 2 * j:2 * j + 2, :], j == 0, j == 7)

        def act_ssd(ac, link):
            ac.wait_ge(S("dt_in"), 1)
            link(act(r_a, r_dt, ACT.Abs))
            link(act(r_b, r_a, ACT.Exp, scale=-1.0))
            link(act(r_b, r_b, ACT.Ln, bias=one("one", HR)))
            act(r_one[:, 0:1], pr("a_log", 0, HR), ACT.Exp).then_inc(S("dt_log"), 1)
            ac.wait_ge(S("dt_cs"), 1)
            link(act(r_dtd, r_cs, ACT.Exp, bias=r_cs[:, P - 1:P], scale=-1.0))
            act(r_ncs, r_cs, ACT.Copy, scale=-1.0)
            act(r_a, r_cs, ACT.Exp).then_inc(S("dt_decays"), 1)
            conv = A["conv"]

            def last_tap(j, i=None, tiles=0, at=0):
                off = PAR["ssd_conv"] + 5 * j
                col = lambda k: (par[:, off + k:off + k + 1] if i is None
                                 else par[:, bass.ds(i * (5 * tiles) + off + k, 1)])
                if j % 2 == 0:
                    ac.wait_ge(S("unit_ready"), j // 2 + 1 if i is None else i * (tiles // 2) + j // 2 + 1)
                act(conv[:, j % 4, :], unit[(j // 2) % 2][:, T * (j % 2):T * (j % 2 + 1)], ACT.Identity,
                    bias=col(4), scale=col(3)).then_inc(S("ssd_tap"), 1)

            def silu(j, i=None, tiles=0):
                ac.wait_ge(S("ssd_taps"), j + 1 if i is None else i * tiles + j + 1)
                dst = xbc[:, j, :] if i is None else xbc[:, bass.ds(i * tiles + j, 1), :]
                src = conv[:, j % 4, :] if i is None else conv[:, j % 4:j % 4 + 1, :]
                act(dst, src, ACT.Silu).then_inc(S("ssd_conv_done"), 1)

            for j in range(4):
                last_tap(j)
                if j >= 2:
                    silu(j - 2)
            with ac.Fori(0, 5) as i:
                for j in range(4, 8):
                    ac.wait_ge(S("ssd_conv_done"), i * 4 + (j - 3))
                    last_tap(j, i, 4)
                    silu(j - 2, i, 4)
            for j in range(22, 24):
                silu(j)
            ac.wait_ge(S("unit_free"), 12 + 2)
            for n in range(8):
                ac.wait_ge(S("unit_ready"), 12 + n + 1)
                act(zs[:, 2 * n:2 * n + 2, :], unit[n % 2][:, :], ACT.Silu).then_inc(S("unit_free"), 1)
            ac.wait_ge(S("ssd_btok_ps"), 1)
            act(A["btok"], bank(0, 0, 512), ACT.Copy).then_inc(S("ssd_btok"), 1)
            for c in range(2):
                if c == 0:
                    for g in range(4):
                        ac.wait_ge(S("ssd_state_ps"), g + 1)
                        act(A["st"].rearrange("p a b -> p (a b)")[:, 512 * g:512 * (g + 1)], bank(3, 0, 512),
                            ACT.Copy).then_inc(S("ssd_state"), 1)
                ac.wait_ge(S("ssd_tok"), 1)
                for g in range(4):
                    n = 4 * c + g
                    for half in range(2):
                        ac.wait_ge(S("ssd_decay_ps"), 2 * n + half + 1)
                        if half == 0 and n >= 2:
                            ac.wait_ge(S("ssd_y_ps"), n - 1)
                        for k in range(4):
                            hd = 4 * half + k
                            ins = act(E2[n % 2][:, hd, :], unit[half][:, P * k:P * (k + 1)], ACT.Exp,
                                      bias=tokv[:, 2 + c, 8 * g + hd:8 * g + hd + 1])
                        ins.then_inc(S("ssd_exp"), 1)
                    if c == 1:
                        ac.wait_ge(S("ssd_y_ps"), n + 1)
                        if g >= 1:
                            ac.wait_ge(S("ssd_y"), n)
                        act(A["ecs"], bank(3, 0, 512), ACT.Copy).then_inc(S("ssd_ecs"), 1)
            for g in range(4):
                ac.wait_ge(S("ssd_gated"), g + 1)
                if g >= 2:
                    ac.wait_ge(S("ssd_gsum"), g - 1)
                if g == 0:
                    ac.wait_ge(S("ssd_y_ps"), 8)
                sq = E2[g % 2].rearrange("p a b -> p (a b)")
                act(sq, xbc[:, 4 * g:4 * g + 4, :], ACT.Square).then_inc(S("ssd_sq"), 1)
            for g in range(4):
                ac.wait_ge(S("ssd_gsum"), g + 1)
                act(A["rg"][:, g, :], misc[g % 2][:, 0:T], ACT.Ln, bias=one("eps"),
                    scale=1.0 / 512).then_inc(S("ssd_glog"), 1)
            ac.wait_ge(S("ssd_glog"), 4)
            act(A["rg"], A["rg"], ACT.Exp, scale=-0.5).then_inc(S("ssd_rg"), 1)

        def dve_ssd(dve, link):
            dve.wait_ge(S("dt_raw"), 1)
            ts(r_dt, misc[1][0:HR, 0:T], pr("dt_bias", 0, HR), None, ALU.add).then_inc(S("dt_in"), 1)
            dve.wait_ge(S("dt_log"), 1)
            link(stt(r_dt, r_dt, 0.0, r_b, ALU.max, ALU.add))
            link(ts(r_da, r_dt, r_one[:, 0:1], -1.0, ALU.mult, ALU.mult))
            link(nc.vector.memset(r_one, 1.0))
            for c in range(2):
                s = slice(P * c, P * (c + 1))
                ins = nc.vector.tensor_tensor_scan(r_cs[:, s], r_one[:, s], r_da[:, s], 0.0, ALU.mult, ALU.add)
            ins.then_inc(S("dt_cs"), 1)
            dve.wait_ge(S("dt_decays"), 1)
            tt(r_dtd, r_dtd, r_dt, ALU.mult).then_inc(S("ssd_rows"), 1)
            conv = A["conv"]

            def taps(j, i=None, tiles=0):
                off = PAR["ssd_conv"] + 5 * j
                col = lambda k: (par[:, off + k:off + k + 1] if i is None
                                 else par[:, bass.ds(i * (5 * tiles) + off + k, 1)])
                if j % 2 == 0:
                    dve.wait_ge(S("ssd_tap"), i * tiles + j + 2)
                src = unit[(j // 2) % 2][:, T * (j % 2):T * (j % 2 + 1)]
                dst = conv[:, j % 4, :]
                link(stt(dst[:, 1:T], src[:, 0:T - 1], col(2), dst[:, 1:T], ALU.mult, ALU.add))
                link(stt(dst[:, 2:T], src[:, 0:T - 2], col(1), dst[:, 2:T], ALU.mult, ALU.add))
                ins = stt(dst[:, 3:T], src[:, 0:T - 3], col(0), dst[:, 3:T], ALU.mult, ALU.add)
                ins.then_inc(S("ssd_taps"), 1)
                if j % 2:
                    dve.wait_ge(S("ssd_taps"), j + 1 if i is None else i * tiles + j + 1)
                    dve.sem_inc(S("unit_free"), 1)

            with dve.Fori(0, 6) as i:
                link.enter(i, 8)
                for j in range(4):
                    taps(j, i, 4)
                link.leave(6)
            dve.wait_ge(S("ssd_tok_ps"), 1)
            nc.vector.tensor_copy(tokv, misc[1][:, 0:160]).then_inc(S("ssd_tok"), 1)
            dve.wait_ge(S("ssd_tok"), 1)
            for c in range(2):
                for q in range(4):
                    m = 4 * c + q
                    dve.wait_ge(S("ssd_x_ps"), m + 1)
                    if c == 1 and q == 0:
                        dve.wait_ge(S("ssd_y_ps"), 4)
                    src = bank(m % 2, 0, 512).rearrange("p (a b) -> p a b", b=64)
                    hs = slice(8 * q, 8 * q + 8)
                    if c == 0:
                        tt(A["xdtd"][:, hs, :], src, tokv[:, 4, hs].unsqueeze(2).to_broadcast([P, 8, 64]),
                           ALU.mult).then_inc(S("ssd_xdtd"), 1)
                    tt(A["xdt"][:, hs, :], src, tokv[:, c, hs].unsqueeze(2).to_broadcast([P, 8, 64]),
                       ALU.mult).then_inc(S("ssd_x_read"), 1)
                dve.wait_ge(S("ssd_cb_ps"), c + 1)
                link(nc.vector.tensor_copy(A["cb"], bank(2, 0, 512)))
                for g in range(4):
                    n = 4 * c + g
                    dve.wait_ge(S("ssd_exp"), 2 * n + 2)
                    e = E2[n % 2]
                    ins = tt(e, e, A["cb"][:, g, :].unsqueeze(1).to_broadcast([P, 8, P]), ALU.mult)
                    ins.then_inc(S("ssd_scores"), 1)
                    if c == 0 and g == 3:
                        dve.wait_ge(S("ssd_scores"), 4)
                        dve.sem_inc(S("ssd_cb"), 1)
                    dve.wait_ge(S("ssd_y_ps"), n + 1)
                    s = slice(P * c, P * (c + 1))
                    if c == 1:
                        dve.wait_ge(S("ssd_ecs"), g + 1)
                        link(tt(A["yo"], misc[1][:, :].rearrange("p (a b) -> p a b", b=P), A["ecs"], ALU.mult))
                    for k in range(4):
                        ins = stt(xbc[:, 4 * g + k, s], xbc[:, 4 * g + k, s], pr("ssd_d", 4 * g + k),
                                  misc[0][:, P * k:P * (k + 1)], ALU.mult, ALU.add)
                    link(ins)
                    if c == 1:
                        link(tt(xbc[:, 4 * g:4 * g + 4, s], xbc[:, 4 * g:4 * g + 4, s], A["yo"], ALU.add))
                    ins = tt(xbc[:, 4 * g:4 * g + 4, s], xbc[:, 4 * g:4 * g + 4, s], zs[:, 4 * g:4 * g + 4, s], ALU.mult)
                    if c == 0:
                        ins.then_inc(S("ssd_y"), 1)
                    else:
                        link(ins)
                        dve.sem_inc(S("ssd_y"), 1)
                        dve.sem_inc(S("ssd_gated"), 1)
            dve.wait_ge(S("ssd_rg"), 1)
            for j in range(16):
                ins = stt(xbc[:, j, :], xbc[:, j, :], pr("ssd_norm", j), A["rg"][:, j // 4, :], ALU.mult, ALU.mult)
                if j % 2:
                    ins.then_inc(S("ssd_yn"), 1)

        F = carve([("fc", (2, 2 * T)), ("fg", (2, T)), ("hid", (4, T))])
        hid = [F["hid"][:, 2 * s:2 * s + 2, :] for s in range(2)]

        def pe_ffn(pe, l):
            c0, n0, b0 = CH0[f"ffn{l}"], U0[f"ffn{l}"], B0[f"ffn{l}"]
            f0 = 16 * l
            pe.wait_ge(S("h_ready"), 4 * HU[f"ffn_pre{l}"] + 4)
            for j in range(2):
                pe_unit(pe, c0 + j, n0 + j)
            for j in range(2):
                pe_unit(pe, c0 + 2 + j, n0 + 2 + j)
            pe.wait_ge(S("hidden_ready"), f0 + 1)
            pe_down(pe, c0 + 4, b0, hid[0], True, False)
            with pe.Fori(0, 7) as i:
                for k in range(2):
                    for j in range(2):
                        pe_unit(pe, c0 + 5 + 3 * k + j, n0 + 4 + 2 * k + j, i, 6, 4)
                    pe.wait_ge(S("hidden_ready"), i * 2 + (f0 + k + 2))
                    pe_down(pe, c0 + 7 + 3 * k, b0, hid[(k + 1) % 2], False, False, i, 6)
            pe.wait_ge(S("hidden_ready"), f0 + 16)
            pe_down(pe, c0 + 47, b0, hid[1], False, True)

        def act_ffn(ac, l):
            n0 = U0[f"ffn{l}"]
            off = PAR["ffn_conv"] + l * FT * 8
            with ac.Fori(0, 16) as i:
                for k in range(2):
                    ac.wait_ge(S("unit_ready"), i * 2 + (n0 + k + 1))
                    fc = F["fc"][:, k, :]
                    for half in range(2):
                        at = off + 8 * k + 4 * half
                        s = slice(T * half, T * (half + 1))
                        ins = act(fc[:, s], unit[k][:, s], ACT.Identity, bias=par[:, bass.ds(i * 16 + at + 3, 1)],
                                  scale=par[:, bass.ds(i * 16 + at + 2, 1)])
                    ins.then_inc(S("ffn_tap"), 1)
                    ac.wait_ge(S("ffn_taps"), i * 2 + (32 * l + k + 1))
                    act(F["fg"][:, k, :], fc[:, 0:T], ACT.Gelu_apprx_tanh).then_inc(S("ffn_gelu"), 1)

        def dve_ffn(dve, l, link):
            off = PAR["ffn_conv"] + l * FT * 8
            b0, f0 = B0[f"ffn{l}"], 32 * l
            dve.wait_ge(S("unit_free"), U0[f"ffn{l}"] + 2)
            with dve.Fori(0, 8) as i:
                link.enter(i, 4)
                for k in range(4):
                    dve.wait_ge(S("ffn_tap"), i * 4 + (f0 + k + 1))
                    fc, u = F["fc"][:, k % 2, :], unit[k % 2]
                    col = lambda half, tap: par[:, bass.ds(i * 32 + off + 8 * k + 4 * half + tap, 1)]
                    for half in range(2):
                        o = T * half
                        ins = stt(fc[:, o + 1:o + T], u[:, o:o + T - 1], col(half, 1), fc[:, o + 1:o + T],
                                  ALU.mult, ALU.add)
                    link(ins)
                    for half in range(2):
                        o = T * half
                        ins = stt(fc[:, o + 2:o + T], u[:, o:o + T - 2], col(half, 0), fc[:, o + 2:o + T],
                                  ALU.mult, ALU.add)
                    ins.then_inc(S("ffn_taps"), 1)
                    dve.wait_ge(S("ffn_taps"), i * 4 + (f0 + k + 1))
                    dve.sem_inc(S("unit_free"), 1)
                    if k % 2 == 0:
                        dve.wait_ge(S("down_done"), i * 2 + (b0 + k // 2 - 1))
                    dve.wait_ge(S("ffn_gelu"), i * 4 + (f0 + k + 1))
                    ins = tt(hid[k // 2][:, k % 2, :], F["fg"][:, k % 2, :], fc[:, T:2 * T], ALU.mult)
                    if k % 2:
                        ins.then_inc(S("hidden_ready"), 1)
                link.leave(8)

        R = carve([("xb", (LT, T)), ("yb", (LT, T)), ("gx", (LT, T)), ("ga", (LT, T)), ("bt", (LT, T)),
                   ("w", (LT, T)), ("conv", (2, T)), ("pj", (4, T)), ("m", (8, T)), ("cv", (4, LT))])
        cv = [R["cv"][:, k, :] for k in range(4)]

        def pe_lru(pe):
            pe.wait_ge(S("h_ready"), 4 * HU["mix_pre1"] + 4)
            c0, n0 = CH0["lru_in"], U0["lru_in"]
            for j in range(10):
                pe_unit(pe, c0 + j, n0 + j)
            for j in range(LT):
                c = CH0["lru_gates"] + j // 5
                if j % 5 == 0:
                    pe_chunk(pe, c)
                pe.wait_ge(S("lru_conv"), j + 1)
                if j >= 2:
                    pe.wait_ge(S("lru_gate_read"), j - 1)
                b = misc[j % 2]
                w = ring[c % RING]
                for g in range(2):
                    ins = mm(b[:, T * g:T * (g + 1)], w[:, 640 * g + P * (j % 5):640 * g + P * (j % 5) + P],
                             R["xb"][:, j, :], start=(g == 0), stop=(g == 1))
                    begun(c, j % 5 == 0 and g == 0, ins)
                ins.then_inc(S("lru_gate_ps"), 1)
            for j in range(5):
                pe.wait_ge(S("lru_out_ready"), 2 * j + 2)
                pe_down(pe, CH0["lru_out"] + j, B0["lru_out"] + j, R["bt"][:, 2 * j:2 * j + 2, :], j == 0, j == 4)

        def act_lru(ac, link):
            lam = par[:, PAR["lam"]:PAR["lam"] + LT]
            link(act(cv[0], lam, ACT.Abs))
            link(act(cv[1], cv[0], ACT.Exp, scale=-1.0))
            act(cv[1], cv[1], ACT.Ln, bias=one("one")).then_inc(S("lam_log"), 1)
            n0 = U0["lru_in"]
            ac.wait_ge(S("unit_free"), n0 + 2)
            for n in range(5):
                ac.wait_ge(S("unit_ready"), n0 + n + 1)
                for k in range(2):
                    j = 2 * n + k
                    if j >= 4:
                        ac.wait_ge(S("lru_conv"), j - 3)
                    act(R["pj"][:, j % 4, :], unit[n % 2][:, T * k:T * (k + 1)], ACT.Identity,
                        bias=pr("lru_b_in", LT + j)).then_inc(S("lru_proj"), 1)
                ac.wait_ge(S("lru_proj"), 2 * n + 2)
                ac.sem_inc(S("unit_free"), 1)
            for n in range(5, 10):
                ac.wait_ge(S("unit_ready"), n0 + n + 1)
                for k in range(2):
                    j = 2 * (n - 5) + k
                    ins = act(R["yb"][:, j, :], unit[n % 2][:, T * k:T * (k + 1)], ACT.Gelu_apprx_tanh,
                              bias=pr("lru_b_in", j))
                ins.then_inc(S("unit_free"), 1)
            for j in range(LT):
                ac.wait_ge(S("lru_gate_ps"), j + 1)
                act(R["gx"][:, j, :], misc[j % 2][:, 0:T], ACT.Sigmoid, bias=pr("b_gx", j))
                act(R["ga"][:, j, :], misc[j % 2][:, T:2 * T], ACT.Sigmoid,
                    bias=pr("b_ga", j)).then_inc(S("lru_gate_read"), 1)
            ac.wait_ge(S("lru_gate_read"), LT)
            ac.wait_ge(S("lam_done"), 1)
            for j in range(LT):
                act(R["w"][:, j, :], R["ga"][:, j, :], ACT.Tanh, scale=cv[3][:, j:j + 1]).then_inc(S("lru_tanh"), 1)
                ac.wait_ge(S("lru_tanh"), j + 1)
                act(R["ga"][:, j, :], R["ga"][:, j, :], ACT.Exp, scale=cv[3][:, j:j + 1]).then_inc(S("lru_a"), 1)
            for j in range(LT):
                ac.wait_ge(S("lru_m2"), j + 1)
                act(R["w"][:, j, :], R["w"][:, j, :], ACT.Sqrt).then_inc(S("lru_mult"), 1)

        def dve_lru(dve, link):
            lam = par[:, PAR["lam"]:PAR["lam"] + LT]
            dve.wait_ge(S("lam_log"), 1)
            link(ts(cv[2], lam, -1.0, 0.0, ALU.mult, ALU.max))
            link(tt(cv[3], cv[2], cv[1], ALU.add))
            ts(cv[3], cv[3], -8.0, None, ALU.mult).then_inc(S("lam_done"), 1)
            for j in range(LT):
                dve.wait_ge(S("lru_proj"), j + 1)
                src, dst = R["pj"][:, j % 4, :], R["xb"][:, j, :]
                w = lambda k: pr("lru_conv", 5 * j + k)
                link(ts(dst, src, w(3), w(4), ALU.mult, ALU.add))
                link(stt(dst[:, 1:T], src[:, 0:T - 1], w(2), dst[:, 1:T], ALU.mult, ALU.add))
                link(stt(dst[:, 2:T], src[:, 0:T - 2], w(1), dst[:, 2:T], ALU.mult, ALU.add))
                stt(dst[:, 3:T], src[:, 0:T - 3], w(0), dst[:, 3:T], ALU.mult, ALU.add).then_inc(S("lru_conv"), 1)
            for j in range(LT):
                dve.wait_ge(S("lru_tanh"), j + 1)
                w, q = R["w"][:, j, :], R["conv"][:, j % 2, :]
                link(ts(q, w, -1.0, 1.0, ALU.mult, ALU.add))
                link(nc.vector.reciprocal(q, q))
                link(ts(w, w, -2.0, 1e-30, ALU.mult, ALU.max))
                tt(w, w, q, ALU.mult).then_inc(S("lru_m2"), 1)
                tt(R["gx"][:, j, :], R["gx"][:, j, :], R["xb"][:, j, :], ALU.mult).then_inc(S("lru_gated"), 1)
            dve.wait_ge(S("lru_gated"), LT)
            for j in range(LT):
                dve.wait_ge(S("lru_mult"), j + 1)
                dve.wait_ge(S("lru_a"), j + 1)
                link(tt(R["bt"][:, j, :], R["w"][:, j, :], R["gx"][:, j, :], ALU.mult))
                link(nc.vector.tensor_tensor_scan(R["gx"][:, j, :], R["ga"][:, j, :], R["bt"][:, j, :], 0.0,
                                                  ALU.mult, ALU.add))
                tt(R["bt"][:, j, :], R["gx"][:, j, :], R["yb"][:, j, :], ALU.mult).then_inc(S("lru_out_ready"), 1)
            dve.wait_ge(S("down_done"), B0["lru_out"] + 5)
            for t in range(8):
                ins = ts(R["m"][:, t, :], acc8[:, t, :], pr("b_out", t), None, ALU.add)
                if t % 2:
                    ins.then_inc(S("lru_m"), 1)

        def ada_chunk(pool, s, l, i=None):
            a = ada_ring[s]
            base = 4 * ADA_N * l + 4 * s
            i = ADA_N // 2 - 1 if i is None else i
            pool.wait_ge(S(f"ada_loaded{s}"), i * 16 + (16 * (ADA_N // 2) * l + 16))
            nc.gpsimd.tensor_tensor(a[:, :, :], a[:, :, :], cact[:, :].unsqueeze(2).to_broadcast([P, 8, AW]),
                                    ALU.mult).then_inc(S("ada_step"), 1)
            for k, n in enumerate((4, 2)):
                pool.wait_ge(S("ada_step"), i * 8 + (base + k + 1))
                nc.gpsimd.tensor_tensor(a[:, 0:n, :], a[:, 0:n, :], a[:, n:2 * n, :],
                                        ALU.add).then_inc(S("ada_step"), 1)
            pool.wait_ge(S("ada_step"), i * 8 + (base + 3))
            nc.gpsimd.tensor_tensor(ada_acc[:, bass.ds(i * (2 * AW) + AW * s, AW)], a[:, 0, :], a[:, 1, :],
                                    ALU.add).then_inc(S("ada_step"), 1)
            pool.wait_ge(S("ada_step"), i * 8 + (base + 4))

        def ada_load(pool, s, chunk):
            src = ada_in[chunk] if isinstance(chunk, int) else \
                ada_in[bass.ds(chunk, 1)].rearrange("o p k n -> p (o k) n")
            pool.dma_start(ada_ring[s][:, :, :], src).then_inc(S(f"ada_loaded{s}"), 16)

        def pool_ada(pool):
            for s in range(2):
                ada_load(pool, s, s)
            pool.wait_ge(S("c_act"), 1)
            with pool.Fori(0, ADA_N // 2) as i:
                for s in range(2):
                    ada_chunk(pool, s, 0, i)
                    ada_load(pool, s, i * 2 + (2 + s))
            pool.wait_ge(S("mod_ps"), 1)
            with pool.Fori(0, ADA_N // 2 - 1) as i:
                for s in range(2):
                    ada_chunk(pool, s, 1, i)
                    ada_load(pool, s, i * 2 + (ADA_N + 2 + s))
            for s in range(2):
                ada_chunk(pool, s, 1)

        B = carve([("qk", (8, T)), ("vt", (2, 512)), ("z", (4, T)), ("dn", (12, T)), ("ya", (4, T)),
                   ("work", (12900,))])

        def carve_work(sizes):
            at, views = 0, {}
            for name, shape in sizes:
                n = int(np.prod(shape))
                v = B["work"][:, at:at + n]
                if len(shape) == 2:
                    v = v.rearrange("p (a b) -> p a b", b=shape[1])
                elif len(shape) == 3:
                    v = v.rearrange("p (a b c) -> p a b c", b=shape[1], c=shape[2])
                views[name] = v
                at += n
            assert at <= 12900, at
            return views

        HB = (4, P)
        W = carve_work([("kt", (2, 4, P)), ("vt", (2, 4, P)), ("rows", (7, T)), ("tok", (8, 36)), ("dt", (2, 4, P)),
                        ("lt", (2, 4, P)), ("t", (2, 4, P)), ("u", (2, 4, P)), ("qk", (2, 4, P)),
                        ("vb", (2, 4, P)), ("kbg", HB), ("kd", HB), ("w", HB), ("qd", HB), ("s", HB)])
        W2 = carve_work([("sq", (8, T)), ("rot", (8, T)), ("e", (2, 2, T)), ("a", (2, T)), ("at", (2, T)),
                         ("st", (8, 8)), ("lam", (8,))])
        W3 = carve_work([("gate", (16, T)), ("mg", (8, T)), ("mt", (8, T))])
        dconv = W["lt"].rearrange("p c h n -> p (c h n)").rearrange("p (a b) -> p a b", b=T)
        R36 = 36
        RB, RG, RE, RBG, RNG, RKD, RX = (W["rows"][0:R36, k, :] for k in range(7))
        tokd = W["tok"]
        dn = B["dn"]
        dq, dk, dv = dn[:, 0:4, :], dn[:, 4:8, :], dn[:, 8:12, :]
        l2 = W["t"].rearrange("p c h n -> p (c h n)")
        l2k = W["u"].rearrange("p c h n -> p (c h n)")
        flat = lambda v: v.rearrange("p a b -> p (a b)")
        oacc = acc8[:, 4:8, :]

        def first_second(d):
            return (0, 1) if d == 0 else (1, 0)

        def pe_b2_in(pe, l):
            pe.wait_ge(S("ada_step"), 4 * ADA_N * (l + 1))
            for j in range(48):
                ins = mm(misc[1][:, j:j + 1], ada_acc[:, P * j:P * (j + 1)], ones[:, 0:1], start=True, stop=True)
            ins.then_inc(S("mod_ps"), 1)
            pe_norm(pe, f"pre1_{l}")
            pe.wait_ge(S("h_ready"), 4 * HU[f"pre1_{l}"] + 4)
            c0, n0 = CH0[f"in2_{l}"], U0[f"in2_{l}"]
            pe.wait_ge(S("mod_done"), l + 1)
            for g in range(2):
                for k in range(8):
                    at = PAR["ba_w"] + (8 * l + k) * 72 + 36 * g
                    ins = mm(misc[1][0:R36, T * g:T * (g + 1)], par[:, at:at + 36], h[:, k, :],
                             start=(k == 0), stop=(k == 7))
            ins.then_inc(S("ba_ps"), 1)
            for j in range(14):
                pe_unit(pe, c0 + j, n0 + j, tokens_out=(j in (10, 11)))

        def act_b2_in(ac, l, link):
            act_norm(ac, f"pre1_{l}", x, x_ready(ac, "ffn_post1" if l == 0 else "res2_0"))
            ac.wait_ge(S("ba_ps"), l + 1)
            ac.wait_ge(S("a_in"), l + 1)
            act(RB, misc[1][0:R36, 0:T], ACT.Sigmoid).then_inc(S("beta"), 1)
            link(act(RE, RX, ACT.Abs))
            link(act(RE, RE, ACT.Exp, scale=-1.0))
            link(act(RE, RE, ACT.Ln, bias=one("one", R36)))
            act(RG[:, 0:1], pr("A_log", l, R36), ACT.Exp).then_inc(S("a_log_done"), 1)
            ac.wait_ge(S("g_sum"), l + 1)
            act(RE, RG, ACT.Exp)
            act(RNG, RG, ACT.Copy, scale=-1.0)
            for c in range(2):
                s = slice(P * c, P * (c + 1))
                act(RKD[0:32, s], RG[0:32, s], ACT.Exp, bias=RG[0:32, P * c + P - 1:P * c + P], scale=-1.0)
                ins = act(RKD[32:R36, s], RG[32:R36, s], ACT.Exp, bias=RG[32:R36, P * c:P * c + 1], scale=-1.0)
            ins.then_inc(S("g_exps"), 1)
            n0 = U0[f"in2_{l}"]

            def centre(j):
                if j >= 4:
                    ac.wait_ge(S("dn_conv"), 12 * l + j - 3)
                if j % 2 == 0:
                    ac.wait_ge(S("unit_ready"), n0 + j // 2 + 1)
                act(dconv[:, j % 4, :], unit[(j // 2) % 2][:, T * (j % 2):T * (j % 2 + 1)], ACT.Identity, bias=one("zero"), scale=pr("dn_conv", 60 * l + 5 * j + 2)).then_inc(S("dn_tap"), 1)

            centre(0)
            centre(1)
            for j in range(12):
                if j + 2 < 12:
                    centre(j + 2)
                ac.wait_ge(S("dn_taps"), 12 * l + j + 1)
                act(dn[:, j, :], dconv[:, j % 4, :], ACT.Silu).then_inc(S("dn_conv"), 1)
            ac.wait_ge(S("unit_free"), n0 + 6 + 2)
            for j in range(6, 14):
                ac.wait_ge(S("unit_ready"), n0 + j + 1)
                u = unit[(n0 + j) % 2]
                if j < 10:
                    ins = act(B["qk"][:, 2 * (j - 6):2 * (j - 6) + 2, :], u[:, :], ACT.Copy)
                elif j < 12:
                    ins = act(B["vt"][:, :, T * (j - 10):T * (j - 9)], u[:, :].rearrange("p (a b) -> p a b", b=T), ACT.Copy)
                else:
                    ins = act(B["z"][:, 2 * (j - 12):2 * (j - 12) + 2, :], u[:, :], ACT.Silu)
                ins.then_inc(S("unit_free"), 1)

        def dve_b2_in(dve, l, link):
            dve.wait_ge(S("mod_ps"), l + 1)
            if l == 1:
                dve.wait_ge(S("x_ready"), 4 * XU["res2_0"] + 4)
            link(tt(mod[:, :], misc[1][:, 0:48], par[:, PAR["ada_b"] + 48 * l:PAR["ada_b"] + 48 * (l + 1)], ALU.add))
            for k, name in enumerate(("n1", "n2")):
                w = par[:, PAR[name] + 8 * l:PAR[name] + 8 * (l + 1)]
                ins = stt(gsc[:, 8 * k:8 * (k + 1)], mod[:, 24 * k + 8:24 * k + 16], 1.0, w, ALU.add, ALU.mult)
            link(ins)
            dve.sem_inc(S("mod_done"), 1)
            dve_modulated(dve, link, f"pre1_{l}", 0)
            dve.wait_ge(S("ba_ps"), l + 1)
            ts(RX, misc[1][0:R36, T:2 * T], pr("dn_dt", l, R36), None, ALU.add).then_inc(S("a_in"), 1)
            dve.wait_ge(S("a_log_done"), l + 1)
            link(stt(RX, RX, 0.0, RE, ALU.max, ALU.add))
            link(ts(RX, RX, RG[:, 0:1], -1.0, ALU.mult, ALU.mult))
            link(nc.vector.memset(RKD, 1.0))
            for c in range(2):
                a, z = P * c, P * (c + 1)
                nc.vector.tensor_tensor_scan(RG[0:32, a:z], RKD[0:32, a:z], RX[0:32, a:z], 0.0, ALU.mult, ALU.add)
                back = lambda v: v[32:R36, a:z][:, ::-1]
                ins = nc.vector.tensor_tensor_scan(back(RG), back(RKD), back(RX), 0.0, ALU.mult, ALU.add)
            ins.then_inc(S("g_sum"), 1)
            dve.wait_ge(S("beta"), l + 1)
            dve.wait_ge(S("g_exps"), l + 1)
            tt(RBG, RB, RE, ALU.mult).then_inc(S("dn_rows"), 1)
            dve.wait_ge(S("unit_free"), U0[f"in2_{l}"] + 2)
            for j in range(12):
                if j % 2 == 0:
                    dve.wait_ge(S("dn_tap"), 12 * l + j + 2)
                src = unit[(j // 2) % 2][:, T * (j % 2):T * (j % 2 + 1)]
                dst = dconv[:, j % 4, :]
                w = lambda k: pr("dn_conv", 60 * l + 5 * j + k)
                link(stt(dst[:, 1:T], src[:, 0:T - 1], w(1), dst[:, 1:T], ALU.mult, ALU.add))
                link(stt(dst[:, 2:T], src[:, 0:T - 2], w(0), dst[:, 2:T], ALU.mult, ALU.add))
                link(stt(dst[:, 0:T - 1], src[:, 1:T], w(3), dst[:, 0:T - 1], ALU.mult, ALU.add))
                stt(dst[:, 0:T - 2], src[:, 2:T], w(4), dst[:, 0:T - 2], ALU.mult, ALU.add).then_inc(S("dn_taps"), 1)
                if j % 2:
                    dve.wait_ge(S("dn_taps"), 12 * l + j + 1)
                    dve.sem_inc(S("unit_free"), 1)

        def dve_modulated(dve, link, name, k0):
            dve.wait_ge(S("rstd_ready"), NI[name] + 1)
            for q in range(4):
                s = tmp[:, 2 * (q % 2):2 * (q % 2) + 2, :]
                for k in range(2):
                    t = 2 * q + k
                    ins = stt(s[:, k, :], x[:, t, :], gsc[:, 8 * k0 + t:8 * k0 + t + 1], rstd[:, :], ALU.mult, ALU.mult)
                link(ins)
                for k in range(2):
                    t = 2 * q + k
                    ins = ts(h[:, t, :], s[:, k, :], mod[:, 24 * k0 + t:24 * k0 + t + 1], None, ALU.add)
                ins.then_inc(S("h_ready"), 1)

        def heads(b):
            return b.rearrange("p (h n) -> p h n", n=P)

        def pe_delta(pe, l):
            for k in range(8):
                if k % 4 == 0:
                    pe.wait_ge(S("dn_sq"), 2 * l + k // 4 + 1)
                src = (l2 if k < 4 else l2k)[:, T * (k % 4):T * (k % 4 + 1)]
                ins = mm(acc8[:, k, :], ones, src, start=(k % 2 == 0), stop=(k % 2 == 1))
            ins.then_inc(S("dn_ssum"), 1)
            pe.wait_ge(S("dn_rows"), l + 1)
            for c in range(2):
                for k, r in enumerate((RB, RNG, RBG, RKD)):
                    at = 36 * (4 * c + k)
                    ins = nc.tensor.transpose(misc[1][:, at:at + 36], r[:, P * c:P * (c + 1)], ident[0:R36, 0:R36])
            ins.then_inc(S("dn_tok_ps"), 1)
            pe.wait_ge(S("unit_free"), U0[f"in2_{l}"] + 14 + 2)
            pe.wait_ge(S("dn_unit"), l + 1)
            for c in range(2):
                for hd in range(4):
                    ins = nc.tensor.transpose(unit[c][:, P * hd:P * (hd + 1)], dk[:, hd, P * c:P * (c + 1)], ident)
                ins.then_inc(S("dn_kt_ps"), 1)
            pe.wait_ge(S("dn_tok"), l + 1)
            for c in range(2):
                for hd in range(4):
                    ins = nc.tensor.transpose(misc[c][:, P * hd:P * (hd + 1)], dv[:, hd, P * c:P * (c + 1)], ident)
                ins.then_inc(S("dn_vt_ps"), 1)
            pe.wait_ge(S("dn_kt"), 2 * l + 2)
            pe.wait_ge(S("dn_vt"), 2 * l + 2)
            for d in range(2):
                n = 2 * l + d
                row = lambda r, hd: (ident[0:R36, 32 * d + hd:32 * d + hd + 1].to_broadcast([R36, P]), r)
                if d == 1:
                    pe.wait_ge(S("dn_dir_done"), n)
                for c in range(2):
                    s = slice(P * c, P * (c + 1))
                    for hd in range(4):
                        sel, r = row(RG, hd)
                        mm(unit[c][:, P * hd:P * (hd + 1)], sel, r[:, s], start=(hd == 0), stop=False, skip_group_check=True)
                    for hd in range(4):
                        ins = mm(unit[c][:, P * hd:P * (hd + 1)], ident, cn("neg_up" if d == 0 else "neg_lo"),
                                 start=False, stop=(hd == 3), skip_group_check=True)
                    ins.then_inc(S("dn_decay_ps"), 1)
                    for hd in range(4):
                        mm(misc[c][:, P * hd:P * (hd + 1)], dk[:, hd, s], dk[:, hd, s], start=True, stop=True)
                    for hd in range(4):
                        ins = mm(bank(c, P * hd, P * (hd + 1)), dk[:, hd, s], dq[:, hd, s], start=True, stop=True)
                    ins.then_inc(S("dn_kk_ps"), 1)
                for c in range(2):
                    pe.wait_ge(S("dn_decay"), 2 * n + c + 1)
                    for hd in range(4):
                        sel, r = row(RB, hd)
                        ins = mm(unit[c][:, P * hd:P * (hd + 1)], sel, r[:, P * c:P * (c + 1)], start=True, stop=True)
                    ins.then_inc(S("dn_beta_ps"), 1)
                for c in range(2):
                    pe.wait_ge(S("dn_lt"), 2 * n + c + 1)
                    for hd in range(4):
                        ins = mm(unit[c][:, P * hd:P * (hd + 1)], W["lt"][:, c, hd, :], ident, start=True, stop=True)
                    ins.then_inc(S("dn_a_ps"), 1)
                for v in range(1, 7):
                    m = 7 * n + v
                    for c in range(2):
                        pe.wait_ge(S("dn_t"), 2 * (m - n) - 2 + c + 1)
                        for hd in range(4):
                            ins = mm(unit[c][:, P * hd:P * (hd + 1)], W["lt"][:, c, hd, :], W["t"][:, c, hd, :],
                                     start=True, stop=True)
                        ins.then_inc(S("dn_a_ps"), 1)
                    for c in range(2):
                        pe.wait_ge(S("dn_u"), 2 * m - 2 + c + 1)
                        pe.wait_ge(S("dn_a"), 2 * m + c + 1)
                        for hd in range(4):
                            ins = mm(bank(c, P * hd, P * (hd + 1)), W["dt"][:, c, hd, :], W["u"][:, c, hd, :],
                                     start=True, stop=True)
                        if v < 6:
                            for hd in range(4):
                                ins = mm(misc[c][:, P * hd:P * (hd + 1)], W["u"][:, c, hd, :], W["dt"][:, c, hd, :],
                                         start=True, stop=True)
                        ins.then_inc(S("dn_de_ps"), 1)
                c1, c2 = first_second(d)
                s2 = slice(P * c2, P * (c2 + 1))
                pe.wait_ge(S("dn_u"), 14 * n + 14)
                for hd in range(4):
                    sel, r = row(RE, hd)
                    ins = mm(unit[0][:, P * hd:P * (hd + 1)], sel, r[:, s2], start=True, stop=True)
                ins.then_inc(S("dn_eg_ps"), 1)
                pe.wait_ge(S("dn_vb"), n + 1)
                for hd in range(4):
                    ins = mm(misc[0][:, P * hd:P * (hd + 1)], W["u"][:, c1, hd, :], W["vb"][:, c1, hd, :],
                             start=True, stop=True)
                ins.then_inc(S("dn_v1_ps"), 1)
                for hd in range(4):
                    ins = mm(bank(0, P * hd, P * (hd + 1)), W["kbg"][:, hd, :], W["u"][:, c2, hd, :], start=True, stop=True)
                ins.then_inc(S("dn_w_ps"), 1)
                pe.wait_ge(S("dn_v1"), n + 1)
                for hd in range(4):
                    ins = mm(bank(1, P * hd, P * (hd + 1)), W["kd"][:, hd, :], W["vb"][:, c1, hd, :], start=True, stop=True)
                ins.then_inc(S("dn_s_ps"), 1)
                for hd in range(4):
                    mm(oacc[:, hd, P * c1:P * (c1 + 1)], W["vb"][:, c1, hd, :], W["qk"][:, c1, hd, :],
                       start=(d == 0 and hd % 2 == 0), stop=False)
                for hd in range(4):
                    mm(misc[1][:, P * hd:P * (hd + 1)], W["u"][:, c2, hd, :], W["vb"][:, c2, hd, :],
                       start=(hd == 0), stop=False)
                pe.wait_ge(S("dn_w"), n + 1)
                pe.wait_ge(S("dn_s"), n + 1)
                for hd in range(4):
                    ins = mm(misc[1][:, P * hd:P * (hd + 1)], W["w"][:, hd, :], W["s"][:, hd, :], start=False, stop=(hd == 3))
                ins.then_inc(S("dn_v2_ps"), 1)
                pe.wait_ge(S("dn_qd"), n + 1)
                for hd in range(4):
                    mm(oacc[:, hd, s2], W["s"][:, hd, :], W["qd"][:, hd, :], start=False, stop=False)
                pe.wait_ge(S("dn_v2"), n + 1)
                for hd in range(4):
                    ins = mm(oacc[:, hd, s2], W["vb"][:, c2, hd, :], W["qk"][:, c2, hd, :], start=False,
                             stop=(d == 1 and hd % 2 == 1))
                ins.then_inc(S("dn_o_ps"), 1)
            pe.wait_ge(S("o_sq"), 2 * l + 1)
            for hd in range(4):
                ins = mm(unit[hd // 2][:, T * (hd % 2):T * (hd % 2 + 1)], ones, l2[:, T * hd:T * (hd + 1)],
                         start=(hd % 2 == 0), stop=(hd % 2 == 1))
            ins.then_inc(S("o_ssum"), 1)

        def act_delta(ac, l, link):
            for k in range(2):
                if k == 0:
                    ac.wait_ge(S("dn_conv"), 12 * l + 8)
                act((l2, l2k)[k], dn[:, 4 * k:4 * k + 4, :], ACT.Square).then_inc(S("dn_sq"), 1)
            ac.wait_ge(S("dn_ssum"), l + 1)
            for k in range(2):
                link(act((l2, l2k)[k], acc[:, 1024 * k:1024 * (k + 1)], ACT.Ln, bias=one("eps")))
            for k in range(2):
                act((l2, l2k)[k], (l2, l2k)[k], ACT.Exp, scale=-0.5).then_inc(S("dn_rnorm"), 1)
            for c in range(2):
                ac.wait_ge(S("dn_kt_ps"), 2 * l + c + 1)
                act(W["kt"][:, c, :, :], unit[c][:, :], ACT.Copy).then_inc(S("dn_kt"), 1)
            for d in range(2):
                n = 2 * l + d
                for c in range(2):
                    ac.wait_ge(S("dn_decay_ps"), 2 * n + c + 1)
                    for hd in range(4):
                        ins = act(W["dt"][:, c, hd, :], unit[c][:, P * hd:P * (hd + 1)], ACT.Exp,
                                  bias=tokd[:, 4 * c + 1, 32 * d + hd:32 * d + hd + 1])
                    ins.then_inc(S("dn_decay"), 1)
                ac.wait_ge(S("dn_w_ps"), n + 1)
                act(flat(W["w"]), bank(0, 0, 512), ACT.Copy, scale=-1.0).then_inc(S("dn_w"), 1)
                ac.wait_ge(S("dn_s_ps"), n + 1)
                act(flat(W["s"]), bank(1, 0, 512), ACT.Copy).then_inc(S("dn_s"), 1)
            ac.wait_ge(S("dn_o_ps"), 2 * l + 2)
            act_onorm(ac, 2 * l, l2, l2)

        def act_onorm(ac, n, sq, out):
            act(sq, acc[:, 1024:2048], ACT.Square).then_inc(S("o_sq"), 1)
            ac.wait_ge(S("o_ssum"), n + 1)
            for k in range(2):
                ins = act(out[:, 512 * k:512 * (k + 1)], unit[k][:, :], ACT.Ln, bias=one("eps"), scale=1.0 / P)
            ins.then_inc(S("o_log"), 1)
            ac.wait_ge(S("o_log"), n + 1)
            act(out, out, ACT.Exp, scale=-0.5).then_inc(S("o_rms"), 1)

        def dve_delta(dve, l, link):
            for k in range(2):
                dve.wait_ge(S("dn_rnorm"), 2 * l + k + 1)
                v = dn[:, 4 * k:4 * k + 4, :].rearrange("p a b -> p (a b)")
                link(stt(v, v, P ** -0.5 if k == 0 else 1.0, (l2, l2k)[k], ALU.mult, ALU.mult))
            dve.sem_inc(S("dn_unit"), 1)
            dve.wait_ge(S("dn_tok_ps"), l + 1)
            nc.vector.tensor_copy(tokd, misc[1][:, 0:288].rearrange("p (a b) -> p a b", b=36)).then_inc(S("dn_tok"), 1)
            for c in range(2):
                dve.wait_ge(S("dn_vt_ps"), 2 * l + c + 1)
                nc.vector.tensor_copy(W["vt"][:, c, :, :], heads(misc[c][:, :])).then_inc(S("dn_vt"), 1)
            dve.wait_ge(S("dn_kt"), 2 * l + 2)
            dve.wait_ge(S("dn_vt"), 2 * l + 2)
            dve.wait_ge(S("dn_tok"), l + 1)
            for d in range(2):
                n = 2 * l + d
                c1, c2 = first_second(d)
                col = lambda c, k: tokd[:, 4 * c + k, 32 * d:32 * d + 4].unsqueeze(2).to_broadcast([P, 4, P])
                for c in range(2):
                    tt(W["vb"][:, c, :, :], W["vt"][:, c, :, :], col(c, 0), ALU.mult)
                tt(W["kbg"], W["kt"][:, c2, :, :], col(c2, 2), ALU.mult)
                tt(W["kd"], W["kt"][:, c1, :, :], col(c1, 3), ALU.mult).then_inc(S("dn_vb"), 1)
                for c in range(2):
                    dve.wait_ge(S("dn_decay"), 2 * n + c + 1)
                    dve.wait_ge(S("dn_kk_ps"), 2 * n + c + 1)
                    dt = W["dt"][:, c, :, :]
                    tt(W["qk"][:, c, :, :], heads(bank(c, 0, 512)), dt, ALU.mult)
                    link(tt(W["lt"][:, c, :, :], heads(misc[c][:, :]), dt, ALU.mult))
                    dve.wait_ge(S("dn_beta_ps"), 2 * n + c + 1)
                    tt(W["lt"][:, c, :, :], W["lt"][:, c, :, :], heads(unit[c][:, :]), ALU.mult).then_inc(S("dn_lt"), 1)
                level = lambda v, k: cn("level", P * (2 * v + (k + d) % 2)).unsqueeze(1).to_broadcast([P, 4, P])
                eye = ident.unsqueeze(1).to_broadcast([P, 4, P])
                for v in range(7):
                    m = 7 * n + v
                    for c in range(2):
                        a, tm, um = W["dt"][:, c, :, :], W["t"][:, c, :, :], W["u"][:, c, :, :]
                        dve.wait_ge(S("dn_a_ps"), 2 * m + c + 1)
                        tt(a, heads(unit[c][:, :]), level(v, 0), ALU.mult).then_inc(S("dn_a"), 1)
                        if v == 0:
                            link(tt(um, W["lt"][:, c, :, :], level(0, 1), ALU.mult))
                            tt(um, eye, um, ALU.subtract).then_inc(S("dn_u"), 1)
                            dve.wait_ge(S("dn_a"), 2 * m + c + 1)
                            tt(tm, eye, a, ALU.subtract).then_inc(S("dn_t"), 1)
                    if v > 0:
                        for c in range(2):
                            tm, um = W["t"][:, c, :, :], W["u"][:, c, :, :]
                            dve.wait_ge(S("dn_de_ps"), 2 * (m - n - 1) + c + 1)
                            if v < 6:
                                tt(tm, tm, heads(misc[c][:, :]), ALU.subtract).then_inc(S("dn_t"), 1)
                            tt(um, um, heads(bank(c, 0, 512)), ALU.subtract).then_inc(S("dn_u"), 1)
                dve.wait_ge(S("dn_eg_ps"), n + 1)
                tt(W["qd"], dq[:, :, P * c2:P * (c2 + 1)], heads(unit[0][:, :]), ALU.mult).then_inc(S("dn_qd"), 1)
                dve.wait_ge(S("dn_v1_ps"), n + 1)
                nc.vector.tensor_copy(W["vb"][:, c1, :, :], heads(misc[0][:, :])).then_inc(S("dn_v1"), 1)
                dve.wait_ge(S("dn_v2_ps"), n + 1)
                nc.vector.tensor_copy(W["vb"][:, c2, :, :], heads(misc[1][:, :])).then_inc(S("dn_v2"), 1)
                dve.wait_ge(S("dn_o_ps"), n + 1)
                dve.sem_inc(S("dn_dir_done"), 1)
            dve.wait_ge(S("o_rms"), 2 * l + 1)
            yb = dn[:, 0:4, :].rearrange("p a b -> p (a b)")
            link(stt(yb, acc[:, 1024:2048], pr("dn_gain", l), l2, ALU.mult, ALU.mult))
            tt(yb, yb, flat(B["z"]), ALU.mult).then_inc(S("yb_done"), 1)

        sq8 = W2["sq"].rearrange("p a b -> p (a b)")
        qk8 = B["qk"].rearrange("p a b -> p (a b)")

        def sbank(n, t):
            return unit[n % 2][:, 0:T] if t == 0 else bank(n % 2, 0, T)

        def lambda_init(l):
            return 0.8 - 0.6 * math.exp(-0.3 * l)

        def pe_attn(pe, l):
            for k in range(8):
                pe.wait_ge(S("at_sq"), 2 * l + k // 4 + 1)
                ins = mm(acc8[:, k, :], cn("half_ones"), W2["sq"][:, k, :], start=(k % 2 == 0), stop=(k % 2 == 1))
            ins.then_inc(S("at_ssum"), 1)
            pe.wait_ge(S("at_lam_in"), l + 1)
            mm(misc[1][:, 0:2], ones[0:64, :], W2["lam"][0:64, 0:2], start=True, stop=True).then_inc(S("at_lam_ps"), 1)
            pe.wait_ge(S("at_unit"), l + 1)
            for k in range(8):
                ins = mm(acc8[:, k, :], cn("rope"), B["qk"][:, k, :], start=(k % 2 == 0), stop=(k % 2 == 1))
            ins.then_inc(S("at_rot_ps"), 1)
            pe.wait_ge(S("at_rope"), l + 1)
            pe.wait_ge(S("at_lam"), l + 1)

            def scores(n):
                hd, qb = n // 2, n % 2
                if n >= 2:
                    pe.wait_ge(S("at_exp"), 8 * l + n - 1)
                for t in range(2):
                    r = slice(64 * t, 64 * (t + 1))
                    ins = mm(sbank(n, t), B["qk"][r, hd, P * qb:P * (qb + 1)], B["qk"][r, 4 + hd, :],
                             start=True, stop=True)
                ins.then_inc(S("at_s_ps"), 1)

            scores(0)
            for n in range(8):
                hd, qb = n // 2, n % 2
                if n + 1 < 8:
                    scores(n + 1)
                pe.wait_ge(S("at_a"), 8 * l + n + 1)
                if n >= 2:
                    pe.wait_ge(S("at_at"), 8 * l + n - 1)
                for kb in range(2):
                    ins = nc.tensor.transpose(misc[n % 2][:, P * kb:P * (kb + 1)], W2["a"][:, n % 2, P * kb:P * (kb + 1)],
                                              ident)
                ins.then_inc(S("at_at_ps"), 1)
                pe.wait_ge(S("at_at"), 8 * l + n + 1)
                for kb in range(2):
                    ins = mm(oacc[:, hd, P * qb:P * (qb + 1)], B["vt"][:, kb, P * hd:P * (hd + 1)],
                             W2["at"][:, n % 2, P * kb:P * (kb + 1)], start=(kb == 0), stop=(kb == 1))
                ins.then_inc(S("at_o_ps"), 1)
            pe.wait_ge(S("o_sq"), 2 * l + 2)
            for hd in range(4):
                ins = mm(unit[hd // 2][:, T * (hd % 2):T * (hd % 2 + 1)], ones, W2["sq"][:, hd, :],
                         start=(hd % 2 == 0), stop=(hd % 2 == 1))
            ins.then_inc(S("o_ssum"), 1)

        def act_attn(ac, l, link):
            ac.wait_ge(S("yb_done"), l + 1)
            for k in range(2):
                act(sq8[:, 1024 * k:1024 * (k + 1)], qk8[:, 1024 * k:1024 * (k + 1)], ACT.Square).then_inc(S("at_sq"), 1)
            ac.wait_ge(S("at_ssum"), l + 1)
            for k in range(2):
                link(act(sq8[:, 1024 * k:1024 * (k + 1)], acc[:, 1024 * k:1024 * (k + 1)], ACT.Ln, bias=one("eps"),
                         scale=1.0 / 64))
            for k in range(2):
                s = sq8[:, 1024 * k:1024 * (k + 1)]
                act(s, s, ACT.Exp, scale=-0.5).then_inc(S("at_rnorm"), 1)
            ac.wait_ge(S("at_lam_ps"), l + 1)
            act(W2["lam"][:, 2:4], misc[1][:, 0:2], ACT.Exp).then_inc(S("at_lam_exp"), 1)
            for n in range(8):
                ac.wait_ge(S("at_max"), 8 * l + n + 1)
                if n >= 2:
                    ac.wait_ge(S("at_a"), 8 * l + n - 1)
                for t in range(2):
                    ins = act(W2["e"][:, n % 2, t, :], sbank(n, t), ACT.Exp, scale=0.125,
                              bias=W2["st"][:, n, 2 + t:3 + t], accum_out=W2["st"][:, n, 4 + t:5 + t])
                ins.then_inc(S("at_exp"), 1)
                ac.wait_ge(S("at_at_ps"), 8 * l + n + 1)
                if n >= 2:
                    ac.wait_ge(S("at_o_ps"), 8 * l + n - 1)
                act(W2["at"][:, n % 2, :], misc[n % 2][:, 0:T], ACT.Copy).then_inc(S("at_at"), 1)
            ac.wait_ge(S("at_o_ps"), 8 * l + 8)
            act_onorm(ac, 2 * l + 1, sq8[:, 0:1024], sq8[:, 0:1024])

        def dve_attn(dve, l, link):
            lam, st = W2["lam"], W2["st"]
            dve.wait_ge(S("yb_done"), l + 1)
            dl = par[0:64, PAR["dlam"] + 4 * l:PAR["dlam"] + 4 * l + 4].rearrange("p (a b) -> p a b", b=2)
            tt(lam[0:64, 0:2], dl[:, :, 0], dl[:, :, 1], ALU.mult).then_inc(S("at_lam_in"), 1)
            for k in range(2):
                dve.wait_ge(S("at_rnorm"), 2 * l + k + 1)
                v = qk8[:, 1024 * k:1024 * (k + 1)]
                link(stt(v, v, pr("qk_gain", 2 * l + k), sq8[:, 1024 * k:1024 * (k + 1)], ALU.mult, ALU.mult))
            dve.sem_inc(S("at_unit"), 1)
            dve.wait_ge(S("at_lam_exp"), l + 1)
            link(tt(lam[:, 4:5], lam[:, 3:4], lam[:, 2:3], ALU.subtract))
            ts(lam[:, 5:6], lam[:, 4:5], -lambda_init(l), None, ALU.add)
            ts(lam[:, 6:7], pr("subln", l), 1.0 - lambda_init(l), None, ALU.mult).then_inc(S("at_lam"), 1)
            dve.wait_ge(S("at_rot_ps"), l + 1)
            wide = lambda name: cn(name, 0, T).unsqueeze(1).to_broadcast([P, 8, T])
            tt(W2["rot"], acc8[:, :, :], wide("sin"), ALU.mult)
            link(tt(B["qk"], B["qk"], wide("cos"), ALU.mult))
            tt(B["qk"], B["qk"], W2["rot"], ALU.add).then_inc(S("at_rope"), 1)

            def maximum(n):
                dve.wait_ge(S("at_s_ps"), 8 * l + n + 1)
                for t in range(2):
                    ins = nc.vector.tensor_reduce(st[:, n, t:t + 1], sbank(n, t), AX.X, ALU.max)
                link(ins)
                ts(st[:, n, 2:4], st[:, n, 0:2], -0.125, None, ALU.mult).then_inc(S("at_max"), 1)

            maximum(0)
            for n in range(8):
                if n + 1 < 8:
                    maximum(n + 1)
                dve.wait_ge(S("at_exp"), 8 * l + n + 1)
                link(nc.vector.reciprocal(st[:, n, 6:8], st[:, n, 4:6]))
                link(tt(st[:, n, 7:8], st[:, n, 7:8], lam[:, 5:6], ALU.mult))
                if n >= 2:
                    dve.wait_ge(S("at_at_ps"), 8 * l + n - 1)
                a = W2["a"][:, n % 2, :]
                link(ts(a, W2["e"][:, n % 2, 0, :], st[:, n, 6:7], None, ALU.mult))
                stt(a, W2["e"][:, n % 2, 1, :], st[:, n, 7:8], a, ALU.mult, ALU.add).then_inc(S("at_a"), 1)
            dve.wait_ge(S("o_rms"), 2 * l + 2)
            stt(flat(B["ya"]), acc[:, 1024:2048], lam[:, 6:7], sq8[:, 0:1024], ALU.mult, ALU.mult).then_inc(S("ya_done"), 1)

        def pe_merge(pe, l):
            c0, n0 = CH0[f"in2_{l}"] + 14, U0[f"in2_{l}"] + 14
            pe.wait_ge(S("ya_done"), l + 1)
            for j in range(8):
                pe_unit(pe, c0 + j, n0 + j)
            for j in range(2):
                pe_down(pe, CH0[f"bra_{l}"] + j, 0, B["ya"][:, 2 * j:2 * j + 2, :], j == 0, j == 1)
            pe.wait_ge(S("merge_a"), 4 * l + 4)
            for j in range(2):
                pe_down(pe, CH0[f"brb_{l}"] + j, 0, dn[:, 2 * j:2 * j + 2, :], j == 0, j == 1)
            pe.wait_ge(S("merged"), 4 * l + 4)
            for j in range(4):
                pe_down(pe, CH0[f"out2_{l}"] + j, 0, W3["mg"][:, 2 * j:2 * j + 2, :], j == 0, j == 3)

        def act_merge(ac, l):
            n0 = U0[f"in2_{l}"] + 14
            ac.wait_ge(S("ya_done"), l + 1)
            for j in range(8):
                ac.wait_ge(S("unit_ready"), n0 + j + 1)
                act(W3["gate"][:, 2 * j:2 * j + 2, :], unit[(n0 + j) % 2][:, :], ACT.Sigmoid).then_inc(S("unit_free"), 1)

        def dve_merge(dve, l, link):
            gate, mg, mt = W3["gate"], W3["mg"], W3["mt"]
            dve.wait_ge(S("down_done"), B0[f"bra_{l}"] + 2)
            dve.wait_ge(S("unit_free"), U0[f"in2_{l}"] + 22 + 2)
            for q in range(4):
                s = slice(2 * q, 2 * q + 2)
                tt(mg[:, s, :], acc8[:, s, :], gate[:, s, :], ALU.mult).then_inc(S("merge_a"), 1)
            dve.wait_ge(S("down_done"), B0[f"brb_{l}"] + 2)
            for q in range(4):
                s = slice(2 * q, 2 * q + 2)
                link(tt(mt[:, s, :], acc8[:, s, :], gate[:, 8 + 2 * q:10 + 2 * q, :], ALU.mult))
                tt(mg[:, s, :], mg[:, s, :], mt[:, s, :], ALU.add).then_inc(S("merged"), 1)

        M = carve([("r", (2, 2, T)), ("hid", (2, 2, T))])

        def pe_mlp(pe, l):
            c0, n0, b0 = CH0[f"mlp_{l}"], U0[f"mlp_{l}"], B0[f"mlp_{l}"]
            pe.wait_ge(S("h_ready"), 4 * HU[f"pre2_{l}"] + 4)
            pe_unit(pe, c0, n0)
            pe_unit(pe, c0 + 1, n0 + 1)
            pe.wait_ge(S("mlp_hidden"), 16 * l + 1)
            pe_down(pe, c0 + 2, b0, M["hid"][:, 0, :, :], True, False)
            with pe.Fori(0, 2) as i:
                for k in range(6):
                    pe_unit(pe, c0 + 3 + 2 * k, n0 + 2 + k, i, 12, 6)
                    pe.wait_ge(S("mlp_hidden"), i * 6 + (16 * l + k + 2))
                    pe_down(pe, c0 + 4 + 2 * k, b0, M["hid"][:, (k + 1) % 2, :, :], False, False, i, 12)
            for k in range(13, 16):
                if k < 15:
                    pe_unit(pe, c0 + 1 + 2 * k, n0 + 1 + k)
                pe.wait_ge(S("mlp_hidden"), 16 * l + k + 1)
                pe_down(pe, c0 + (2 + 2 * k if k < 15 else 31), b0, M["hid"][:, k % 2, :, :], False, k == 15)

        def act_mlp(ac, l):
            n0 = U0[f"mlp_{l}"]
            with ac.Fori(0, 8) as i:
                for k in range(2):
                    ac.wait_ge(S("unit_ready"), i * 2 + (n0 + k + 1))
                    ac.wait_ge(S("mlp_free"), i * 2 + (16 * l + k + 1))
                    act(M["r"][:, k, :, :], unit[(n0 + k) % 2][:, :], ACT.Relu).then_inc(S("unit_free"), 1)

        def dve_mlp(dve, l):
            n0, b0 = U0[f"mlp_{l}"], B0[f"mlp_{l}"]
            if l == 0:
                dve.sem_inc(S("mlp_free"), 2)
            with dve.Fori(0, 8) as i:
                for k in range(2):
                    dve.wait_ge(S("unit_free"), i * 2 + (n0 + k + 3))
                    dve.wait_ge(S("down_done"), i * 2 + (b0 + k - 1))
                    r = M["r"][:, k, :, :]
                    tt(M["hid"][:, k, :, :], r, r, ALU.mult).then_inc(S("mlp_hidden"), 1)
                    dve.wait_ge(S("mlp_hidden"), i * 2 + (16 * l + k + 1))
                    dve.sem_inc(S("mlp_free"), 1)

        block = ctx.enter_context(nc.Block())

        @block.sync
        def _(sp):
            def load(c):
                sp.dma_start(ring[c % RING][:, :], w_in[c]).then_inc(loaded[c % RING], 16)
            sp.dma_start(x[:, :, :], x_in).then_inc(S("x_loaded"), 16)
            for c in range(RING):
                load(c)
            turns = NCHUNK // RING
            with sp.Fori(1, turns) as i:
                for s in range(RING):
                    sp.wait_ge(S("chunk_begun"), i * RING + (s - RING + 1))
                    sp.dma_start(ring[s][:, :], w_in[bass.ds(i * RING + s, 1)].rearrange("o p n -> p (o n)")
                                 ).then_inc(loaded[s], 16)
            for c in range(turns * RING, NCHUNK):
                sp.wait_ge(S("chunk_begun"), c - RING + 1)
                load(c)
            for q in range(4):
                sp.wait_ge(S("x_ready"), 4 * XU["res2_1"] + q + 1)
                sp.dma_start(out[:, 2 * q:2 * q + 2, :], x[:, 2 * q:2 * q + 2, :]).then_inc(S("stored"), 16)
            sp.wait_ge(S("stored"), 64)

        @block.gpsimd
        def _(pool):
            pool_ada(pool)

        @block.tensor
        def _(pe):
            pe.wait_ge(S("con_loaded"), 16)
            pe.wait_ge(S("par_loaded"), 16)
            pe_norm(pe, "mix_pre0")
            pe_ssd(pe)
            pe_norm(pe, "mix_post0")
            pe_norm(pe, "ffn_pre0")
            pe_ffn(pe, 0)
            pe_norm(pe, "ffn_post0")
            pe_norm(pe, "mix_pre1")
            pe_lru(pe)
            pe_norm(pe, "mix_post1")
            pe_norm(pe, "ffn_pre1")
            pe_ffn(pe, 1)
            pe_norm(pe, "ffn_post1")
            for l in range(2):
                pe_b2_in(pe, l)
                pe_delta(pe, l)
                pe_attn(pe, l)
                pe_merge(pe, l)
                pe_norm(pe, f"pre2_{l}")
                pe_mlp(pe, l)

        @block.scalar
        def _(ac):
            ac.dma_start(par[:, :], par_in).then_inc(S("par_loaded"), 16)
            ac.dma_start(con[:, :], con_in).then_inc(S("con_loaded"), 16)
            link = Chain(ac, S("act_link"))
            from_acc = lambda name: (lambda q: ac.wait_ge(S("down_done"), B0[name[0]] + name[1]))
            ac.wait_ge(S("par_loaded"), 16)
            ac.wait_ge(S("con_loaded"), 16)
            act(cact[:, :], par[:, PAR["c"]:PAR["c"] + 8], ACT.Silu).then_inc(S("c_act"), 1)
            act_norm(ac, "mix_pre0", x, lambda q: ac.wait_ge(S("x_loaded"), 16))
            act_ssd(ac, link)
            act_norm(ac, "mix_post0", acc8, from_acc(("ssd_out", 8)))
            act_norm(ac, "ffn_pre0", x, x_ready(ac, "mix_post0"))
            act_ffn(ac, 0)
            act_norm(ac, "ffn_post0", acc8, from_acc(("ffn0", 16)))
            act_norm(ac, "mix_pre1", x, x_ready(ac, "ffn_post0"))
            act_lru(ac, link)
            act_norm(ac, "mix_post1", R["m"], lambda q: ac.wait_ge(S("lru_m"), q + 1))
            act_norm(ac, "ffn_pre1", x, x_ready(ac, "mix_post1"))
            act_ffn(ac, 1)
            act_norm(ac, "ffn_post1", acc8, from_acc(("ffn1", 16)))
            for l in range(2):
                act_b2_in(ac, l, link)
                act_delta(ac, l, link)
                act_attn(ac, l, link)
                act_merge(ac, l)
                act_norm(ac, f"pre2_{l}", x, x_ready(ac, f"res1_{l}"))
                act_mlp(ac, l)

        @block.vector
        def _(dve):
            link = Chain(dve, S("dve_link"))
            dve.sem_inc(S("unit_free"), 2)
            dve.sem_inc(S("x_ready"), 4)
            dve.wait_ge(S("par_loaded"), 16)
            dve.wait_ge(S("con_loaded"), 16)
            dve.wait_ge(S("x_loaded"), 16)
            block1 = lambda name, l: (lambda t: pr(name, 8 * l + t))
            dve_pre(dve, "mix_pre0", block1("mix_pre", 0), 0)
            dve_ssd(dve, link)
            dve_post(dve, link, "mix_post0", block1("mix_post", 0), acc8)
            dve_pre(dve, "ffn_pre0", block1("ffn_pre", 0), 0)
            dve_ffn(dve, 0, link)
            dve_post(dve, link, "ffn_post0", block1("ffn_post", 0), acc8)
            dve_pre(dve, "mix_pre1", block1("mix_pre", 1), 0)
            dve_lru(dve, link)
            dve_post(dve, link, "mix_post1", block1("mix_post", 1), R["m"])
            dve_pre(dve, "ffn_pre1", block1("ffn_pre", 1), 0)
            dve_ffn(dve, 1, link)
            dve_post(dve, link, "ffn_post1", block1("ffn_post", 1), acc8)
            gate = lambda k: (lambda t: mod[:, k + t:k + t + 1])
            for l in range(2):
                dve_b2_in(dve, l, link)
                dve_delta(dve, l, link)
                dve_attn(dve, l, link)
                dve_merge(dve, l, link)
                dve_residual(dve, f"res1_{l}", gate(16), B0[f"out2_{l}"] + 4)
                dve_modulated(dve, link, f"pre2_{l}", 1)
                dve_mlp(dve, l)
                dve_residual(dve, f"res2_{l}", gate(40), B0[f"mlp_{l}"] + 16)


def arrays_of(a):
    ada = np.ascontiguousarray(
        a["ada_w_2"].reshape(2, 8, P, ADA_N, AW).transpose(0, 3, 2, 1, 4)).reshape(2 * ADA_N, P, 8, AW)
    return {
        "x_in": np.ascontiguousarray(a["x"][0].T.reshape(DT_, P, T).transpose(1, 0, 2)),
        "w_in": stream(a),
        "ada_in": ada,
        "par_in": parameters(a),
        "con_in": constants(),
    }


def kernel(**inputs):
    import concourse.bacc as bacc
    from concourse.bass_utils import run_bass_kernel_spmd

    arrays = arrays_of({k: np.asarray(v) for k, v in inputs.items()})
    nc = bacc.Bacc("TRN2", target_bir_lowering=False, num_devices=1)
    aps = [nc.dram_tensor(n, v.shape, mybir.dt.from_np(v.dtype), kind="ExternalInput").ap() for n, v in arrays.items()]
    out = nc.dram_tensor("out", (P, DT_, T), mybir.dt.float32, kind="ExternalOutput").ap()
    build(nc, *aps, out)
    r = run_bass_kernel_spmd(nc, [arrays], core_ids=[0])
    y = r.results[0]["out"]
    return np.ascontiguousarray(y.transpose(1, 0, 2).reshape(D, T).T)[None]
```

```python
import math

import numpy as np

import concourse.bass as bass
from concourse import mybir
from concourse.alu_op_type import AluOpType as ALU

P = 128
T = 256
D = 1024
DT_ = D // P
NCHK = T // P
RAW = 3
CW = 2048
H_SSD, G_SSD = 32, 4
XT = 16
BCT = 8
LT = 10
FT = 32
NH = 4
AW = 128
ADA_N = 6 * D // AW
EPS = 1e-6
NEG = -1e30

STAGES = [("ssd_in", 20, 0), ("ssd_out", 0, 8), ("ffn0", 32, 16), ("lru_in", 10, 0), 
          ("lru_out", 0, 5), ("ffn1", 32, 16)]
for _l in range(2):
    STAGES += [(f"in2_{_l}", 22, 0), (f"bra_{_l}", 0, 2), (f"brb_{_l}", 0, 2), (f"out2_{_l}", 0, 4),
               (f"mlp_{_l}", 16, 16)]
CH0, U0, B0 = {}, {}, {}
_c = _u = _b = 0
for _n, _a, _bb in STAGES:
    CH0[_n], U0[_n], B0[_n] = _c, _u, _b
    _c += _a + _bb
    _u += _a
    _b += _bb
NCHUNK = _c
EPOCHS = [0, CH0["ssd_out"], CH0["lru_out"], CH0["in2_0"] + 14, CH0["in2_1"] + 14, NCHUNK]


def _columns(sizes):
    at, out = 0, {}
    for name, n in sizes:
        out[name] = at
        at += n
    return out, at


PAR, NPAR = _columns([
    ("mix_pre", 16), ("mix_post", 16), ("ffn_pre", 16), ("ffn_post", 16),
    ("ssd_conv", 24 * 5), ("dt_w", 8 * 32), ("dt_bias", 1), ("a_log", 1), ("ssd_d", 16), ("ssd_norm", 16),
    ("lru_b_in", 20), ("lru_conv", LT * 5), ("b_gx", LT), ("b_ga", LT), ("lam", LT), ("b_out", 8),
    ("ffn_conv", 2 * FT * 8), ("c", 8), ("ada_b", 96), ("n1", 16), ("n2", 16), ("dn_conv", 2 * 12 * 5),
    ("ba_w", 2 * 8 * 72), ("A_log", 2), ("dn_dt", 2), ("dn_gain", 2), ("qk_gain", 4), ("dlam", 8), ("subln", 2)])
CON, NCON = _columns([
    ("ident", P), ("ones", P), ("half_ones", P), ("neg_up", P), ("neg_lo", P), ("rope", P), ("level", 14 * P),
    ("cos", T), ("sin", T), ("eps", 1), ("one", 1), ("tiny", 1), ("zero", 1)])


def constants():
    c = np.zeros((P, NCON), np.float32)
    i = np.arange(P)
    def put(name, m, k=0):
        c[:, CON[name] + k:CON[name] + k + m.shape[1]] = m
    put("ident", np.eye(P))
    put("ones", np.ones((P, P)))
    put("half_ones", (i[:, None] // 64 == i[None, :] // 64))
    put("neg_up", np.where(i[:, None] <= i[None, :], 0, NEG))
    put("neg_lo", np.where(i[:, None] >= i[None, :], 0, NEG))
    rope = np.zeros((P, P))
    for b in (0, 64):
        for j in range(32):
            rope[b + j + 32, b + j] = -1.0
            rope[b + j, b + j + 32] = 1.0
    put("rope", rope)
    for n in range(7):
        m = 1 << n
        low = ((i[:, None] // m) % 2 == 1) & ((i[None, :] // m) == (i[:, None] // m) - 1)
        put("level", low, 2 * n * P)
        put("level", low.T, (2 * n + 1) * P)
    inv = 1.0 / (10000.0 ** (np.arange(0, 64, 2, dtype=np.float32) / 64))
    ang = np.arange(T, dtype=np.float32)[:, None] * inv.astype(np.float32)[None, :]
    ang = np.concatenate([ang, ang, ang, ang], axis=-1).T
    put("cos", np.cos(ang))
    put("sin", np.sin(ang))
    put("eps", np.full((P, 1), EPS))
    put("one", np.ones((P, 1)))
    put("tiny", np.full((P, 1), 1e-30))
    return c


def tiled(v):
    return np.reshape(v, (-1, P)).T


def parameters(a):
    p = np.zeros((P, NPAR), np.float32)
    def put(name, m, k=0):
        p[0:m.shape[0], PAR[name] + k:PAR[name] + k + m.shape[1]] = m
    for l in range(2):
        for name, src in (("mix_pre", "norm_mix_pre"), ("mix_post", "norm_mix_post"), ("ffn_pre", "norm_ffn_pre"),
                          ("ffn_post", "norm_ffn_post"), ("n1", "norm1_g_2"), ("n2", "norm2_g_2")):
            put(name, tiled(a[src][l]), 8 * l)
        w, b = a["ffn_conv_w"][l], a["ffn_conv_b"][l]
        for half in range(2):
            for j in range(3):
                m = tiled(w[j])[:, FT * half:FT * (half + 1)]
                p[:, PAR["ffn_conv"] + l * FT * 8 + 4 * half + j:PAR["ffn_conv"] + (l + 1) * FT * 8:8] = m
            p[:, PAR["ffn_conv"] + l * FT * 8 + 4 * half + 3:PAR["ffn_conv"] + (l + 1) * FT * 8:8] = \
                tiled(b)[:, FT * half:FT * (half + 1)]
        put("ada_b", tiled(a["ada_b_2"][l]), 48 * l)
        for j in range(5):
            p[:, PAR["dn_conv"] + 60 * l + j:PAR["dn_conv"] + 60 * (l + 1):5] = tiled(a["dn_conv_2"][l, j])
        ba = a["w_in_2"][l][:, 3584:3600]
        for k in range(8):
            rows = ba[k * P:(k + 1) * P]
            for d in range(2):
                at = (l * 8 + k) * 72 + 32 * d
                put("ba_w", rows[:, 4 * d:4 * d + 4], at)
                put("ba_w", rows[:, 8 + 4 * d:12 + 4 * d], at + 36)
        for d in range(2):
            r = slice(32 * d, 32 * d + 4)
            p[r, PAR["A_log"] + l] = a["dn_A_log_2"][l, d]
            p[r, PAR["dn_dt"] + l] = a["dn_dt_bias_2"][l, d]
        put("dn_gain", a["dn_out_gain_2"][l][:, None], l)
        for t in range(2):
            put("qk_gain", np.concatenate([a["qk_norm_gain_2"][l, t]] * 2)[:, None], 2 * l + t)
        put("dlam", a["diff_lambda_2"][l].T, 4 * l)
        put("subln", a["diff_subln_gain_2"][l][:, None], l)
    for j in range(4):
        p[:, PAR["ssd_conv"] + j:PAR["ssd_conv"] + 120:5] = tiled(a["ssd_conv_w"][0, j])
        p[:, PAR["lru_conv"] + j:PAR["lru_conv"] + 50:5] = tiled(a["lru_conv_w"][0, j])
    p[:, PAR["ssd_conv"] + 4:PAR["ssd_conv"] + 120:5] = tiled(a["ssd_conv_b"][0])
    p[:, PAR["lru_conv"] + 4:PAR["lru_conv"] + 50:5] = tiled(a["lru_conv_b"][0])
    put("dt_w", a["ssd_w_in"][0][:, 5120:].reshape(8, P, 32).transpose(1, 0, 2).reshape(P, 256))
    put("dt_bias", a["ssd_dt_bias"][0][:, None])
    put("a_log", a["ssd_a_log"][0][:, None])
    put("ssd_d", tiled(np.repeat(a["ssd_d"][0], 64)))
    put("ssd_norm", tiled(a["ssd_norm"][0]))
    put("lru_b_in", tiled(a["lru_b_in"][0]))
    put("b_gx", tiled(a["lru_b_gx"][0]))
    put("b_ga", tiled(a["lru_b_ga"][0]))
    put("lam", tiled(a["lru_lambda"][0]))
    put("b_out", tiled(a["lru_b_out"][0]))
    put("c", tiled(a["c_2"][0]))
    return p


def stream(a):
    w = np.zeros((NCHUNK, P, CW), np.float32)

    def kind_a(at, m):
        n = m.shape[1] // 256
        w[at:at + n] = m.reshape(8, P, n, 2, P).transpose(2, 1, 3, 0, 4).reshape(n, P, CW)

    def kind_b(at, m):
        n = m.shape[0] // 256
        w[at:at + n] = m.reshape(n, 2, P, D).transpose(0, 2, 1, 3).reshape(n, P, CW)

    s = a["ssd_w_in"][0]
    kind_a(CH0["ssd_in"], s[:, 2048:5120])
    kind_a(CH0["ssd_in"] + 12, s[:, 0:2048])
    kind_b(CH0["ssd_out"], a["ssd_w_out"][0])
    kind_a(CH0["lru_in"], np.concatenate([a["lru_w_in"][0][:, 1280:], a["lru_w_in"][0][:, :1280]], axis=1))
    kind_b(CH0["lru_out"], a["lru_w_out"][0])
    for l in range(2):
        up, down = a["ffn_w_up"][l], a["ffn_w_down"][l]
        ups = np.stack([up[:, :FT * P].reshape(D, FT, P), up[:, FT * P:].reshape(D, FT, P)], axis=2).reshape(D, -1)
        spread(w, CH0[f"ffn{l}"], ups, down, kind_a, kind_b)
        m = a["w_in_2"][l]
        at = CH0[f"in2_{l}"]
        kind_a(at, m[:, 1536:3072])
        kind_a(at + 6, m[:, 0:1536])
        kind_a(at + 12, m[:, 3072:3584])
        kind_a(at + 14, m[:, 3600:5648])
        kind_b(CH0[f"bra_{l}"], a["w_branch_a_2"][l])
        kind_b(CH0[f"brb_{l}"], a["w_branch_b_2"][l])
        kind_b(CH0[f"out2_{l}"], a["w_out_2"][l])
        mlp_chunks(w, CH0[f"mlp_{l}"], a["w_mlp1_2"][l], a["w_mlp2_2"][l], kind_a, kind_b)
    return w


def lru_gates(a):
    return np.concatenate([a[n][0].transpose(1, 0, 2).reshape(P, LT * P) for n in ("lru_w_gx", "lru_w_ga")], axis=1)


def spread(w, at, up, down, kind_a, kind_b):
    for p in range(16):
        a0 = at + (0 if p == 0 else 3 * p - 1)
        kind_a(a0, up[:, 512 * p:512 * (p + 1)])
        b0 = at + 3 * p + 4 if p < 15 else at + 47
        kind_b(b0, down[256 * p:256 * (p + 1)])


def mlp_chunks(w, at, up, down, kind_a, kind_b):
    for p in range(16):
        kind_a(at + (0 if p == 0 else 2 * p - 1), up[:, 256 * p:256 * (p + 1)])
        kind_b(at + (2 * p + 2 if p < 15 else 31), down[256 * p:256 * (p + 1)])


class Chain:

    def __init__(self, engine, sem):
        self.engine, self.sem, self.n, self.at = engine, sem, 0, None

    def __call__(self, ins):
        ins.then_inc(self.sem, 1)
        self.n += 1
        value = self.n if self.at is None else self.at[0] * self.at[1] + self.n
        self.engine.wait_ge(self.sem, value)

    def enter(self, i, per):
        self.at, self.start = (i, per), self.n

    def leave(self, turns):
        per = self.at[1]
        assert self.n - self.start == per, (self.n - self.start, per)
        self.n, self.at = self.start + per * turns, None


def build(nc, x_in, w_in, gates_in, ada_in, par_in, con_in, out):
    f32 = mybir.dt.float32
    f32r = mybir.dt.float32r
    ACT = mybir.ActivationFunctionType
    AX = mybir.AxisListType
    sems = {}
    from contextlib import ExitStack
    ctx = ExitStack()
    with ctx:
        def sb(name, shape, dtype=f32):
            return ctx.enter_context(nc.sbuf_tensor(name, shape, dtype))

        def S(name):
            if name not in sems:
                sems[name] = ctx.enter_context(nc.semaphore(name))
            return sems[name]

        raw = [sb(f"raw{i}", [P, CW]) for i in range(RAW)]
        x = sb("x", [P, DT_, T])
        h = sb("h", [P, DT_, T])
        h_hi = sb("h_hi", [P, DT_, T], f32r)
        h_lo = sb("h_lo", [P, DT_, T], f32r)
        mv_hi = sb("mv_hi", [P, 2, 2, T], f32r)
        mv_lo = sb("mv_lo", [P, 2, 2, T], f32r)
        par = sb("par", [P, NPAR])
        con = sb("con", [P, NCON])
        ada_ring = [sb(f"ada_ring{i}", [P, 8, AW]) for i in range(2)]
        ada_acc = sb("ada_acc", [P, 6 * D])
        rstd = sb("rstd", [P, T])
        lnv = sb("lnv", [P, T])
        tmp = sb("tmp", [P, 4, T])
        cact = sb("cact", [P, 8])
        mod = sb("mod", [P, 48])
        gsc = sb("gsc", [P, 16])
        keep_cols, late_cols = 10752, 10640
        keep = sb("keep", [P, keep_cols])
        with nc.sbuf_tensor("late", [P, late_cols], f32) as late:
            pass
        w_hi = [sb(f"w_hi{i}", [P, CW], f32r) for i in range(2)]
        w_lo = [sb(f"w_lo{i}", [P, CW], f32r) for i in range(2)]

        unit = [ctx.enter_context(nc.psum_tensor(f"unit{i}", [P, 512], f32)) for i in range(2)]
        misc = [ctx.enter_context(nc.psum_tensor(f"misc{i}", [P, 512], f32)) for i in range(2)]
        acc = ctx.enter_context(nc.psum_tensor("acc", [P, 4 * 512], f32))
        acc8 = acc[:, :].rearrange("p (t n) -> p t n", n=T)

        def carve(region, sizes):
            at, views = 0, {}
            for name, shape in sizes:
                n = int(np.prod(shape))
                v = region[:, at:at + n]
                if len(shape) == 2:
                    v = v.rearrange("p (a b) -> p a b", b=shape[1])
                elif len(shape) == 3:
                    v = v.rearrange("p (a b c) -> p a b c", b=shape[1], c=shape[2])
                views[name] = v
                at += n
            assert at <= (keep_cols if region is keep else late_cols), at
            return views

        def pr(name, k=0, rows=P):
            return par[0:rows, PAR[name] + k:PAR[name] + k + 1]

        def cn(name, k=0, n=P):
            return con[:, CON[name] + k:CON[name] + k + n]

        def one(name, rows=P):
            return con[0:rows, CON[name]:CON[name] + 1]

        ident, ones = cn("ident"), cn("ones")
        bank = lambda b, a, z: acc[:, 512 * b + a:512 * b + z]
        mm = nc.tensor.matmul
        act = nc.scalar.activation
        tt = nc.vector.tensor_tensor
        stt = nc.vector.scalar_tensor_tensor
        ts = nc.vector.tensor_scalar

        NORMS = ["mix_pre0", "mix_post0", "ffn_pre0", "ffn_post0", "mix_pre1", "mix_post1", "ffn_pre1",
                 "ffn_post1", "pre1_0", "pre2_0", "pre1_1", "pre2_1"]
        NI = {n: i for i, n in enumerate(NORMS)}
        XU = {"load": 0, "mix_post0": 1, "ffn_post0": 2, "mix_post1": 3, "ffn_post1": 4, "res1_0": 5,
              "res2_0": 6, "res1_1": 7, "res2_1": 8}
        HU = {"mix_pre0": 0, "ffn_pre0": 1, "mix_pre1": 2, "ffn_pre1": 3, "pre1_0": 4, "pre2_0": 5,
              "pre1_1": 6, "pre2_1": 7}

        def act_norm(ac, name, source, ready, between=None):
            n = NI[name]
            for q in range(4):
                ready(q)
                act(h[:, 2 * q:2 * q + 2, :], source[:, 2 * q:2 * q + 2, :], ACT.Square).then_inc(S("squares"), 1)
            ac.preload_act_table_set(LN_EXP)
            if between is not None:
                between()
            ac.wait_ge(S("square_sums"), n + 1)
            act(lnv[:, :], misc[0][:, 0:T], ACT.Ln, bias=one("eps"), scale=1.0 / D).then_inc(S("log_var"), 1)
            ac.wait_ge(S("log_var"), n + 1)
            act(rstd[:, :], lnv[:, :], ACT.Exp, scale=-0.5).then_inc(S("rstd_ready"), 1)

        def pe_norm(pe, name):
            n = NI[name]
            for q in range(4):
                pe.wait_ge(S("squares"), 4 * n + q + 1)
                for t in (2 * q, 2 * q + 1):
                    last = mm(misc[0][:, 0:T], ones, h[:, t, :], start=(t == 0), stop=(t == 7))
            last.then_inc(S("square_sums"), 1)

        def x_ready(eng, name):
            return lambda q: eng.wait_ge(S("x_ready"), 4 * XU[name] + q + 1)

        def dve_h(dve, name, tiles):
            u = 4 * HU[name]
            dve.wait_ge(S("rstd_ready"), NI[name] + 1)

            def low(q):
                s = slice(2 * q, 2 * q + 2)
                dve.wait_ge(S("h_hi_done"), u + q + 1)
                tt(h_lo[:, s, :], h[:, s, :], h_hi[:, s, :].bitcast(f32), ALU.subtract).then_inc(S("h_ready"), 1)

            for q in range(4):
                tiles(q).then_inc(S("h_exact"), 1)
                if q >= 1:
                    low(q - 1)
            low(3)

        def act_h(ac, name):
            u = 4 * HU[name]
            for q in range(4):
                s = slice(2 * q, 2 * q + 2)
                ac.wait_ge(S("h_exact"), u + q + 1)
                act(h_hi[:, s, :], h[:, s, :], ACT.Copy).then_inc(S("h_hi_done"), 1)

        def dve_pre(dve, name, weight):
            def tiles(q):
                for t in (2 * q, 2 * q + 1):
                    ins = stt(h[:, t, :], x[:, t, :], weight(t), rstd[:, :], ALU.mult, ALU.mult)
                return ins
            dve_h(dve, name, tiles)

        def dve_post(dve, link, name, weight, source):
            dve.wait_ge(S("rstd_ready"), NI[name] + 1)
            for q in range(4):
                s = tmp[:, 2 * (q % 2):2 * (q % 2) + 2, :]
                for k in range(2):
                    ins = stt(s[:, k, :], source[:, 2 * q + k, :], weight(2 * q + k), rstd[:, :], ALU.mult, ALU.mult)
                link(ins)
                tt(x[:, 2 * q:2 * q + 2, :], x[:, 2 * q:2 * q + 2, :], s, ALU.add).then_inc(S("x_ready"), 1)

        def dve_residual(dve, name, gate, stage):
            done_after(dve, END[stage] - 1)
            for t in range(8):
                ins = stt(x[:, t, :], acc8[:, t, :], gate(t), x[:, t, :], ALU.mult, ALU.add)
                if t % 2:
                    ins.then_inc(S("x_ready"), 1)

        LN_EXP = "natural_log_exp_and_others"

        loaded = [S(f"chunk_loaded{i}") for i in range(RAW)]
        END = {n: CH0[n] + na + nb for n, na, nb in STAGES}

        def at(i, per, n):
            return n if i is None else i * per + n

        def done_after(eng, c, i=None, chunks=0):
            eng.wait_ge(S("half_done"), at(i, 2 * chunks, 2 * c + 2))

        def half(tile, c, k):
            return tile[c % 2][:, CW // 2 * k:CW // 2 * (k + 1)]

        def act_split(ac, c, i=None, chunks=0):
            for k in range(2):
                if k == 0:
                    ac.wait_ge(loaded[c % RAW], at(i, 16 * chunks // RAW, 16 * (c // RAW + 1)))
                if i is not None or 2 * c + k - 3 > 0:
                    ac.wait_ge(S("half_done"), at(i, 2 * chunks, 2 * c + k - 3))
                act(half(w_hi, c, k), raw[c % RAW][:, CW // 2 * k:CW // 2 * (k + 1)], ACT.Copy
                    ).then_inc(S("high_parts"), 1)

        def dve_split(dve, c, i=None, chunks=0):
            for k in range(2):
                dve.wait_ge(S("high_parts"), at(i, 2 * chunks, 2 * c + k + 1))
                tt(half(w_lo, c, k), raw[c % RAW][:, CW // 2 * k:CW // 2 * (k + 1)],
                   half(w_hi, c, k).bitcast(f32), ALU.subtract).then_inc(S("chunk_split"), 1)

        def ahead(split, eng, c, i=None, chunks=0):
            if c + 2 < next(e for e in EPOCHS if e > c):
                split(eng, c + 2, i, chunks)

        def epoch(split, eng, c):
            assert c in EPOCHS
            split(eng, c)
            split(eng, c + 1)

        def three(out, w, wl, m, ml, first, last):
            mm(out, w, m, start=first, stop=False)
            mm(out, w, ml, start=False, stop=False)
            return mm(out, wl, m, start=False, stop=last)

        def pe_unit(pe, c, n, i=None, chunks=0, units=0, tokens_out=False, h_count=None):
            b = unit[n % 2]
            pe.wait_ge(S("unit_free"), at(i, units, n + 1))
            for k in range(2):
                pe.wait_ge(S("chunk_split"), at(i, 2 * chunks, 2 * c + k + 1))
                w, wl = (half(v, c, k).rearrange("p (k n) -> p k n", k=8) for v in (w_hi, w_lo))
                for m in range(2 if tokens_out else 1):
                    for j in range(8):
                        if h_count is not None and k == 0 and j % 2 == 0:
                            pe.wait_ge(S("h_ready"), h_count + j // 2 + 1)
                        if tokens_out:
                            s = slice(P * m, P * (m + 1))
                            o = b[:, T * m + P * k:T * m + P * (k + 1)]
                            ins = three(o, h_hi[:, j, s], h_lo[:, j, s], w[:, j, :], wl[:, j, :], j == 0, j == 7)
                        else:
                            ins = three(b[:, T * k:T * (k + 1)], w[:, j, :], wl[:, j, :], h_hi[:, j, :],
                                        h_lo[:, j, :], j == 0, j == 7)
                ins.then_inc(S("half_done"), 1)

        def pe_units(pe, c0, n0, count):
            with pe.Fori(0, count // 2) as i:
                for j in range(2):
                    pe_unit(pe, c0 + j, n0 + j, i, 2, 2)

        def pe_down(pe, c, b, first, last, i=None, chunks=0, downs=0):
            pe.wait_ge(S("mv_ready"), at(i, downs, b + 1))
            for k in range(2):
                pe.wait_ge(S("chunk_split"), at(i, 2 * chunks, 2 * c + k + 1))
                w, wl = (half(v, c, k).rearrange("p (t n) -> p t n", t=8) for v in (w_hi, w_lo))
                for t in range(8):
                    ins = three(acc8[:, t, :], w[:, t, :], wl[:, t, :], mv_hi[:, b % 2, k, :], mv_lo[:, b % 2, k, :],
                                first and k == 0 and t % 2 == 0, last and k == 1 and t % 2 == 1)
                ins.then_inc(S("half_done"), 1)

        def act_moving(ac, b, src, i=None, downs=0):
            act(mv_hi[:, b % 2, :, :], src, ACT.Copy).then_inc(S("mv_hi_done"), 1)

        def dve_moving(dve, b, src, i=None, downs=0):
            dve.wait_ge(S("mv_hi_done"), at(i, downs, b + 1))
            tt(mv_lo[:, b % 2, :, :], src, mv_hi[:, b % 2, :, :].bitcast(f32), ALU.subtract
               ).then_inc(S("mv_ready"), 1)

        def pe_out(pe, stage):
            n = END[stage] - CH0[stage]
            for j in range(n):
                pe_down(pe, CH0[stage] + j, B0[stage] + j, j == 0, j == n - 1)

        def act_out(ac, stage, pair, ready, all_ahead=True):
            n = END[stage] - CH0[stage]
            for j in range(-2, n):
                c = CH0[stage] + j
                if j >= 0 and (j < n - 1 or all_ahead):
                    ahead(act_split, ac, c)
                    done_after(ac, c)
                if j + 2 < n:
                    ready(j + 2)
                    act_moving(ac, B0[stage] + j + 2, pair(j + 2))

        def dve_out(dve, stage, pair):
            n = END[stage] - CH0[stage]
            for j in range(-2, n):
                if 0 <= j < n - 1:
                    ahead(dve_split, dve, CH0[stage] + j)
                if j + 2 < n:
                    dve_moving(dve, B0[stage] + j + 2, pair(j + 2))

        A = carve(keep, [("zs", (16, T)), ("xbc", (24, T)), ("rows", (2, T))])
        A.update(carve(late, [("xdt", (32, 64)), ("xdtd", (32, 64)), ("btok", (4, P)), ("cb", (4, P)),
                              ("e", (8, P)), ("e2", (8, P)), ("st", (32, 64)), ("tok", (5, 32))]))
        A["conv"] = tmp[:, :, :]
        A["rg"] = tmp[:, :, :]
        over = A["xdtd"].rearrange("p a b -> p (a b)")
        A["ecs"] = over[:, 0:512].rearrange("p (a b) -> p a b", b=P)
        A["yo"] = over[:, 512:1024].rearrange("p (a b) -> p a b", b=P)
        xbc, zs = A["xbc"], A["zs"]
        HR = 32
        r_cs, r_a = (A["rows"][0:HR, k, :] for k in range(2))
        r_dt, r_da, r_b, r_ncs, r_dtd, r_one = (zs[0:HR, k, :] for k in range(6))
        tokv = A["tok"]
        E2 = [A["e"], A["e2"]]

        def pe_ssd(pe):
            def decays(n):
                c, g = n // 4, n % 4
                for half in range(2):
                    m = 2 * n + half
                    if m >= 2:
                        pe.wait_ge(S("ssd_exp"), m - 1)
                    b = unit[m % 2]
                    if m < 2:
                        pe.wait_ge(S("unit_free"), 22)
                    for k in range(4):
                        hd = 8 * g + 4 * half + k
                        mm(b[:, P * k:P * (k + 1)], ident[0:HR, hd:hd + 1].to_broadcast([HR, P]),
                           r_cs[:, P * c:P * (c + 1)], start=(k == 0), stop=False, skip_group_check=True)
                    for k in range(4):
                        ins = mm(b[:, P * k:P * (k + 1)], ident, cn("neg_up"), start=False, stop=(k == 3),
                                 skip_group_check=True)
                    ins.then_inc(S("ssd_decay_ps"), 1)

            pe.wait_ge(S("h_ready"), 4)
            for k in range(8):
                ins = mm(misc[1][0:HR, 0:T], par[:, PAR["dt_w"] + 32 * k:PAR["dt_w"] + 32 * (k + 1)], h[:, k, :],
                         start=(k == 0), stop=(k == 7))
            ins.then_inc(S("dt_raw"), 1)
            pe_units(pe, CH0["ssd_in"], U0["ssd_in"], 12)
            pe.wait_ge(S("ssd_rows"), 1)
            for n, (src, c) in enumerate(((r_dt, 0), (r_dt, 1), (r_ncs, 0), (r_ncs, 1), (r_dtd, 0))):
                ins = nc.tensor.transpose(misc[1][:, 32 * n:32 * (n + 1)], src[:, P * c:P * (c + 1)], ident[0:HR, 0:HR])
            ins.then_inc(S("ssd_tok_ps"), 1)
            pe_units(pe, CH0["ssd_in"] + 12, U0["ssd_in"] + 12, 8)
            pe.wait_ge(S("ssd_conv_done"), 24)
            for g in range(4):
                ins = nc.tensor.transpose(bank(0, P * g, P * (g + 1)), xbc[:, 16 + g, 0:P], ident)
            ins.then_inc(S("ssd_btok_ps"), 1)
            for c in range(2):
                for q in range(4):
                    m = 4 * c + q
                    if m >= 2:
                        pe.wait_ge(S("ssd_x_read"), m - 1)
                    if m == 0:
                        pe.wait_ge(S("ssd_btok"), 1)
                    for k in range(4):
                        ins = nc.tensor.transpose(bank(m % 2, P * k, P * (k + 1)), xbc[:, 4 * q + k, P * c:P * (c + 1)],
                                                  ident)
                    ins.then_inc(S("ssd_x_ps"), 1)
                if c == 1:
                    pe.wait_ge(S("ssd_cb"), 1)
                for g in range(4):
                    ins = mm(bank(2, P * g, P * (g + 1)), xbc[:, 16 + g, P * c:P * (c + 1)],
                             xbc[:, 20 + g, P * c:P * (c + 1)], start=True, stop=True)
                ins.then_inc(S("ssd_cb_ps"), 1)
                if c == 0:
                    for g in range(4):
                        pe.wait_ge(S("ssd_xdtd"), g + 1)
                        if g >= 1:
                            pe.wait_ge(S("ssd_state"), g)
                        mm(bank(3, 0, 512), A["btok"][:, g, :],
                           A["xdtd"].rearrange("p a b -> p (a b)")[:, 512 * g:512 * (g + 1)],
                           start=True, stop=True).then_inc(S("ssd_state_ps"), 1)
                    pe.wait_ge(S("ssd_state"), 4)
                if c == 0:
                    decays(0)
                if c == 1:
                    pe.wait_ge(S("ssd_x_read"), 8)
                for g in range(4):
                    n = 4 * c + g
                    if n + 1 < 8:
                        decays(n + 1)
                    pe.wait_ge(S("ssd_scores"), n + 1)
                    if n >= 1:
                        pe.wait_ge(S("ssd_y"), n)
                    if n == 0:
                        pe.wait_ge(S("ssd_tok"), 1)
                    for hd in range(8):
                        lo = 64 * (hd % 2)
                        ins = mm(misc[0][lo:lo + 64, P * (hd // 2):P * (hd // 2) + P], A["xdt"][:, 8 * g + hd, :],
                                 E2[n % 2][:, hd, :], start=True, stop=True, skip_group_check=True)
                    if c == 1:
                        for k in range(4):
                            st = A["st"].rearrange("p a b -> p (a b)")[:, 512 * g + P * k:512 * g + P * (k + 1)]
                            mm(misc[1][:, P * k:P * (k + 1)], st, xbc[:, 20 + g, P:T], start=True, stop=True)
                        for k in range(4):
                            for e in range(2):
                                hd = 8 * g + 2 * k + e
                                ins = mm(bank(3, P * k, P * (k + 1))[64 * e:64 * (e + 1), :],
                                         ident[0:HR, hd:hd + 1].to_broadcast([HR, 64]), r_a[:, P:T],
                                         start=True, stop=True, skip_group_check=True)
                    ins.then_inc(S("ssd_y_ps"), 1)
            pe.wait_ge(S("ssd_y"), 8)
            for g in range(4):
                pe.wait_ge(S("ssd_sq"), g + 1)
                if g >= 2:
                    pe.wait_ge(S("ssd_glog"), g - 1)
                for k in range(4):
                    ins = mm(misc[g % 2][:, 0:T], ones, h[:, 4 * (g % 2) + k, :], start=(k == 0), stop=(k == 3))
                ins.then_inc(S("ssd_gsum"), 1)
            pe_out(pe, "ssd_out")

        def ssd_pair(j):
            return xbc[:, 2 * j:2 * j + 2, :]

        def act_ssd(ac, link):
            ac.preload_act_table_set(LN_EXP)
            ac.wait_ge(S("dt_in"), 1)
            link(act(r_a, r_dt, ACT.Abs))
            link(act(r_b, r_a, ACT.Exp, scale=-1.0))
            link(act(r_b, r_b, ACT.Ln, bias=one("one", HR)))
            act(r_one[:, 0:1], pr("a_log", 0, HR), ACT.Exp).then_inc(S("dt_log"), 1)
            ac.wait_ge(S("dt_cs"), 1)
            link(act(r_dtd, r_cs, ACT.Exp, bias=r_cs[:, P - 1:P], scale=-1.0))
            act(r_ncs, r_cs, ACT.Copy, scale=-1.0)
            act(r_a, r_cs, ACT.Exp).then_inc(S("dt_decays"), 1)
            conv = A["conv"]

            def last_tap(j):
                if j % 2 == 0:
                    ahead(act_split, ac, j // 2)
                    done_after(ac, j // 2)
                if j >= 4:
                    ac.wait_ge(S("ssd_conv_done"), j - 3)
                act(conv[:, j % 4, :], unit[(j // 2) % 2][:, T * (j % 2):T * (j % 2 + 1)], ACT.Identity,
                    bias=pr("ssd_conv", 5 * j + 4), scale=pr("ssd_conv", 5 * j + 3)).then_inc(S("ssd_tap"), 1)

            def silu(j):
                ac.wait_ge(S("ssd_taps"), j + 1)
                act(xbc[:, j, :], conv[:, j % 4, :], ACT.Silu).then_inc(S("ssd_conv_done"), 1)

            for j in range(26):
                if j < 24:
                    last_tap(j)
                if j >= 2:
                    silu(j - 2)
            ac.wait_ge(S("unit_free"), 12 + 2)
            ac.wait_ge(S("ssd_tok_ps"), 1)
            for n in range(8):
                ahead(act_split, ac, 12 + n)
                done_after(ac, 12 + n)
                act(zs[:, 2 * n:2 * n + 2, :], unit[n % 2][:, :], ACT.Silu).then_inc(S("unit_free"), 1)
            ac.wait_ge(S("ssd_btok_ps"), 1)
            act(A["btok"], bank(0, 0, 512), ACT.Copy).then_inc(S("ssd_btok"), 1)
            for g in range(4):
                ac.wait_ge(S("ssd_state_ps"), g + 1)
                act(A["st"].rearrange("p a b -> p (a b)")[:, 512 * g:512 * (g + 1)], bank(3, 0, 512),
                    ACT.Copy).then_inc(S("ssd_state"), 1)
            ac.wait_ge(S("ssd_tok"), 1)

            def exps(n):
                c, g = n // 4, n % 4
                for half in range(2):
                    ac.wait_ge(S("ssd_decay_ps"), 2 * n + half + 1)
                    if half == 0 and n >= 2:
                        ac.wait_ge(S("ssd_y_ps"), n - 1)
                    for k in range(4):
                        hd = 4 * half + k
                        ins = act(E2[n % 2][:, hd, :], unit[half][:, P * k:P * (k + 1)], ACT.Exp,
                                  bias=tokv[:, 2 + c, 8 * g + hd:8 * g + hd + 1])
                    ins.then_inc(S("ssd_exp"), 1)

            exps(0)
            for n in range(8):
                if n + 1 < 8:
                    exps(n + 1)
                if n >= 4:
                    ac.wait_ge(S("ssd_y_ps"), n + 1)
                    if n >= 5:
                        ac.wait_ge(S("ssd_y"), n)
                    act(A["ecs"], bank(3, 0, 512), ACT.Copy).then_inc(S("ssd_ecs"), 1)
            for g in range(4):
                ac.wait_ge(S("ssd_gated"), g + 1)
                if g >= 2:
                    ac.wait_ge(S("ssd_gsum"), g - 1)
                act(h[:, 4 * (g % 2):4 * (g % 2) + 4, :], xbc[:, 4 * g:4 * g + 4, :], ACT.Square
                    ).then_inc(S("ssd_sq"), 1)
            ac.preload_act_table_set(LN_EXP)
            ac.wait_ge(S("ssd_y"), 8)
            epoch(act_split, ac, CH0["ssd_out"])
            for g in range(4):
                ac.wait_ge(S("ssd_gsum"), g + 1)
                act(A["rg"][:, g, :], misc[g % 2][:, 0:T], ACT.Ln, bias=one("eps"),
                    scale=1.0 / 512).then_inc(S("ssd_glog"), 1)
            ac.wait_ge(S("ssd_glog"), 4)
            act(A["rg"], A["rg"], ACT.Exp, scale=-0.5).then_inc(S("ssd_rg"), 1)
            act_out(ac, "ssd_out", ssd_pair, lambda j: ac.wait_ge(S("ssd_yn"), j + 1), all_ahead=False)

        def dve_ssd(dve, link):
            dve.wait_ge(S("dt_raw"), 1)
            ts(r_dt, misc[1][0:HR, 0:T], pr("dt_bias", 0, HR), None, ALU.add).then_inc(S("dt_in"), 1)
            dve.wait_ge(S("dt_log"), 1)
            link(stt(r_dt, r_dt, 0.0, r_b, ALU.max, ALU.add))
            link(ts(r_da, r_dt, r_one[:, 0:1], -1.0, ALU.mult, ALU.mult))
            link(nc.vector.memset(r_one, 1.0))
            for c in range(2):
                s = slice(P * c, P * (c + 1))
                ins = nc.vector.tensor_tensor_scan(r_cs[:, s], r_one[:, s], r_da[:, s], 0.0, ALU.mult, ALU.add)
            ins.then_inc(S("dt_cs"), 1)
            dve.wait_ge(S("dt_decays"), 1)
            tt(r_dtd, r_dtd, r_dt, ALU.mult).then_inc(S("ssd_rows"), 1)
            conv = A["conv"]

            for j in range(24):
                if j % 2 == 0:
                    ahead(dve_split, dve, j // 2)
                    dve.wait_ge(S("ssd_tap"), j + 2)
                src = unit[(j // 2) % 2][:, T * (j % 2):T * (j % 2 + 1)]
                dst = conv[:, j % 4, :]
                w = lambda k: pr("ssd_conv", 5 * j + k)
                link(stt(dst[:, 1:T], src[:, 0:T - 1], w(2), dst[:, 1:T], ALU.mult, ALU.add))
                link(stt(dst[:, 2:T], src[:, 0:T - 2], w(1), dst[:, 2:T], ALU.mult, ALU.add))
                stt(dst[:, 3:T], src[:, 0:T - 3], w(0), dst[:, 3:T], ALU.mult, ALU.add).then_inc(S("ssd_taps"), 1)
                if j % 2:
                    dve.wait_ge(S("ssd_taps"), j + 1)
                    dve.sem_inc(S("unit_free"), 1)
            for n in range(8):
                ahead(dve_split, dve, 12 + n)
            done_after(dve, 19)
            dve.wait_ge(S("ssd_tok_ps"), 1)
            nc.vector.tensor_copy(tokv, misc[1][:, 0:160]).then_inc(S("ssd_tok"), 1)
            dve.wait_ge(S("ssd_tok"), 1)
            for c in range(2):
                for q in range(4):
                    m = 4 * c + q
                    dve.wait_ge(S("ssd_x_ps"), m + 1)
                    if c == 1 and q == 0:
                        dve.wait_ge(S("ssd_y_ps"), 4)
                    src = bank(m % 2, 0, 512).rearrange("p (a b) -> p a b", b=64)
                    hs = slice(8 * q, 8 * q + 8)
                    if c == 0:
                        tt(A["xdtd"][:, hs, :], src, tokv[:, 4, hs].unsqueeze(2).to_broadcast([P, 8, 64]),
                           ALU.mult).then_inc(S("ssd_xdtd"), 1)
                    tt(A["xdt"][:, hs, :], src, tokv[:, c, hs].unsqueeze(2).to_broadcast([P, 8, 64]),
                       ALU.mult).then_inc(S("ssd_x_read"), 1)
                dve.wait_ge(S("ssd_cb_ps"), c + 1)
                link(nc.vector.tensor_copy(A["cb"], bank(2, 0, 512)))
                for g in range(4):
                    n = 4 * c + g
                    dve.wait_ge(S("ssd_exp"), 2 * n + 2)
                    e = E2[n % 2]
                    ins = tt(e, e, A["cb"][:, g, :].unsqueeze(1).to_broadcast([P, 8, P]), ALU.mult)
                    ins.then_inc(S("ssd_scores"), 1)
                    if c == 0 and g == 3:
                        dve.wait_ge(S("ssd_scores"), 4)
                        dve.sem_inc(S("ssd_cb"), 1)
                    dve.wait_ge(S("ssd_y_ps"), n + 1)
                    s = slice(P * c, P * (c + 1))
                    if c == 1:
                        dve.wait_ge(S("ssd_ecs"), g + 1)
                        link(tt(A["yo"], misc[1][:, :].rearrange("p (a b) -> p a b", b=P), A["ecs"], ALU.mult))
                    for k in range(4):
                        ins = stt(xbc[:, 4 * g + k, s], xbc[:, 4 * g + k, s], pr("ssd_d", 4 * g + k),
                                  misc[0][:, P * k:P * (k + 1)], ALU.mult, ALU.add)
                    link(ins)
                    if c == 1:
                        link(tt(xbc[:, 4 * g:4 * g + 4, s], xbc[:, 4 * g:4 * g + 4, s], A["yo"], ALU.add))
                    ins = tt(xbc[:, 4 * g:4 * g + 4, s], xbc[:, 4 * g:4 * g + 4, s], zs[:, 4 * g:4 * g + 4, s], ALU.mult)
                    if c == 0:
                        ins.then_inc(S("ssd_y"), 1)
                    else:
                        link(ins)
                        dve.sem_inc(S("ssd_y"), 1)
                        dve.sem_inc(S("ssd_gated"), 1)
            epoch(dve_split, dve, CH0["ssd_out"])
            dve.wait_ge(S("ssd_rg"), 1)
            for j in range(16):
                ins = stt(xbc[:, j, :], xbc[:, j, :], pr("ssd_norm", j), A["rg"][:, j // 4, :], ALU.mult, ALU.mult)
                if j % 2:
                    ins.then_inc(S("ssd_yn"), 1)
            dve_out(dve, "ssd_out", ssd_pair)

        F = carve(keep, [("fc", (2, 2 * T)), ("fg", (2, T)), ("hid", (2, T))])

        def pe_ffn(pe, l):
            c0, n0, b0 = CH0[f"ffn{l}"], U0[f"ffn{l}"], B0[f"ffn{l}"]
            pe_unit(pe, c0, n0, h_count=4 * HU[f"ffn_pre{l}"])
            pe_unit(pe, c0 + 1, n0 + 1)
            for j in range(2):
                pe_unit(pe, c0 + 2 + j, n0 + 2 + j)
            pe_down(pe, c0 + 4, b0, True, False)
            with pe.Fori(0, 7) as i:
                for k in range(2):
                    for j in range(2):
                        pe_unit(pe, c0 + 5 + 3 * k + j, n0 + 4 + 2 * k + j, i, 6, 4)
                    pe_down(pe, c0 + 7 + 3 * k, b0 + 1 + k, False, False, i, 6, 2)
            pe_down(pe, c0 + 47, b0 + 15, False, True)

        def act_ffn(ac, l):
            c0, b0, f0 = CH0[f"ffn{l}"], B0[f"ffn{l}"], 32 * l
            off = PAR["ffn_conv"] + l * FT * 8

            def column(u, k, i):
                return par[:, off + 8 * u + k:off + 8 * u + k + 1] if i is None else \
                    par[:, bass.ds(i * 32 + (off + 8 * u + k), 1)]

            def last_tap(u, c, i):
                done_after(ac, c, i, 6)
                if i is not None or u >= 2:
                    ac.wait_ge(S("ffn_product"), at(i, 4, f0 + u - 1))
                fc = F["fc"][:, u % 2, :]
                for side in range(2):
                    s = slice(T * side, T * (side + 1))
                    ins = act(fc[:, s], unit[u % 2][:, s], ACT.Identity, bias=column(u, 4 * side + 3, i),
                              scale=column(u, 4 * side + 2, i))
                ins.then_inc(S("ffn_tap"), 1)

            def gelu(u, i):
                ac.wait_ge(S("ffn_taps"), at(i, 4, f0 + u + 1))
                act(F["fg"][:, u % 2, :], F["fc"][:, u % 2, 0:T], ACT.Gelu_apprx_tanh).then_inc(S("ffn_gelu"), 1)

            def moving(p, i=None):
                ac.wait_ge(S("ffn_product"), at(i, 4, f0 + 2 * p + 2))
                act_moving(ac, b0 + p, F["hid"])

            def pair(p, i=None):
                c = c0 + max(3 * p - 1, 0)
                ahead(act_split, ac, c, i, 6)
                if p >= 1:
                    moving(p - 1, i)
                last_tap(2 * p, c, i)
                ahead(act_split, ac, c + 1, i, 6)
                gelu(2 * p, i)
                last_tap(2 * p + 1, c + 1, i)
                if p >= 1:
                    ahead(act_split, ac, c + 2, i, 6)
                gelu(2 * p + 1, i)

            pair(0)
            pair(1)
            with ac.Fori(0, 7) as i:
                for p in (2, 3):
                    pair(p, i)
            moving(15)

        def dve_ffn(dve, l, link):
            c0, b0, f0 = CH0[f"ffn{l}"], B0[f"ffn{l}"], 32 * l
            off = PAR["ffn_conv"] + l * FT * 8
            dve.wait_ge(S("unit_free"), U0[f"ffn{l}"] + 2)

            def column(u, k, i):
                return par[:, off + 8 * u + k:off + 8 * u + k + 1] if i is None else \
                    par[:, bass.ds(i * 32 + (off + 8 * u + k), 1)]

            def taps(u, i):
                dve.wait_ge(S("ffn_tap"), at(i, 4, f0 + u + 1))
                fc, src = F["fc"][:, u % 2, :], unit[u % 2]
                for side in range(2):
                    o = T * side
                    ins = stt(fc[:, o + 1:o + T], src[:, o:o + T - 1], column(u, 4 * side + 1, i),
                              fc[:, o + 1:o + T], ALU.mult, ALU.add)
                link(ins)
                for side in range(2):
                    o = T * side
                    ins = stt(fc[:, o + 2:o + T], src[:, o:o + T - 2], column(u, 4 * side, i),
                              fc[:, o + 2:o + T], ALU.mult, ALU.add)
                ins.then_inc(S("ffn_taps"), 1)
                dve.wait_ge(S("ffn_taps"), at(i, 4, f0 + u + 1))
                dve.sem_inc(S("unit_free"), 1)

            def product(u, i):
                if i is not None or u >= 2:
                    dve.wait_ge(S("mv_ready"), at(i, 2, b0 + u // 2))
                dve.wait_ge(S("ffn_gelu"), at(i, 4, f0 + u + 1))
                tt(F["hid"][:, u % 2, :], F["fg"][:, u % 2, :], F["fc"][:, u % 2, T:2 * T], ALU.mult
                   ).then_inc(S("ffn_product"), 1)

            def moving(p, i=None):
                dve.wait_ge(S("ffn_product"), at(i, 4, f0 + 2 * p + 2))
                dve_moving(dve, b0 + p, F["hid"], i, 2)

            def pair(p, i=None):
                c = c0 + max(3 * p - 1, 0)
                ahead(dve_split, dve, c, i, 6)
                if p >= 1:
                    moving(p - 1, i)
                taps(2 * p, i)
                ahead(dve_split, dve, c + 1, i, 6)
                taps(2 * p + 1, i)
                product(2 * p, i)
                if p >= 1:
                    ahead(dve_split, dve, c + 2, i, 6)
                product(2 * p + 1, i)

            pair(0)
            pair(1)
            with dve.Fori(0, 7) as i:
                link.enter(i, 4)
                for p in (2, 3):
                    pair(p, i)
                link.leave(7)
            moving(15)

        R = carve(keep, [("xb", (LT, T)), ("yb", (LT, T)), ("conv", (2, T)), ("pj", (4, T)), ("cv", (4, LT)),
                         ("gates", (2, LT, P))])
        R.update(carve(late, [("gx", (LT, T)), ("ga", (LT, T)), ("bt", (LT, T)), ("w", (LT, T))]))
        R["m"] = R["gates"].rearrange("p g h n -> p (g h n)")[:, 0:8 * T].rearrange("p (a b) -> p a b", b=T)
        cv = [R["cv"][:, k, :] for k in range(4)]

        def pe_lru(pe):
            c0, n0 = CH0["lru_in"], U0["lru_in"]
            pe_unit(pe, c0, n0, h_count=4 * HU["mix_pre1"])
            pe_unit(pe, c0 + 1, n0 + 1)
            pe_units(pe, c0 + 2, n0 + 2, 8)
            pe.wait_ge(S("gates_loaded"), 16)
            for j in range(LT):
                pe.wait_ge(S("lru_conv"), j + 1)
                if j >= 2:
                    pe.wait_ge(S("lru_gate_read"), j - 1)
                for g in range(2):
                    ins = mm(misc[j % 2][:, T * g:T * (g + 1)], R["gates"][:, g, j, :], R["xb"][:, j, :],
                             start=(g == 0), stop=(g == 1))
                ins.then_inc(S("lru_gate_ps"), 1)
            pe_out(pe, "lru_out")

        def lru_pair(j):
            return R["yb"][:, 2 * j:2 * j + 2, :]

        def act_lru(ac, link):
            ac.dma_start(R["gates"].rearrange("p g h n -> p (g h n)"), gates_in).then_inc(S("gates_loaded"), 16)
            ac.preload_act_table_set(LN_EXP)
            lam = par[:, PAR["lam"]:PAR["lam"] + LT]
            link(act(cv[0], lam, ACT.Abs))
            link(act(cv[1], cv[0], ACT.Exp, scale=-1.0))
            act(cv[1], cv[1], ACT.Ln, bias=one("one")).then_inc(S("lam_log"), 1)
            c0, n0 = CH0["lru_in"], U0["lru_in"]
            ac.wait_ge(S("unit_free"), n0 + 2)
            for n in range(5):
                done_after(ac, c0 + n)
                for k in range(2):
                    j = 2 * n + k
                    if j >= 4:
                        ac.wait_ge(S("lru_conv"), j - 3)
                    act(R["pj"][:, j % 4, :], unit[n % 2][:, T * k:T * (k + 1)], ACT.Identity,
                        bias=pr("lru_b_in", LT + j)).then_inc(S("lru_proj"), 1)
                ac.wait_ge(S("lru_proj"), 2 * n + 2)
                ac.sem_inc(S("unit_free"), 1)
                ahead(act_split, ac, c0 + n)
            for n in range(5, 10):
                ahead(act_split, ac, c0 + n)
                done_after(ac, c0 + n)
                for k in range(2):
                    j = 2 * (n - 5) + k
                    ins = act(R["yb"][:, j, :], unit[n % 2][:, T * k:T * (k + 1)], ACT.Gelu_apprx_tanh,
                              bias=pr("lru_b_in", j))
                ins.then_inc(S("unit_free"), 1)
            for j in range(LT):
                ac.wait_ge(S("lru_gate_ps"), j + 1)
                act(R["gx"][:, j, :], misc[j % 2][:, 0:T], ACT.Sigmoid, bias=pr("b_gx", j))
                act(R["ga"][:, j, :], misc[j % 2][:, T:2 * T], ACT.Sigmoid,
                    bias=pr("b_ga", j)).then_inc(S("lru_gate_read"), 1)
            ac.wait_ge(S("lru_gate_read"), LT)
            ac.wait_ge(S("lam_done"), 1)
            for j in range(LT):
                act(R["w"][:, j, :], R["ga"][:, j, :], ACT.Tanh, scale=cv[3][:, j:j + 1]).then_inc(S("lru_tanh"), 1)
                ac.wait_ge(S("lru_tanh"), j + 1)
                act(R["ga"][:, j, :], R["ga"][:, j, :], ACT.Exp, scale=cv[3][:, j:j + 1]).then_inc(S("lru_a"), 1)
            for j in range(LT):
                ac.wait_ge(S("lru_m2"), j + 1)
                act(R["w"][:, j, :], R["w"][:, j, :], ACT.Sqrt).then_inc(S("lru_mult"), 1)
            ac.wait_ge(S("lru_out_ready"), LT)
            epoch(act_split, ac, CH0["lru_out"])
            act_out(ac, "lru_out", lru_pair, lambda j: None)

        def dve_lru(dve, link):
            lam = par[:, PAR["lam"]:PAR["lam"] + LT]
            dve.wait_ge(S("lam_log"), 1)
            link(ts(cv[2], lam, -1.0, 0.0, ALU.mult, ALU.max))
            link(tt(cv[3], cv[2], cv[1], ALU.add))
            ts(cv[3], cv[3], -8.0, None, ALU.mult).then_inc(S("lam_done"), 1)
            for j in range(LT):
                dve.wait_ge(S("lru_proj"), j + 1)
                src, dst = R["pj"][:, j % 4, :], R["xb"][:, j, :]
                w = lambda k: pr("lru_conv", 5 * j + k)
                link(ts(dst, src, w(3), w(4), ALU.mult, ALU.add))
                link(stt(dst[:, 1:T], src[:, 0:T - 1], w(2), dst[:, 1:T], ALU.mult, ALU.add))
                link(stt(dst[:, 2:T], src[:, 0:T - 2], w(1), dst[:, 2:T], ALU.mult, ALU.add))
                stt(dst[:, 3:T], src[:, 0:T - 3], w(0), dst[:, 3:T], ALU.mult, ALU.add).then_inc(S("lru_conv"), 1)
                if j % 2:
                    ahead(dve_split, dve, CH0["lru_in"] + j // 2)
            for n in range(5, 10):
                ahead(dve_split, dve, CH0["lru_in"] + n)
            for j in range(LT):
                dve.wait_ge(S("lru_tanh"), j + 1)
                w, q = R["w"][:, j, :], R["conv"][:, j % 2, :]
                link(ts(q, w, -1.0, 1.0, ALU.mult, ALU.add))
                link(nc.vector.reciprocal(q, q))
                link(ts(w, w, -2.0, 1e-30, ALU.mult, ALU.max))
                tt(w, w, q, ALU.mult).then_inc(S("lru_m2"), 1)
                tt(R["gx"][:, j, :], R["gx"][:, j, :], R["xb"][:, j, :], ALU.mult).then_inc(S("lru_gated"), 1)
            dve.wait_ge(S("lru_gated"), LT)
            for j in range(LT):
                dve.wait_ge(S("lru_mult"), j + 1)
                dve.wait_ge(S("lru_a"), j + 1)
                link(tt(R["bt"][:, j, :], R["w"][:, j, :], R["gx"][:, j, :], ALU.mult))
                link(nc.vector.tensor_tensor_scan(R["gx"][:, j, :], R["ga"][:, j, :], R["bt"][:, j, :], 0.0,
                                                  ALU.mult, ALU.add))
                tt(R["yb"][:, j, :], R["gx"][:, j, :], R["yb"][:, j, :], ALU.mult).then_inc(S("lru_out_ready"), 1)
            dve.wait_ge(S("lru_out_ready"), LT)
            epoch(dve_split, dve, CH0["lru_out"])
            dve_out(dve, "lru_out", lru_pair)
            done_after(dve, END["lru_out"] - 1)
            for t in range(8):
                ins = ts(R["m"][:, t, :], acc8[:, t, :], pr("b_out", t), None, ALU.add)
                if t % 2:
                    ins.then_inc(S("lru_m"), 1)
            ahead(dve_split, dve, END["lru_out"] - 1)

        def ada_chunk(pool, s, l, i=None):
            a = ada_ring[s]
            base = 4 * ADA_N * l + 4 * s
            i = ADA_N // 2 - 1 if i is None else i
            pool.wait_ge(S(f"ada_loaded{s}"), i * 16 + (16 * (ADA_N // 2) * l + 16))
            nc.gpsimd.tensor_tensor(a[:, :, :], a[:, :, :], cact[:, :].unsqueeze(2).to_broadcast([P, 8, AW]),
                                    ALU.mult).then_inc(S("ada_step"), 1)
            for k, n in enumerate((4, 2)):
                pool.wait_ge(S("ada_step"), i * 8 + (base + k + 1))
                nc.gpsimd.tensor_tensor(a[:, 0:n, :], a[:, 0:n, :], a[:, n:2 * n, :],
                                        ALU.add).then_inc(S("ada_step"), 1)
            pool.wait_ge(S("ada_step"), i * 8 + (base + 3))
            nc.gpsimd.tensor_tensor(ada_acc[:, bass.ds(i * (2 * AW) + AW * s, AW)], a[:, 0, :], a[:, 1, :],
                                    ALU.add).then_inc(S("ada_step"), 1)
            pool.wait_ge(S("ada_step"), i * 8 + (base + 4))

        def ada_load(pool, s, chunk):
            src = ada_in[chunk] if isinstance(chunk, int) else \
                ada_in[bass.ds(chunk, 1)].rearrange("o p k n -> p (o k) n")
            pool.dma_start(ada_ring[s][:, :, :], src).then_inc(S(f"ada_loaded{s}"), 16)

        def pool_ada(pool):
            for s in range(2):
                ada_load(pool, s, s)
            pool.wait_ge(S("c_act"), 1)
            with pool.Fori(0, ADA_N // 2) as i:
                for s in range(2):
                    ada_chunk(pool, s, 0, i)
                    ada_load(pool, s, i * 2 + (2 + s))
            pool.wait_ge(S("mod_ps"), 1)
            with pool.Fori(0, ADA_N // 2 - 1) as i:
                for s in range(2):
                    ada_chunk(pool, s, 1, i)
                    ada_load(pool, s, i * 2 + (ADA_N + 2 + s))
            for s in range(2):
                ada_chunk(pool, s, 1)

        B = carve(keep, [("qk", (8, T)), ("vt", (2, 512)), ("z", (4, T)), ("dn", (12, T)), ("ya", (4, T)),
                         ("rows", (7, T)), ("tok", (8, 36))])
        HB = (4, P)
        W = carve(late, [("kt", (2, 4, P)), ("vt", (2, 4, P)), ("dt", (2, 4, P)), ("lt", (2, 4, P)),
                         ("t", (2, 4, P)), ("u", (2, 4, P)), ("qk", (2, 4, P)), ("vb", (2, 4, P)),
                         ("kbg", HB), ("kd", HB), ("qd", HB), ("s", HB)])
        W["w"] = W["kbg"]
        W2 = carve(late, [("sq", (8, T)), ("rot", (8, T)), ("e", (2, 2, T)), ("a", (2, T)), ("at", (2, T)),
                          ("st", (8, 8)), ("lam", (8,))])
        gate = keep[:, 0:16 * T].rearrange("p (a b) -> p a b", b=T)
        merged = B["dn"][:, 4:12, :]
        dconv = tmp
        R36 = 36
        RB, RG, RE, RBG, RNG, RKD, RX = (B["rows"][0:R36, k, :] for k in range(7))
        tokd = B["tok"]
        dn = B["dn"]
        dq, dk, dv = dn[:, 0:4, :], dn[:, 4:8, :], dn[:, 8:12, :]
        l2 = W["t"].rearrange("p c h n -> p (c h n)")
        l2k = W["u"].rearrange("p c h n -> p (c h n)")
        flat = lambda v: v.rearrange("p a b -> p (a b)")
        oacc = acc8[:, 4:8, :]

        def first_second(d):
            return (0, 1) if d == 0 else (1, 0)

        def pe_b2_in(pe, l):
            pe.wait_ge(S("ada_step"), 4 * ADA_N * (l + 1))
            for j in range(48):
                ins = mm(misc[1][:, j:j + 1], ada_acc[:, P * j:P * (j + 1)], ones[:, 0:1], start=True, stop=True)
            ins.then_inc(S("mod_ps"), 1)
            pe_norm(pe, f"pre1_{l}")
            pe.wait_ge(S("h_exact"), 4 * HU[f"pre1_{l}"] + 4)
            c0, n0 = CH0[f"in2_{l}"], U0[f"in2_{l}"]
            pe.wait_ge(S("mod_done"), l + 1)
            for g in range(2):
                for k in range(8):
                    at = PAR["ba_w"] + (8 * l + k) * 72 + 36 * g
                    ins = mm(misc[1][0:R36, T * g:T * (g + 1)], par[:, at:at + 36], h[:, k, :],
                             start=(k == 0), stop=(k == 7))
            ins.then_inc(S("ba_ps"), 1)
            pe_unit(pe, c0, n0, h_count=4 * HU[f"pre1_{l}"])
            pe_unit(pe, c0 + 1, n0 + 1)
            pe_units(pe, c0 + 2, n0 + 2, 8)
            for j in range(10, 14):
                pe_unit(pe, c0 + j, n0 + j, tokens_out=(j < 12))

        def act_b2_in(ac, l, link):
            act_norm(ac, f"pre1_{l}", x, x_ready(ac, "ffn_post1" if l == 0 else "res2_0"))
            act_h(ac, f"pre1_{l}")
            c0, n0 = CH0[f"in2_{l}"], U0[f"in2_{l}"]

            def centre(j):
                if j >= 4:
                    ac.wait_ge(S("dn_conv"), 12 * l + j - 3)
                if j % 2 == 0:
                    ahead(act_split, ac, c0 + j // 2)
                    done_after(ac, c0 + j // 2)
                act(dconv[:, j % 4, :], unit[(j // 2) % 2][:, T * (j % 2):T * (j % 2 + 1)], ACT.Identity,
                    bias=one("zero"), scale=pr("dn_conv", 60 * l + 5 * j + 2)).then_inc(S("dn_tap"), 1)

            centre(0)
            centre(1)
            for j in range(12):
                if j + 2 < 12:
                    centre(j + 2)
                ac.wait_ge(S("dn_taps"), 12 * l + j + 1)
                act(dn[:, j, :], dconv[:, j % 4, :], ACT.Silu).then_inc(S("dn_conv"), 1)
            ac.wait_ge(S("unit_free"), n0 + 6 + 2)
            for j in range(6, 14):
                if j == 7:
                    ac.preload_act_table(ACT.Sigmoid)
                    ac.wait_ge(S("ba_ps"), l + 1)
                    ac.wait_ge(S("a_in"), l + 1)
                    act(RB, misc[1][0:R36, 0:T], ACT.Sigmoid).then_inc(S("beta"), 1)
                    ac.preload_act_table_set(LN_EXP)
                    link(act(RE, RX, ACT.Abs))
                    link(act(RE, RE, ACT.Exp, scale=-1.0))
                    link(act(RE, RE, ACT.Ln, bias=one("one", R36)))
                    act(RG[:, 0:1], pr("A_log", l, R36), ACT.Exp).then_inc(S("a_log_done"), 1)
                    ac.wait_ge(S("g_sum"), l + 1)
                    act(RE, RG, ACT.Exp)
                    act(RNG, RG, ACT.Copy, scale=-1.0)
                    for c in range(2):
                        s = slice(P * c, P * (c + 1))
                        act(RKD[0:32, s], RG[0:32, s], ACT.Exp, bias=RG[0:32, P * c + P - 1:P * c + P], scale=-1.0)
                        ins = act(RKD[32:R36, s], RG[32:R36, s], ACT.Exp, bias=RG[32:R36, P * c:P * c + 1], scale=-1.0)
                    ins.then_inc(S("g_exps"), 1)
                ahead(act_split, ac, c0 + j)
                done_after(ac, c0 + j)
                u = unit[(n0 + j) % 2]
                if j < 10:
                    ins = act(B["qk"][:, 2 * (j - 6):2 * (j - 6) + 2, :], u[:, :], ACT.Copy)
                elif j < 12:
                    ins = act(B["vt"][:, :, T * (j - 10):T * (j - 9)], u[:, :].rearrange("p (a b) -> p a b", b=T), ACT.Copy)
                else:
                    ins = act(B["z"][:, 2 * (j - 12):2 * (j - 12) + 2, :], u[:, :], ACT.Silu)
                ins.then_inc(S("unit_free"), 1)

        def dve_b2_in(dve, l, link):
            dve.wait_ge(S("mod_ps"), l + 1)
            if l == 1:
                dve.wait_ge(S("x_ready"), 4 * XU["res2_0"] + 4)
            link(tt(mod[:, :], misc[1][:, 0:48], par[:, PAR["ada_b"] + 48 * l:PAR["ada_b"] + 48 * (l + 1)], ALU.add))
            for k, name in enumerate(("n1", "n2")):
                w = par[:, PAR[name] + 8 * l:PAR[name] + 8 * (l + 1)]
                ins = stt(gsc[:, 8 * k:8 * (k + 1)], mod[:, 24 * k + 8:24 * k + 16], 1.0, w, ALU.add, ALU.mult)
            link(ins)
            dve.sem_inc(S("mod_done"), 1)
            dve_modulated(dve, link, f"pre1_{l}", 0)
            dve.wait_ge(S("unit_free"), U0[f"in2_{l}"] + 2)
            for j in range(12):
                if j % 2 == 0:
                    ahead(dve_split, dve, CH0[f"in2_{l}"] + j // 2)
                    dve.wait_ge(S("dn_tap"), 12 * l + j + 2)
                src = unit[(j // 2) % 2][:, T * (j % 2):T * (j % 2 + 1)]
                dst = dconv[:, j % 4, :]
                w = lambda k: pr("dn_conv", 60 * l + 5 * j + k)
                link(stt(dst[:, 1:T], src[:, 0:T - 1], w(1), dst[:, 1:T], ALU.mult, ALU.add))
                link(stt(dst[:, 2:T], src[:, 0:T - 2], w(0), dst[:, 2:T], ALU.mult, ALU.add))
                link(stt(dst[:, 0:T - 1], src[:, 1:T], w(3), dst[:, 0:T - 1], ALU.mult, ALU.add))
                stt(dst[:, 0:T - 2], src[:, 2:T], w(4), dst[:, 0:T - 2], ALU.mult, ALU.add).then_inc(S("dn_taps"), 1)
                if j % 2:
                    dve.wait_ge(S("dn_taps"), 12 * l + j + 1)
                    dve.sem_inc(S("unit_free"), 1)
            ahead(dve_split, dve, CH0[f"in2_{l}"] + 6)
            dve.wait_ge(S("ba_ps"), l + 1)
            ts(RX, misc[1][0:R36, T:2 * T], pr("dn_dt", l, R36), None, ALU.add).then_inc(S("a_in"), 1)
            dve.wait_ge(S("a_log_done"), l + 1)
            link(stt(RX, RX, 0.0, RE, ALU.max, ALU.add))
            link(ts(RX, RX, RG[:, 0:1], -1.0, ALU.mult, ALU.mult))
            link(nc.vector.memset(RKD, 1.0))
            for c in range(2):
                a, z = P * c, P * (c + 1)
                nc.vector.tensor_tensor_scan(RG[0:32, a:z], RKD[0:32, a:z], RX[0:32, a:z], 0.0, ALU.mult, ALU.add)
                back = lambda v: v[32:R36, a:z][:, ::-1]
                ins = nc.vector.tensor_tensor_scan(back(RG), back(RKD), back(RX), 0.0, ALU.mult, ALU.add)
            ins.then_inc(S("g_sum"), 1)
            dve.wait_ge(S("beta"), l + 1)
            dve.wait_ge(S("g_exps"), l + 1)
            tt(RBG, RB, RE, ALU.mult).then_inc(S("dn_rows"), 1)
            for j in range(7, 14):
                ahead(dve_split, dve, CH0[f"in2_{l}"] + j)

        def dve_modulated(dve, link, name, k0):
            def tiles(q):
                s = tmp[:, 2 * (q % 2):2 * (q % 2) + 2, :]
                for k in range(2):
                    t = 2 * q + k
                    ins = stt(s[:, k, :], x[:, t, :], gsc[:, 8 * k0 + t:8 * k0 + t + 1], rstd[:, :], ALU.mult, ALU.mult)
                link(ins)
                for k in range(2):
                    t = 2 * q + k
                    ins = ts(h[:, t, :], s[:, k, :], mod[:, 24 * k0 + t:24 * k0 + t + 1], None, ALU.add)
                return ins
            dve_h(dve, name, tiles)

        def heads(b):
            return b.rearrange("p (h n) -> p h n", n=P)

        def pe_delta(pe, l):
            for k in range(8):
                if k % 4 == 0:
                    pe.wait_ge(S("dn_sq"), 2 * l + k // 4 + 1)
                src = (l2 if k < 4 else l2k)[:, T * (k % 4):T * (k % 4 + 1)]
                ins = mm(acc8[:, k, :], ones, src, start=(k % 2 == 0), stop=(k % 2 == 1))
            ins.then_inc(S("dn_ssum"), 1)
            pe.wait_ge(S("dn_rows"), l + 1)
            for c in range(2):
                for k, r in enumerate((RB, RNG, RBG, RKD)):
                    at = 36 * (4 * c + k)
                    ins = nc.tensor.transpose(misc[1][:, at:at + 36], r[:, P * c:P * (c + 1)], ident[0:R36, 0:R36])
            ins.then_inc(S("dn_tok_ps"), 1)
            pe.wait_ge(S("unit_free"), U0[f"in2_{l}"] + 14 + 2)
            pe.wait_ge(S("dn_unit"), l + 1)
            for c in range(2):
                for hd in range(4):
                    ins = nc.tensor.transpose(unit[c][:, P * hd:P * (hd + 1)], dk[:, hd, P * c:P * (c + 1)], ident)
                ins.then_inc(S("dn_kt_ps"), 1)
            pe.wait_ge(S("dn_tok"), l + 1)
            for c in range(2):
                for hd in range(4):
                    ins = nc.tensor.transpose(misc[c][:, P * hd:P * (hd + 1)], dv[:, hd, P * c:P * (c + 1)], ident)
                ins.then_inc(S("dn_vt_ps"), 1)
            pe.wait_ge(S("dn_kt"), 2 * l + 2)
            pe.wait_ge(S("dn_vt"), 2 * l + 2)
            for d in range(2):
                n = 2 * l + d
                row = lambda r, hd: (ident[0:R36, 32 * d + hd:32 * d + hd + 1].to_broadcast([R36, P]), r)
                if d == 1:
                    pe.wait_ge(S("dn_dir_done"), n)
                for c in range(2):
                    s = slice(P * c, P * (c + 1))
                    for hd in range(4):
                        sel, r = row(RG, hd)
                        mm(unit[c][:, P * hd:P * (hd + 1)], sel, r[:, s], start=(hd == 0), stop=False, skip_group_check=True)
                    for hd in range(4):
                        ins = mm(unit[c][:, P * hd:P * (hd + 1)], ident, cn("neg_up" if d == 0 else "neg_lo"),
                                 start=False, stop=(hd == 3), skip_group_check=True)
                    ins.then_inc(S("dn_decay_ps"), 1)
                    for hd in range(4):
                        mm(misc[c][:, P * hd:P * (hd + 1)], dk[:, hd, s], dk[:, hd, s], start=True, stop=True)
                    for hd in range(4):
                        ins = mm(bank(c, P * hd, P * (hd + 1)), dk[:, hd, s], dq[:, hd, s], start=True, stop=True)
                    ins.then_inc(S("dn_kk_ps"), 1)
                for c in range(2):
                    pe.wait_ge(S("dn_decay"), 2 * n + c + 1)
                    for hd in range(4):
                        sel, r = row(RB, hd)
                        ins = mm(unit[c][:, P * hd:P * (hd + 1)], sel, r[:, P * c:P * (c + 1)], start=True, stop=True)
                    ins.then_inc(S("dn_beta_ps"), 1)
                for c in range(2):
                    pe.wait_ge(S("dn_lt"), 2 * n + c + 1)
                    for hd in range(4):
                        ins = mm(unit[c][:, P * hd:P * (hd + 1)], W["lt"][:, c, hd, :], ident, start=True, stop=True)
                    ins.then_inc(S("dn_a_ps"), 1)
                for v in range(1, 7):
                    m = 7 * n + v
                    for c in range(2):
                        pe.wait_ge(S("dn_t"), 2 * (m - n) - 2 + c + 1)
                        for hd in range(4):
                            ins = mm(unit[c][:, P * hd:P * (hd + 1)], W["lt"][:, c, hd, :], W["t"][:, c, hd, :],
                                     start=True, stop=True)
                        ins.then_inc(S("dn_a_ps"), 1)
                    for c in range(2):
                        pe.wait_ge(S("dn_u"), 2 * m - 2 + c + 1)
                        pe.wait_ge(S("dn_a"), 2 * m + c + 1)
                        for hd in range(4):
                            ins = mm(bank(c, P * hd, P * (hd + 1)), W["dt"][:, c, hd, :], W["u"][:, c, hd, :],
                                     start=True, stop=True)
                        if v < 6:
                            for hd in range(4):
                                ins = mm(misc[c][:, P * hd:P * (hd + 1)], W["u"][:, c, hd, :], W["dt"][:, c, hd, :],
                                         start=True, stop=True)
                        ins.then_inc(S("dn_de_ps"), 1)
                c1, c2 = first_second(d)
                s2 = slice(P * c2, P * (c2 + 1))
                pe.wait_ge(S("dn_u"), 14 * n + 14)
                for hd in range(4):
                    sel, r = row(RE, hd)
                    ins = mm(unit[0][:, P * hd:P * (hd + 1)], sel, r[:, s2], start=True, stop=True)
                ins.then_inc(S("dn_eg_ps"), 1)
                pe.wait_ge(S("dn_vb"), n + 1)
                for hd in range(4):
                    ins = mm(misc[0][:, P * hd:P * (hd + 1)], W["u"][:, c1, hd, :], W["vb"][:, c1, hd, :],
                             start=True, stop=True)
                ins.then_inc(S("dn_v1_ps"), 1)
                for hd in range(4):
                    ins = mm(bank(0, P * hd, P * (hd + 1)), W["kbg"][:, hd, :], W["u"][:, c2, hd, :], start=True, stop=True)
                ins.then_inc(S("dn_w_ps"), 1)
                pe.wait_ge(S("dn_v1"), n + 1)
                for hd in range(4):
                    ins = mm(bank(1, P * hd, P * (hd + 1)), W["kd"][:, hd, :], W["vb"][:, c1, hd, :], start=True, stop=True)
                ins.then_inc(S("dn_s_ps"), 1)
                for hd in range(4):
                    mm(oacc[:, hd, P * c1:P * (c1 + 1)], W["vb"][:, c1, hd, :], W["qk"][:, c1, hd, :],
                       start=(d == 0 and hd % 2 == 0), stop=False)
                for hd in range(4):
                    mm(misc[1][:, P * hd:P * (hd + 1)], W["u"][:, c2, hd, :], W["vb"][:, c2, hd, :],
                       start=(hd == 0), stop=False)
                pe.wait_ge(S("dn_w"), n + 1)
                pe.wait_ge(S("dn_s"), n + 1)
                for hd in range(4):
                    ins = mm(misc[1][:, P * hd:P * (hd + 1)], W["w"][:, hd, :], W["s"][:, hd, :], start=False, stop=(hd == 3))
                ins.then_inc(S("dn_v2_ps"), 1)
                pe.wait_ge(S("dn_qd"), n + 1)
                for hd in range(4):
                    mm(oacc[:, hd, s2], W["s"][:, hd, :], W["qd"][:, hd, :], start=False, stop=False)
                pe.wait_ge(S("dn_v2"), n + 1)
                for hd in range(4):
                    ins = mm(oacc[:, hd, s2], W["vb"][:, c2, hd, :], W["qk"][:, c2, hd, :], start=False,
                             stop=(d == 1 and hd % 2 == 1))
                ins.then_inc(S("dn_o_ps"), 1)
            pe.wait_ge(S("o_sq"), 2 * l + 1)
            for hd in range(4):
                ins = mm(unit[hd // 2][:, T * (hd % 2):T * (hd % 2 + 1)], ones, l2[:, T * hd:T * (hd + 1)],
                         start=(hd % 2 == 0), stop=(hd % 2 == 1))
            ins.then_inc(S("o_ssum"), 1)

        def act_delta(ac, l, link):
            ac.preload_act_table_set(LN_EXP)
            for k in range(2):
                if k == 0:
                    ac.wait_ge(S("dn_conv"), 12 * l + 8)
                act((l2, l2k)[k], dn[:, 4 * k:4 * k + 4, :], ACT.Square).then_inc(S("dn_sq"), 1)
            ac.wait_ge(S("dn_ssum"), l + 1)
            for k in range(2):
                link(act((l2, l2k)[k], acc[:, 1024 * k:1024 * (k + 1)], ACT.Ln, bias=one("eps")))
            for k in range(2):
                act((l2, l2k)[k], (l2, l2k)[k], ACT.Exp, scale=-0.5).then_inc(S("dn_rnorm"), 1)
            for c in range(2):
                ac.wait_ge(S("dn_kt_ps"), 2 * l + c + 1)
                act(W["kt"][:, c, :, :], unit[c][:, :], ACT.Copy).then_inc(S("dn_kt"), 1)
            for d in range(2):
                n = 2 * l + d
                for c in range(2):
                    ac.wait_ge(S("dn_decay_ps"), 2 * n + c + 1)
                    for hd in range(4):
                        ins = act(W["dt"][:, c, hd, :], unit[c][:, P * hd:P * (hd + 1)], ACT.Exp,
                                  bias=tokd[:, 4 * c + 1, 32 * d + hd:32 * d + hd + 1])
                    ins.then_inc(S("dn_decay"), 1)
                ac.wait_ge(S("dn_w_ps"), n + 1)
                act(flat(W["w"]), bank(0, 0, 512), ACT.Copy, scale=-1.0).then_inc(S("dn_w"), 1)
                ac.wait_ge(S("dn_s_ps"), n + 1)
                act(flat(W["s"]), bank(1, 0, 512), ACT.Copy).then_inc(S("dn_s"), 1)
            ac.wait_ge(S("dn_o_ps"), 2 * l + 2)
            act_onorm(ac, 2 * l, l2, l2)

        def act_onorm(ac, n, sq, out):
            act(sq, acc[:, 1024:2048], ACT.Square).then_inc(S("o_sq"), 1)
            ac.wait_ge(S("o_ssum"), n + 1)
            for k in range(2):
                ins = act(out[:, 512 * k:512 * (k + 1)], unit[k][:, :], ACT.Ln, bias=one("eps"), scale=1.0 / P)
            ins.then_inc(S("o_log"), 1)
            ac.wait_ge(S("o_log"), n + 1)
            act(out, out, ACT.Exp, scale=-0.5).then_inc(S("o_rms"), 1)

        def dve_delta(dve, l, link):
            for k in range(2):
                dve.wait_ge(S("dn_rnorm"), 2 * l + k + 1)
                v = dn[:, 4 * k:4 * k + 4, :].rearrange("p a b -> p (a b)")
                link(stt(v, v, P ** -0.5 if k == 0 else 1.0, (l2, l2k)[k], ALU.mult, ALU.mult))
            dve.sem_inc(S("dn_unit"), 1)
            dve.wait_ge(S("dn_tok_ps"), l + 1)
            nc.vector.tensor_copy(tokd, misc[1][:, 0:288].rearrange("p (a b) -> p a b", b=36)).then_inc(S("dn_tok"), 1)
            for c in range(2):
                dve.wait_ge(S("dn_vt_ps"), 2 * l + c + 1)
                nc.vector.tensor_copy(W["vt"][:, c, :, :], heads(misc[c][:, :])).then_inc(S("dn_vt"), 1)
            dve.wait_ge(S("dn_kt"), 2 * l + 2)
            dve.wait_ge(S("dn_vt"), 2 * l + 2)
            dve.wait_ge(S("dn_tok"), l + 1)
            for d in range(2):
                n = 2 * l + d
                c1, c2 = first_second(d)
                col = lambda c, k: tokd[:, 4 * c + k, 32 * d:32 * d + 4].unsqueeze(2).to_broadcast([P, 4, P])
                for c in range(2):
                    tt(W["vb"][:, c, :, :], W["vt"][:, c, :, :], col(c, 0), ALU.mult)
                tt(W["kbg"], W["kt"][:, c2, :, :], col(c2, 2), ALU.mult)
                tt(W["kd"], W["kt"][:, c1, :, :], col(c1, 3), ALU.mult).then_inc(S("dn_vb"), 1)
                for c in range(2):
                    dve.wait_ge(S("dn_decay"), 2 * n + c + 1)
                    dve.wait_ge(S("dn_kk_ps"), 2 * n + c + 1)
                    dt = W["dt"][:, c, :, :]
                    tt(W["qk"][:, c, :, :], heads(bank(c, 0, 512)), dt, ALU.mult)
                    link(tt(W["lt"][:, c, :, :], heads(misc[c][:, :]), dt, ALU.mult))
                    dve.wait_ge(S("dn_beta_ps"), 2 * n + c + 1)
                    tt(W["lt"][:, c, :, :], W["lt"][:, c, :, :], heads(unit[c][:, :]), ALU.mult).then_inc(S("dn_lt"), 1)
                level = lambda v, k: cn("level", P * (2 * v + (k + d) % 2)).unsqueeze(1).to_broadcast([P, 4, P])
                eye = ident.unsqueeze(1).to_broadcast([P, 4, P])
                for v in range(7):
                    m = 7 * n + v
                    for c in range(2):
                        a, tm, um = W["dt"][:, c, :, :], W["t"][:, c, :, :], W["u"][:, c, :, :]
                        dve.wait_ge(S("dn_a_ps"), 2 * m + c + 1)
                        tt(a, heads(unit[c][:, :]), level(v, 0), ALU.mult).then_inc(S("dn_a"), 1)
                        if v == 0:
                            link(tt(um, W["lt"][:, c, :, :], level(0, 1), ALU.mult))
                            tt(um, eye, um, ALU.subtract).then_inc(S("dn_u"), 1)
                            dve.wait_ge(S("dn_a"), 2 * m + c + 1)
                            tt(tm, eye, a, ALU.subtract).then_inc(S("dn_t"), 1)
                    if v > 0:
                        for c in range(2):
                            tm, um = W["t"][:, c, :, :], W["u"][:, c, :, :]
                            dve.wait_ge(S("dn_de_ps"), 2 * (m - n - 1) + c + 1)
                            side = lambda b, odd: b.rearrange("p (k e m) -> p k e m", e=2, m=1 << v)[:, :, odd, :]
                            tm, um = (b.rearrange("p h n -> p (h n)") for b in (tm, um))
                            if v < 6:
                                tt(side(tm, d), side(tm, d), side(misc[c][:, :], d), ALU.subtract).then_inc(S("dn_t"), 1)
                            tt(side(um, 1 - d), side(um, 1 - d), side(bank(c, 0, 512), 1 - d), ALU.subtract
                               ).then_inc(S("dn_u"), 1)
                dve.wait_ge(S("dn_eg_ps"), n + 1)
                tt(W["qd"], dq[:, :, P * c2:P * (c2 + 1)], heads(unit[0][:, :]), ALU.mult).then_inc(S("dn_qd"), 1)
                dve.wait_ge(S("dn_v1_ps"), n + 1)
                nc.vector.tensor_copy(W["vb"][:, c1, :, :], heads(misc[0][:, :])).then_inc(S("dn_v1"), 1)
                dve.wait_ge(S("dn_v2_ps"), n + 1)
                nc.vector.tensor_copy(W["vb"][:, c2, :, :], heads(misc[1][:, :])).then_inc(S("dn_v2"), 1)
                dve.wait_ge(S("dn_o_ps"), n + 1)
                dve.sem_inc(S("dn_dir_done"), 1)
            dve.wait_ge(S("o_rms"), 2 * l + 1)
            yb = dn[:, 0:4, :].rearrange("p a b -> p (a b)")
            link(stt(yb, acc[:, 1024:2048], pr("dn_gain", l), l2, ALU.mult, ALU.mult))
            tt(yb, yb, flat(B["z"]), ALU.mult).then_inc(S("yb_done"), 1)

        sq8 = W2["sq"].rearrange("p a b -> p (a b)")
        qk8 = B["qk"].rearrange("p a b -> p (a b)")

        def sbank(n, t):
            return unit[n % 2][:, 0:T] if t == 0 else bank(n % 2, 0, T)

        def lambda_init(l):
            return 0.8 - 0.6 * math.exp(-0.3 * l)

        def pe_attn(pe, l):
            for k in range(8):
                pe.wait_ge(S("at_sq"), 2 * l + k // 4 + 1)
                ins = mm(acc8[:, k, :], cn("half_ones"), W2["sq"][:, k, :], start=(k % 2 == 0), stop=(k % 2 == 1))
            ins.then_inc(S("at_ssum"), 1)
            pe.wait_ge(S("at_lam_in"), l + 1)
            mm(misc[1][:, 0:2], ones[0:64, :], W2["lam"][0:64, 0:2], start=True, stop=True).then_inc(S("at_lam_ps"), 1)
            pe.wait_ge(S("at_unit"), l + 1)
            for k in range(8):
                ins = mm(acc8[:, k, :], cn("rope"), B["qk"][:, k, :], start=(k % 2 == 0), stop=(k % 2 == 1))
            ins.then_inc(S("at_rot_ps"), 1)
            pe.wait_ge(S("at_rope"), l + 1)
            pe.wait_ge(S("at_lam"), l + 1)

            def scores(n):
                hd, qb = n // 2, n % 2
                if n >= 2:
                    pe.wait_ge(S("at_exp"), 8 * l + n - 1)
                for t in range(2):
                    r = slice(64 * t, 64 * (t + 1))
                    ins = mm(sbank(n, t), B["qk"][r, hd, P * qb:P * (qb + 1)], B["qk"][r, 4 + hd, :],
                             start=True, stop=True)
                ins.then_inc(S("at_s_ps"), 1)

            scores(0)
            scores(1)
            for n in range(8):
                hd, qb = n // 2, n % 2
                if n + 2 < 8:
                    scores(n + 2)
                pe.wait_ge(S("at_a"), 8 * l + n + 1)
                if n >= 2:
                    pe.wait_ge(S("at_at"), 8 * l + n - 1)
                for kb in range(2):
                    ins = nc.tensor.transpose(misc[n % 2][:, P * kb:P * (kb + 1)], W2["a"][:, n % 2, P * kb:P * (kb + 1)],
                                              ident)
                ins.then_inc(S("at_at_ps"), 1)
                pe.wait_ge(S("at_at"), 8 * l + n + 1)
                for kb in range(2):
                    ins = mm(oacc[:, hd, P * qb:P * (qb + 1)], B["vt"][:, kb, P * hd:P * (hd + 1)],
                             W2["at"][:, n % 2, P * kb:P * (kb + 1)], start=(kb == 0), stop=(kb == 1))
                ins.then_inc(S("at_o_ps"), 1)
            pe.wait_ge(S("o_sq"), 2 * l + 2)
            for hd in range(4):
                ins = mm(unit[hd // 2][:, T * (hd % 2):T * (hd % 2 + 1)], ones, W2["sq"][:, hd, :],
                         start=(hd % 2 == 0), stop=(hd % 2 == 1))
            ins.then_inc(S("o_ssum"), 1)

        def act_attn(ac, l, link):
            ac.wait_ge(S("yb_done"), l + 1)
            for k in range(2):
                act(sq8[:, 1024 * k:1024 * (k + 1)], qk8[:, 1024 * k:1024 * (k + 1)], ACT.Square).then_inc(S("at_sq"), 1)
            ac.wait_ge(S("at_ssum"), l + 1)
            for k in range(2):
                link(act(sq8[:, 1024 * k:1024 * (k + 1)], acc[:, 1024 * k:1024 * (k + 1)], ACT.Ln, bias=one("eps"),
                         scale=1.0 / 64))
            for k in range(2):
                s = sq8[:, 1024 * k:1024 * (k + 1)]
                act(s, s, ACT.Exp, scale=-0.5).then_inc(S("at_rnorm"), 1)
            ac.wait_ge(S("at_lam_ps"), l + 1)
            act(W2["lam"][:, 2:4], misc[1][:, 0:2], ACT.Exp).then_inc(S("at_lam_exp"), 1)

            def exps(n):
                ac.wait_ge(S("at_max"), 8 * l + n + 1)
                if n >= 2:
                    ac.wait_ge(S("at_a"), 8 * l + n - 1)
                for t in range(2):
                    ins = act(W2["e"][:, n % 2, t, :], sbank(n, t), ACT.Exp, scale=0.125,
                              bias=W2["st"][:, n, 2 + t:3 + t], accum_out=W2["st"][:, n, 4 + t:5 + t])
                ins.then_inc(S("at_exp"), 1)

            exps(0)
            for n in range(8):
                if n + 1 < 8:
                    exps(n + 1)
                ac.wait_ge(S("at_at_ps"), 8 * l + n + 1)
                if n >= 2:
                    ac.wait_ge(S("at_o_ps"), 8 * l + n - 1)
                act(W2["at"][:, n % 2, :], misc[n % 2][:, 0:T], ACT.Copy).then_inc(S("at_at"), 1)
            ac.wait_ge(S("at_o_ps"), 8 * l + 8)
            act_onorm(ac, 2 * l + 1, sq8[:, 0:1024], sq8[:, 0:1024])

        def dve_attn(dve, l, link):
            lam, st = W2["lam"], W2["st"]
            dve.wait_ge(S("yb_done"), l + 1)
            dl = par[0:64, PAR["dlam"] + 4 * l:PAR["dlam"] + 4 * l + 4].rearrange("p (a b) -> p a b", b=2)
            tt(lam[0:64, 0:2], dl[:, :, 0], dl[:, :, 1], ALU.mult).then_inc(S("at_lam_in"), 1)
            for k in range(2):
                dve.wait_ge(S("at_rnorm"), 2 * l + k + 1)
                v = qk8[:, 1024 * k:1024 * (k + 1)]
                link(stt(v, v, pr("qk_gain", 2 * l + k), sq8[:, 1024 * k:1024 * (k + 1)], ALU.mult, ALU.mult))
            dve.sem_inc(S("at_unit"), 1)
            dve.wait_ge(S("at_lam_exp"), l + 1)
            link(tt(lam[:, 4:5], lam[:, 3:4], lam[:, 2:3], ALU.subtract))
            ts(lam[:, 5:6], lam[:, 4:5], -lambda_init(l), None, ALU.add)
            ts(lam[:, 6:7], pr("subln", l), 1.0 - lambda_init(l), None, ALU.mult).then_inc(S("at_lam"), 1)
            dve.wait_ge(S("at_rot_ps"), l + 1)
            wide = lambda name: cn(name, 0, T).unsqueeze(1).to_broadcast([P, 8, T])
            tt(W2["rot"], acc8[:, :, :], wide("sin"), ALU.mult)
            link(tt(B["qk"], B["qk"], wide("cos"), ALU.mult))
            tt(B["qk"], B["qk"], W2["rot"], ALU.add).then_inc(S("at_rope"), 1)

            def maximum(n):
                dve.wait_ge(S("at_s_ps"), 8 * l + n + 1)
                for t in range(2):
                    ins = nc.vector.tensor_reduce(st[:, n, t:t + 1], sbank(n, t), AX.X, ALU.max)
                link(ins)
                ts(st[:, n, 2:4], st[:, n, 0:2], -0.125, None, ALU.mult).then_inc(S("at_max"), 1)

            maximum(0)
            maximum(1)
            for n in range(8):
                dve.wait_ge(S("at_exp"), 8 * l + n + 1)
                link(nc.vector.reciprocal(st[:, n, 6:8], st[:, n, 4:6]))
                link(tt(st[:, n, 7:8], st[:, n, 7:8], lam[:, 5:6], ALU.mult))
                if n >= 2:
                    dve.wait_ge(S("at_at_ps"), 8 * l + n - 1)
                a = W2["a"][:, n % 2, :]
                link(ts(a, W2["e"][:, n % 2, 0, :], st[:, n, 6:7], None, ALU.mult))
                stt(a, W2["e"][:, n % 2, 1, :], st[:, n, 7:8], a, ALU.mult, ALU.add).then_inc(S("at_a"), 1)
                if n + 2 < 8:
                    maximum(n + 2)
            dve.wait_ge(S("o_rms"), 2 * l + 2)
            stt(flat(B["ya"]), acc[:, 1024:2048], lam[:, 6:7], sq8[:, 0:1024], ALU.mult, ALU.mult).then_inc(S("ya_done"), 1)

        def pe_merge(pe, l):
            c0, n0 = CH0[f"in2_{l}"] + 14, U0[f"in2_{l}"] + 14
            pe.wait_ge(S("ya_done"), l + 1)
            pe_units(pe, c0, n0, 8)
            pe_out(pe, f"bra_{l}")
            pe.wait_ge(S("merge_a"), 4 * l + 4)
            pe_out(pe, f"brb_{l}")
            pe.wait_ge(S("merged"), 4 * l + 4)
            pe_out(pe, f"out2_{l}")

        def ya_pair(j):
            return B["ya"][:, 2 * j:2 * j + 2, :]

        def yb_pair(j):
            return dn[:, 2 * j:2 * j + 2, :]

        def merged_pair(j):
            return merged[:, 2 * j:2 * j + 2, :]

        def act_merge(ac, l):
            c0, n0 = CH0[f"in2_{l}"] + 14, U0[f"in2_{l}"] + 14
            ac.wait_ge(S("ya_done"), l + 1)
            epoch(act_split, ac, c0)
            for j in range(8):
                ahead(act_split, ac, c0 + j)
                done_after(ac, c0 + j)
                act(gate[:, 2 * j:2 * j + 2, :], unit[(n0 + j) % 2][:, :], ACT.Sigmoid).then_inc(S("unit_free"), 1)
            act_out(ac, f"bra_{l}", ya_pair, lambda j: None)
            act_out(ac, f"brb_{l}", yb_pair, lambda j: None)
            act_out(ac, f"out2_{l}", merged_pair, lambda j: ac.wait_ge(S("merged"), 4 * l + j + 1))

        def dve_merge(dve, l, link):
            c0 = CH0[f"in2_{l}"] + 14
            dve.wait_ge(S("ya_done"), l + 1)
            epoch(dve_split, dve, c0)
            for j in range(8):
                ahead(dve_split, dve, c0 + j)
            dve_out(dve, f"bra_{l}", ya_pair)
            ahead(dve_split, dve, END[f"bra_{l}"] - 1)
            done_after(dve, END[f"bra_{l}"] - 1)
            dve.wait_ge(S("unit_free"), U0[f"in2_{l}"] + 22 + 2)
            for q in range(4):
                s = slice(2 * q, 2 * q + 2)
                tt(merged[:, s, :], acc8[:, s, :], gate[:, s, :], ALU.mult).then_inc(S("merge_a"), 1)
            dve_out(dve, f"brb_{l}", yb_pair)
            ahead(dve_split, dve, END[f"brb_{l}"] - 1)
            done_after(dve, END[f"brb_{l}"] - 1)
            for q in range(4):
                s = slice(2 * q, 2 * q + 2)
                m = tmp[:, 2 * (q % 2):2 * (q % 2) + 2, :]
                link(tt(m, acc8[:, s, :], gate[:, 8 + 2 * q:10 + 2 * q, :], ALU.mult))
                tt(merged[:, s, :], merged[:, s, :], m, ALU.add).then_inc(S("merged"), 1)
            dve.wait_ge(S("merged"), 4 * l + 4)
            dve_out(dve, f"out2_{l}", merged_pair)

        M = carve(keep, [("r", (2, 2, T)), ("hid", (2, 2, T))])

        def pe_mlp(pe, l):
            c0, n0, b0 = CH0[f"mlp_{l}"], U0[f"mlp_{l}"], B0[f"mlp_{l}"]
            pe_unit(pe, c0, n0, h_count=4 * HU[f"pre2_{l}"])
            pe_unit(pe, c0 + 1, n0 + 1)
            pe_down(pe, c0 + 2, b0, True, False)
            with pe.Fori(0, 2) as i:
                for k in range(6):
                    pe_unit(pe, c0 + 3 + 2 * k, n0 + 2 + k, i, 12, 6)
                    pe_down(pe, c0 + 4 + 2 * k, b0 + 1 + k, False, False, i, 12, 6)
            pe_unit(pe, c0 + 27, n0 + 14)
            pe_down(pe, c0 + 28, b0 + 13, False, False)
            pe_unit(pe, c0 + 29, n0 + 15)
            pe_down(pe, c0 + 30, b0 + 14, False, False)
            pe_down(pe, c0 + 31, b0 + 15, False, True)

        def act_mlp(ac, l):
            c0, n0, b0, f0 = CH0[f"mlp_{l}"], U0[f"mlp_{l}"], B0[f"mlp_{l}"], 16 * l

            def relu(u, i=None):
                c = c0 + max(2 * u - 1, 0)
                ahead(act_split, ac, c, i, 12)
                done_after(ac, c, i, 12)
                if i is not None or u >= 2:
                    ac.wait_ge(S("mlp_square"), at(i, 6, f0 + u - 1))
                act(M["r"][:, u % 2, :, :], unit[(n0 + u) % 2][:, :], ACT.Relu).then_inc(S("unit_free"), 1)

            def moving(u, i=None):
                ac.wait_ge(S("mlp_square"), at(i, 6, f0 + u + 1))
                act_moving(ac, b0 + u, M["hid"][:, u % 2, :, :])

            relu(0)
            moving(0)

            def unit_and_down(u, i=None):
                relu(u, i)
                c = c0 + 2 * u
                if u < 15:
                    ahead(act_split, ac, c, i, 12)
                    done_after(ac, c, i, 12)
                    moving(u, i)
                else:
                    moving(u)
                    ahead(act_split, ac, c)

            with ac.Fori(0, 2) as i:
                for u in range(1, 7):
                    unit_and_down(u, i)
            for u in range(13, 16):
                unit_and_down(u)

        def dve_mlp(dve, l):
            c0, n0, b0, f0 = CH0[f"mlp_{l}"], U0[f"mlp_{l}"], B0[f"mlp_{l}"], 16 * l

            def square(u, i=None):
                ahead(dve_split, dve, c0 + max(2 * u - 1, 0), i, 12)
                dve.wait_ge(S("unit_free"), at(i, 6, n0 + u + 3))
                if i is not None or u >= 2:
                    dve.wait_ge(S("mv_ready"), at(i, 6, b0 + u - 1))
                r = M["r"][:, u % 2, :, :]
                tt(M["hid"][:, u % 2, :, :], r, r, ALU.mult).then_inc(S("mlp_square"), 1)

            def moving(u, i=None):
                dve.wait_ge(S("mlp_square"), at(i, 6, f0 + u + 1))
                dve_moving(dve, b0 + u, M["hid"][:, u % 2, :, :], i, 6)

            square(0)
            moving(0)

            def unit_and_down(u, i=None):
                square(u, i)
                if u < 15:
                    ahead(dve_split, dve, c0 + 2 * u, i, 12)
                    moving(u, i)
                else:
                    moving(u)
                    ahead(dve_split, dve, c0 + 2 * u)

            with dve.Fori(0, 2) as i:
                for u in range(1, 7):
                    unit_and_down(u, i)
            for u in range(13, 16):
                unit_and_down(u)

        block = ctx.enter_context(nc.Block())

        @block.sync
        def _(sp):
            def load(c):
                sp.dma_start(raw[c % RAW][:, :], w_in[c]).then_inc(loaded[c % RAW], 16)
            sp.dma_start(x[:, :, :], x_in).then_inc(S("x_loaded"), 16)
            for c in range(RAW):
                load(c)
            turns = NCHUNK // RAW
            with sp.Fori(1, turns) as i:
                for s in range(RAW):
                    sp.wait_ge(S("chunk_split"), i * (2 * RAW) + (2 * (s - RAW) + 2))
                    sp.dma_start(raw[s][:, :], w_in[bass.ds(i * RAW + s, 1)].rearrange("o p n -> p (o n)")
                                 ).then_inc(loaded[s], 16)
            for c in range(turns * RAW, NCHUNK):
                sp.wait_ge(S("chunk_split"), 2 * (c - RAW) + 2)
                load(c)
            for q in range(4):
                sp.wait_ge(S("x_ready"), 4 * XU["res2_1"] + q + 1)
                sp.dma_start(out[:, 2 * q:2 * q + 2, :], x[:, 2 * q:2 * q + 2, :]).then_inc(S("stored"), 16)
            sp.wait_ge(S("stored"), 64)

        @block.gpsimd
        def _(pool):
            pool_ada(pool)

        @block.tensor
        def _(pe):
            pe.wait_ge(S("con_loaded"), 16)
            pe.wait_ge(S("par_loaded"), 16)
            pe_norm(pe, "mix_pre0")
            pe_ssd(pe)
            pe_norm(pe, "mix_post0")
            pe_norm(pe, "ffn_pre0")
            pe_ffn(pe, 0)
            pe_norm(pe, "ffn_post0")
            pe_norm(pe, "mix_pre1")
            pe_lru(pe)
            pe_norm(pe, "mix_post1")
            pe_norm(pe, "ffn_pre1")
            pe_ffn(pe, 1)
            pe_norm(pe, "ffn_post1")
            for l in range(2):
                pe_b2_in(pe, l)
                pe_delta(pe, l)
                pe_attn(pe, l)
                pe_merge(pe, l)
                pe_norm(pe, f"pre2_{l}")
                pe_mlp(pe, l)

        @block.scalar
        def _(ac):
            ac.dma_start(par[:, :], par_in).then_inc(S("par_loaded"), 16)
            ac.dma_start(con[:, :], con_in).then_inc(S("con_loaded"), 16)
            link = Chain(ac, S("act_link"))

            def from_acc(stage):
                return lambda q: done_after(ac, END[stage] - 1)

            def split_after(stage):
                return lambda: ahead(act_split, ac, END[stage] - 1)

            ac.wait_ge(S("par_loaded"), 16)
            ac.wait_ge(S("con_loaded"), 16)
            act(cact[:, :], par[:, PAR["c"]:PAR["c"] + 8], ACT.Silu).then_inc(S("c_act"), 1)
            act_norm(ac, "mix_pre0", x, lambda q: ac.wait_ge(S("x_loaded"), 16), lambda: epoch(act_split, ac, 0))
            act_h(ac, "mix_pre0")
            act_ssd(ac, link)
            act_norm(ac, "mix_post0", acc8, from_acc("ssd_out"), split_after("ssd_out"))
            act_norm(ac, "ffn_pre0", x, x_ready(ac, "mix_post0"))
            act_h(ac, "ffn_pre0")
            act_ffn(ac, 0)
            act_norm(ac, "ffn_post0", acc8, from_acc("ffn0"), split_after("ffn0"))
            act_norm(ac, "mix_pre1", x, x_ready(ac, "ffn_post0"))
            act_h(ac, "mix_pre1")
            act_lru(ac, link)
            act_norm(ac, "mix_post1", R["m"], lambda q: ac.wait_ge(S("lru_m"), q + 1))
            act_norm(ac, "ffn_pre1", x, x_ready(ac, "mix_post1"))
            act_h(ac, "ffn_pre1")
            act_ffn(ac, 1)
            act_norm(ac, "ffn_post1", acc8, from_acc("ffn1"), split_after("ffn1"))
            for l in range(2):
                act_b2_in(ac, l, link)
                act_delta(ac, l, link)
                act_attn(ac, l, link)
                act_merge(ac, l)
                act_norm(ac, f"pre2_{l}", x, x_ready(ac, f"res1_{l}"))
                act_h(ac, f"pre2_{l}")
                act_mlp(ac, l)
                ahead(act_split, ac, END[f"mlp_{l}"] - 1)

        @block.vector
        def _(dve):
            link = Chain(dve, S("dve_link"))
            dve.sem_inc(S("unit_free"), 2)
            dve.sem_inc(S("x_ready"), 4)
            dve.wait_ge(S("par_loaded"), 16)
            dve.wait_ge(S("con_loaded"), 16)
            dve.wait_ge(S("x_loaded"), 16)
            epoch(dve_split, dve, 0)
            block1 = lambda name, l: (lambda t: pr(name, 8 * l + t))
            dve_pre(dve, "mix_pre0", block1("mix_pre", 0))
            dve_ssd(dve, link)
            ahead(dve_split, dve, END["ssd_out"] - 1)
            dve_post(dve, link, "mix_post0", block1("mix_post", 0), acc8)
            dve_pre(dve, "ffn_pre0", block1("ffn_pre", 0))
            dve_ffn(dve, 0, link)
            ahead(dve_split, dve, END["ffn0"] - 1)
            dve_post(dve, link, "ffn_post0", block1("ffn_post", 0), acc8)
            dve_pre(dve, "mix_pre1", block1("mix_pre", 1))
            dve_lru(dve, link)
            dve_post(dve, link, "mix_post1", block1("mix_post", 1), R["m"])
            dve_pre(dve, "ffn_pre1", block1("ffn_pre", 1))
            dve_ffn(dve, 1, link)
            ahead(dve_split, dve, END["ffn1"] - 1)
            dve_post(dve, link, "ffn_post1", block1("ffn_post", 1), acc8)
            gain = lambda k: (lambda t: mod[:, k + t:k + t + 1])
            for l in range(2):
                dve_b2_in(dve, l, link)
                dve_delta(dve, l, link)
                dve_attn(dve, l, link)
                dve_merge(dve, l, link)
                dve_residual(dve, f"res1_{l}", gain(16), f"out2_{l}")
                ahead(dve_split, dve, END[f"out2_{l}"] - 1)
                dve_modulated(dve, link, f"pre2_{l}", 1)
                dve_mlp(dve, l)
                dve_residual(dve, f"res2_{l}", gain(40), f"mlp_{l}")
                ahead(dve_split, dve, END[f"mlp_{l}"] - 1)


def arrays_of(a):
    ada = np.ascontiguousarray(
        a["ada_w_2"].reshape(2, 8, P, ADA_N, AW).transpose(0, 3, 2, 1, 4)).reshape(2 * ADA_N, P, 8, AW)
    return {
        "x_in": np.ascontiguousarray(a["x"][0].T.reshape(DT_, P, T).transpose(1, 0, 2)),
        "w_in": stream(a),
        "gates_in": lru_gates(a),
        "ada_in": ada,
        "par_in": parameters(a),
        "con_in": constants(),
    }


def kernel(**inputs):
    import concourse.bacc as bacc
    from concourse.bass_utils import run_bass_kernel_spmd

    arrays = arrays_of({k: np.asarray(v) for k, v in inputs.items()})
    nc = bacc.Bacc("TRN2", target_bir_lowering=False, num_devices=1)
    aps = [nc.dram_tensor(n, v.shape, mybir.dt.from_np(v.dtype), kind="ExternalInput").ap() for n, v in arrays.items()]
    out = nc.dram_tensor("out", (P, DT_, T), mybir.dt.float32, kind="ExternalOutput").ap()
    build(nc, *aps, out)
    r = run_bass_kernel_spmd(nc, [arrays], core_ids=[0])
    y = r.results[0]["out"]
    return np.ascontiguousarray(y.transpose(1, 0, 2).reshape(D, T).T)[None]
```

```python
import math

import numpy as np

import concourse.bass as bass
from concourse import mybir
from concourse.alu_op_type import AluOpType as ALU

P = 128
T = 256
D = 1024
DT_ = D // P
NCHK = T // P
RAW = 3
CW = 2048
H_SSD, G_SSD = 32, 4
XT = 16
BCT = 8
LT = 10
FT = 32
NH = 4
AW = 128
ADA_N = 6 * D // AW
EPS = 1e-6
NEG = -1e30

STAGES = [("ssd_in", 20, 0), ("ssd_out", 0, 8), ("ffn0", 32, 16), ("lru_in", 10, 0), 
          ("lru_out", 0, 5), ("ffn1", 32, 16)]
for _l in range(2):
    STAGES += [(f"in2_{_l}", 14, 0), (f"bra_{_l}", 0, 2), (f"ga_{_l}", 4, 0), (f"brb_{_l}", 0, 2),
               (f"gb_{_l}", 4, 0), (f"out2_{_l}", 0, 4),
               (f"mlp_{_l}", 16, 16)]
CH0, U0, B0 = {}, {}, {}
_c = _u = _b = 0
for _n, _a, _bb in STAGES:
    CH0[_n], U0[_n], B0[_n] = _c, _u, _b
    _c += _a + _bb
    _u += _a
    _b += _bb
NCHUNK = _c
EPOCHS = [0, CH0["ssd_out"], CH0["bra_0"], CH0["bra_1"], NCHUNK]


def _columns(sizes):
    at, out = 0, {}
    for name, n in sizes:
        out[name] = at
        at += n
    return out, at


PAR, NPAR = _columns([
    ("mix_pre", 16), ("mix_post", 16), ("ffn_pre", 16), ("ffn_post", 16),
    ("ssd_conv", 24 * 5), ("dt_w", 8 * 32), ("dt_bias", 1), ("a_log", 1), ("ssd_d", 16), ("ssd_norm", 16),
    ("lru_b_in", 20), ("lru_conv", LT * 5), ("b_gx", LT), ("b_ga", LT), ("lam", LT), ("b_out", 8),
    ("ffn_conv", 2 * FT * 8), ("c", 8), ("ada_b", 96), ("n1", 16), ("n2", 16), ("dn_conv", 2 * 12 * 5),
    ("ba_w", 2 * 8 * 72), ("A_log", 2), ("dn_dt", 2), ("dn_gain", 2), ("qk_gain", 4), ("dlam", 8), ("subln", 2)])
CON, NCON = _columns([
    ("eps", 1), ("one", 1), ("tiny", 1), ("zero", 1), ("ident", P), ("ones", P), ("half_ones", P),
    ("neg_up", P), ("neg_lo", P), ("rope", P), ("level", 14 * P),
    ("cos", T), ("sin", T)])
CON_FIRST = CON["half_ones"]


def constants():
    c = np.zeros((P, NCON), np.float32)
    i = np.arange(P)
    def put(name, m, k=0):
        c[:, CON[name] + k:CON[name] + k + m.shape[1]] = m
    put("ident", np.eye(P))
    put("ones", np.ones((P, P)))
    put("half_ones", (i[:, None] // 64 == i[None, :] // 64))
    put("neg_up", np.where(i[:, None] <= i[None, :], 0, NEG))
    put("neg_lo", np.where(i[:, None] >= i[None, :], 0, NEG))
    rope = np.zeros((P, P))
    for b in (0, 64):
        for j in range(32):
            rope[b + j + 32, b + j] = -1.0
            rope[b + j, b + j + 32] = 1.0
    put("rope", rope)
    for n in range(7):
        m = 1 << n
        low = ((i[:, None] // m) % 2 == 1) & ((i[None, :] // m) == (i[:, None] // m) - 1)
        put("level", low, 2 * n * P)
        put("level", low.T, (2 * n + 1) * P)
    inv = 1.0 / (10000.0 ** (np.arange(0, 64, 2, dtype=np.float32) / 64))
    ang = np.arange(T, dtype=np.float32)[:, None] * inv.astype(np.float32)[None, :]
    ang = np.concatenate([ang, ang, ang, ang], axis=-1).T
    put("cos", np.cos(ang))
    put("sin", np.sin(ang))
    put("eps", np.full((P, 1), EPS))
    put("one", np.ones((P, 1)))
    put("tiny", np.full((P, 1), 1e-30))
    return c


def tiled(v):
    return np.reshape(v, (-1, P)).T


def parameters(a):
    p = np.zeros((P, NPAR), np.float32)
    def put(name, m, k=0):
        p[0:m.shape[0], PAR[name] + k:PAR[name] + k + m.shape[1]] = m
    for l in range(2):
        for name, src in (("mix_pre", "norm_mix_pre"), ("mix_post", "norm_mix_post"), ("ffn_pre", "norm_ffn_pre"),
                          ("ffn_post", "norm_ffn_post"), ("n1", "norm1_g_2"), ("n2", "norm2_g_2")):
            put(name, tiled(a[src][l]), 8 * l)
        w, b = a["ffn_conv_w"][l], a["ffn_conv_b"][l]
        for half in range(2):
            for j in range(3):
                m = tiled(w[j])[:, FT * half:FT * (half + 1)]
                p[:, PAR["ffn_conv"] + l * FT * 8 + 4 * half + j:PAR["ffn_conv"] + (l + 1) * FT * 8:8] = m
            p[:, PAR["ffn_conv"] + l * FT * 8 + 4 * half + 3:PAR["ffn_conv"] + (l + 1) * FT * 8:8] = \
                tiled(b)[:, FT * half:FT * (half + 1)]
        put("ada_b", tiled(a["ada_b_2"][l]), 48 * l)
        for j in range(5):
            p[:, PAR["dn_conv"] + 60 * l + j:PAR["dn_conv"] + 60 * (l + 1):5] = tiled(a["dn_conv_2"][l, j])
        ba = a["w_in_2"][l][:, 3584:3600]
        for k in range(8):
            rows = ba[k * P:(k + 1) * P]
            for d in range(2):
                at = (l * 8 + k) * 72 + 32 * d
                put("ba_w", rows[:, 4 * d:4 * d + 4], at)
                put("ba_w", rows[:, 8 + 4 * d:12 + 4 * d], at + 36)
        for d in range(2):
            r = slice(32 * d, 32 * d + 4)
            p[r, PAR["A_log"] + l] = a["dn_A_log_2"][l, d]
            p[r, PAR["dn_dt"] + l] = a["dn_dt_bias_2"][l, d]
        put("dn_gain", a["dn_out_gain_2"][l][:, None], l)
        for t in range(2):
            put("qk_gain", np.concatenate([a["qk_norm_gain_2"][l, t]] * 2)[:, None], 2 * l + t)
        put("dlam", a["diff_lambda_2"][l].T, 4 * l)
        put("subln", a["diff_subln_gain_2"][l][:, None], l)
    for j in range(4):
        p[:, PAR["ssd_conv"] + j:PAR["ssd_conv"] + 120:5] = tiled(a["ssd_conv_w"][0, j])
        p[:, PAR["lru_conv"] + j:PAR["lru_conv"] + 50:5] = tiled(a["lru_conv_w"][0, j])
    p[:, PAR["ssd_conv"] + 4:PAR["ssd_conv"] + 120:5] = tiled(a["ssd_conv_b"][0])
    p[:, PAR["lru_conv"] + 4:PAR["lru_conv"] + 50:5] = tiled(a["lru_conv_b"][0])
    put("dt_w", a["ssd_w_in"][0][:, 5120:].reshape(8, P, 32).transpose(1, 0, 2).reshape(P, 256))
    put("dt_bias", a["ssd_dt_bias"][0][:, None])
    put("a_log", a["ssd_a_log"][0][:, None])
    put("ssd_d", tiled(np.repeat(a["ssd_d"][0], 64)))
    put("ssd_norm", tiled(a["ssd_norm"][0]))
    put("lru_b_in", tiled(a["lru_b_in"][0]))
    put("b_gx", tiled(a["lru_b_gx"][0]))
    put("b_ga", tiled(a["lru_b_ga"][0]))
    put("lam", tiled(a["lru_lambda"][0]))
    put("b_out", tiled(a["lru_b_out"][0]))
    put("c", tiled(a["c_2"][0]))
    return p


def stream(a):
    w = np.zeros((NCHUNK, P, CW), np.float32)

    def kind_a(at, m):
        n = m.shape[1] // 256
        w[at:at + n] = m.reshape(8, P, n, 2, P).transpose(2, 1, 3, 0, 4).reshape(n, P, CW)

    def kind_b(at, m):
        n = m.shape[0] // 256
        w[at:at + n] = m.reshape(n, 2, P, D).transpose(0, 2, 1, 3).reshape(n, P, CW)

    s = a["ssd_w_in"][0]
    kind_a(CH0["ssd_in"], s[:, 2048:5120])
    kind_a(CH0["ssd_in"] + 12, s[:, 0:2048])
    kind_b(CH0["ssd_out"], a["ssd_w_out"][0])
    kind_a(CH0["lru_in"], np.concatenate([a["lru_w_in"][0][:, 1280:], a["lru_w_in"][0][:, :1280]], axis=1))
    kind_b(CH0["lru_out"], a["lru_w_out"][0])
    for l in range(2):
        up, down = a["ffn_w_up"][l], a["ffn_w_down"][l]
        ups = np.stack([up[:, :FT * P].reshape(D, FT, P), up[:, FT * P:].reshape(D, FT, P)], axis=2).reshape(D, -1)
        spread(w, CH0[f"ffn{l}"], ups, down, kind_a, kind_b)
        m = a["w_in_2"][l]
        at = CH0[f"in2_{l}"]
        kind_a(at, m[:, 1536:3072])
        kind_a(at + 6, m[:, 0:1536])
        kind_a(at + 12, m[:, 3072:3584])
        kind_a(CH0[f"ga_{l}"], m[:, 3600:4624])
        kind_a(CH0[f"gb_{l}"], m[:, 4624:5648])
        kind_b(CH0[f"bra_{l}"], a["w_branch_a_2"][l])
        kind_b(CH0[f"brb_{l}"], a["w_branch_b_2"][l])
        kind_b(CH0[f"out2_{l}"], a["w_out_2"][l])
        mlp_chunks(w, CH0[f"mlp_{l}"], a["w_mlp1_2"][l], a["w_mlp2_2"][l], kind_a, kind_b)
    return w


def lru_gates(a):
    return np.concatenate([a[n][0].transpose(1, 0, 2).reshape(P, LT * P) for n in ("lru_w_gx", "lru_w_ga")], axis=1)


def spread(w, at, up, down, kind_a, kind_b):
    for p in range(16):
        a0 = at + (0 if p == 0 else 3 * p - 1)
        kind_a(a0, up[:, 512 * p:512 * (p + 1)])
        b0 = at + 3 * p + 4 if p < 15 else at + 47
        kind_b(b0, down[256 * p:256 * (p + 1)])


def mlp_chunks(w, at, up, down, kind_a, kind_b):
    for p in range(16):
        kind_a(at + (0 if p == 0 else 2 * p - 1), up[:, 256 * p:256 * (p + 1)])
        kind_b(at + (2 * p + 2 if p < 15 else 31), down[256 * p:256 * (p + 1)])


class Chain:

    def __init__(self, engine, sem):
        self.engine, self.sem, self.n, self.at = engine, sem, 0, None

    def __call__(self, ins):
        ins.then_inc(self.sem, 1)
        self.n += 1
        value = self.n if self.at is None else self.at[0] * self.at[1] + self.n
        self.engine.wait_ge(self.sem, value)

    def enter(self, i, per):
        self.at, self.start = (i, per), self.n

    def leave(self, turns):
        per = self.at[1]
        assert self.n - self.start == per, (self.n - self.start, per)
        self.n, self.at = self.start + per * turns, None


def build(nc, x_in, w_in, gates_in, ada_in, par_in, con_in, out):
    f32 = mybir.dt.float32
    f32r = mybir.dt.float32r
    ACT = mybir.ActivationFunctionType
    AX = mybir.AxisListType
    sems = {}
    from contextlib import ExitStack
    ctx = ExitStack()
    with ctx:
        def sb(name, shape, dtype=f32):
            return ctx.enter_context(nc.sbuf_tensor(name, shape, dtype))

        def S(name):
            if name not in sems:
                sems[name] = ctx.enter_context(nc.semaphore(name))
            return sems[name]

        raw = [sb(f"raw{i}", [P, CW]) for i in range(RAW)]
        x = sb("x", [P, DT_, T])
        h = sb("h", [P, DT_, T])
        h_hi = sb("h_hi", [P, DT_, T], f32r)
        h_lo = sb("h_lo", [P, DT_, T], f32r)
        mv_hi = sb("mv_hi", [P, 2, 2, T], f32r)
        mv_lo = sb("mv_lo", [P, 2, 2, T], f32r)
        par = sb("par", [P, NPAR])
        con = sb("con", [P, NCON])
        ada_ring = [sb(f"ada_ring{i}", [P, 8, AW]) for i in range(2)]
        ada_acc = sb("ada_acc", [P, 6 * D])
        rstd = sb("rstd", [P, T])
        tmp = sb("tmp", [P, 4, T])
        cact = sb("cact", [P, 8])
        mod2 = sb("mod", [P, 2, 48])
        gsc2 = sb("gsc", [P, 2, 16])
        keep_cols, late_cols = 10752, 10240
        keep = sb("keep", [P, keep_cols])
        with nc.sbuf_tensor("late", [P, late_cols], f32) as late:
            pass
        w_hi = [sb(f"w_hi{i}", [P, CW], f32r) for i in range(2)]
        w_lo = [sb(f"w_lo{i}", [P, CW], f32r) for i in range(2)]

        unit = [ctx.enter_context(nc.psum_tensor(f"unit{i}", [P, 512], f32)) for i in range(2)]
        misc = [ctx.enter_context(nc.psum_tensor(f"misc{i}", [P, 512], f32)) for i in range(2)]
        acc = ctx.enter_context(nc.psum_tensor("acc", [P, 4 * 512], f32))
        acc8 = acc[:, :].rearrange("p (t n) -> p t n", n=T)

        def carve(region, sizes):
            at, views = 0, {}
            for name, shape in sizes:
                n = int(np.prod(shape))
                v = region[:, at:at + n]
                if len(shape) == 2:
                    v = v.rearrange("p (a b) -> p a b", b=shape[1])
                elif len(shape) == 3:
                    v = v.rearrange("p (a b c) -> p a b c", b=shape[1], c=shape[2])
                views[name] = v
                at += n
            assert at <= (keep_cols if region is keep else late_cols), at
            return views

        def pr(name, k=0, rows=P):
            return par[0:rows, PAR[name] + k:PAR[name] + k + 1]

        def cn(name, k=0, n=P):
            return con[:, CON[name] + k:CON[name] + k + n]

        def one(name, rows=P):
            return con[0:rows, CON[name]:CON[name] + 1]

        ident, ones = cn("ident"), cn("ones")
        bank = lambda b, a, z: acc[:, 512 * b + a:512 * b + z]
        mm = nc.tensor.matmul
        act = nc.scalar.activation
        tt = nc.vector.tensor_tensor
        stt = nc.vector.scalar_tensor_tensor
        ts = nc.vector.tensor_scalar

        NORMS = ["mix_pre0", "mix_post0", "ffn_pre0", "ffn_post0", "mix_pre1", "mix_post1", "ffn_pre1",
                 "ffn_post1", "pre1_0", "pre2_0", "pre1_1", "pre2_1"]
        NI = {n: i for i, n in enumerate(NORMS)}
        XU = {"load": 0, "mix_post0": 1, "ffn_post0": 2, "mix_post1": 3, "ffn_post1": 4, "res1_0": 5,
              "res2_0": 6, "res1_1": 7, "res2_1": 8}
        HU = {"mix_pre0": 0, "ffn_pre0": 1, "mix_pre1": 2, "ffn_pre1": 3, "pre1_0": 4, "pre2_0": 5,
              "pre1_1": 6, "pre2_1": 7}

        def act_norm(ac, name, source, ready, between=None):
            n = NI[name]
            ac.preload_act_table_set(LN_EXP)
            for q in range(4):
                ready(q)
                act(h[:, 2 * q:2 * q + 2, :], source[:, 2 * q:2 * q + 2, :], ACT.Square).then_inc(S("squares"), 1)
            if between is not None:
                between()
            ac.wait_ge(S("square_sums"), n + 1)
            act(rstd[:, :], misc[0][:, 0:T], ACT.Ln, bias=one("eps"), scale=1.0 / D).then_inc(S("log_var"), 1)
            ac.wait_ge(S("log_var"), n + 1)
            act(rstd[:, :], rstd[:, :], ACT.Exp, scale=-0.5).then_inc(S("rstd_ready"), 1)

        def pe_norm(pe, name):
            n = NI[name]
            for q in range(4):
                pe.wait_ge(S("squares"), 4 * n + q + 1)
                for t in (2 * q, 2 * q + 1):
                    last = mm(misc[0][:, 0:T], ones, h[:, t, :], start=(t == 0), stop=(t == 7))
            last.then_inc(S("square_sums"), 1)

        def x_ready(eng, name):
            return lambda q: eng.wait_ge(S("x_ready"), 4 * XU[name] + q + 1)

        def dve_h(dve, name, tiles):
            u = 4 * HU[name]
            dve.wait_ge(S("rstd_ready"), NI[name] + 1)

            def low(q):
                s = slice(2 * q, 2 * q + 2)
                dve.wait_ge(S("h_hi_done"), u + q + 1)
                tt(h_lo[:, s, :], h[:, s, :], h_hi[:, s, :].bitcast(f32), ALU.subtract).then_inc(S("h_ready"), 1)

            for q in range(4):
                tiles(q).then_inc(S("h_exact"), 1)
                if q >= 1:
                    low(q - 1)
            low(3)

        def act_h(ac, name):
            u = 4 * HU[name]
            for q in range(4):
                s = slice(2 * q, 2 * q + 2)
                ac.wait_ge(S("h_exact"), u + q + 1)
                act(h_hi[:, s, :], h[:, s, :], ACT.Copy).then_inc(S("h_hi_done"), 1)

        def dve_pre(dve, name, weight):
            def tiles(q):
                for t in (2 * q, 2 * q + 1):
                    ins = stt(h[:, t, :], x[:, t, :], weight(t), rstd[:, :], ALU.mult, ALU.mult)
                return ins
            dve_h(dve, name, tiles)

        def dve_post(dve, link, name, weight, source):
            dve.wait_ge(S("rstd_ready"), NI[name] + 1)
            for q in range(4):
                s = tmp[:, 2 * (q % 2):2 * (q % 2) + 2, :]
                for k in range(2):
                    ins = stt(s[:, k, :], source[:, 2 * q + k, :], weight(2 * q + k), rstd[:, :], ALU.mult, ALU.mult)
                link(ins)
                tt(x[:, 2 * q:2 * q + 2, :], x[:, 2 * q:2 * q + 2, :], s, ALU.add).then_inc(S("x_ready"), 1)

        def dve_residual(dve, name, gate, stage):
            done_after(dve, END[stage] - 1)
            for t in range(8):
                ins = stt(x[:, t, :], acc8[:, t, :], gate(t), x[:, t, :], ALU.mult, ALU.add)
                if t % 2:
                    ins.then_inc(S("x_ready"), 1)

        LN_EXP = "natural_log_exp_and_others"

        loaded = [S(f"chunk_loaded{i}") for i in range(RAW)]
        END = {n: CH0[n] + na + nb for n, na, nb in STAGES}

        def at(i, per, n):
            return n if i is None else i * per + n

        def done_after(eng, c, i=None, chunks=0):
            eng.wait_ge(S("half_done"), at(i, 2 * chunks, 2 * c + 2))

        def half(tile, c, k):
            return tile[c % 2][:, CW // 2 * k:CW // 2 * (k + 1)]

        def act_split(ac, c, i=None, chunks=0):
            for k in range(2):
                if k == 0:
                    ac.wait_ge(loaded[c % RAW], at(i, 16 * chunks // RAW, 16 * (c // RAW + 1)))
                if i is not None or 2 * c + k - 3 > 0:
                    ac.wait_ge(S("half_done"), at(i, 2 * chunks, 2 * c + k - 3))
                act(half(w_hi, c, k), raw[c % RAW][:, CW // 2 * k:CW // 2 * (k + 1)], ACT.Copy
                    ).then_inc(S("high_parts"), 1)

        def dve_split(dve, c, i=None, chunks=0):
            for k in range(2):
                dve.wait_ge(S("high_parts"), at(i, 2 * chunks, 2 * c + k + 1))
                tt(half(w_lo, c, k), raw[c % RAW][:, CW // 2 * k:CW // 2 * (k + 1)],
                   half(w_hi, c, k).bitcast(f32), ALU.subtract).then_inc(S("chunk_split"), 1)

        def ahead(split, eng, c, i=None, chunks=0):
            if c + 2 < next(e for e in EPOCHS if e > c):
                split(eng, c + 2, i, chunks)

        def epoch(split, eng, c):
            assert c in EPOCHS
            split(eng, c)
            split(eng, c + 1)

        def three(out, w, wl, m, ml, first, last):
            mm(out, w, m, start=first, stop=False)
            mm(out, w, ml, start=False, stop=False)
            return mm(out, wl, m, start=False, stop=last)

        def pe_unit(pe, c, n, i=None, chunks=0, units=0, tokens_out=False, h_count=None):
            b = unit[n % 2]
            pe.wait_ge(S("unit_free"), at(i, units, n + 1))
            for k in range(2):
                pe.wait_ge(S("chunk_split"), at(i, 2 * chunks, 2 * c + k + 1))
                w, wl = (half(v, c, k).rearrange("p (k n) -> p k n", k=8) for v in (w_hi, w_lo))
                for m in range(2 if tokens_out else 1):
                    for j in range(8):
                        if h_count is not None and k == 0 and j % 2 == 0:
                            pe.wait_ge(S("h_ready"), h_count + j // 2 + 1)
                        if tokens_out:
                            s = slice(P * m, P * (m + 1))
                            o = b[:, T * m + P * k:T * m + P * (k + 1)]
                            ins = three(o, h_hi[:, j, s], h_lo[:, j, s], w[:, j, :], wl[:, j, :], j == 0, j == 7)
                        else:
                            ins = three(b[:, T * k:T * (k + 1)], w[:, j, :], wl[:, j, :], h_hi[:, j, :],
                                        h_lo[:, j, :], j == 0, j == 7)
                ins.then_inc(S("half_done"), 1)

        def pe_units(pe, c0, n0, count):
            with pe.Fori(0, count // 2) as i:
                for j in range(2):
                    pe_unit(pe, c0 + j, n0 + j, i, 2, 2)

        def pe_down(pe, c, b, first, last, i=None, chunks=0, downs=0):
            pe.wait_ge(S("mv_ready"), at(i, downs, b + 1))
            for k in range(2):
                pe.wait_ge(S("chunk_split"), at(i, 2 * chunks, 2 * c + k + 1))
                w, wl = (half(v, c, k).rearrange("p (t n) -> p t n", t=8) for v in (w_hi, w_lo))
                for t in range(8):
                    ins = three(acc8[:, t, :], w[:, t, :], wl[:, t, :], mv_hi[:, b % 2, k, :], mv_lo[:, b % 2, k, :],
                                first and k == 0 and t % 2 == 0, last and k == 1 and t % 2 == 1)
                ins.then_inc(S("half_done"), 1)

        def act_moving(ac, b, src, i=None, downs=0):
            act(mv_hi[:, b % 2, :, :], src, ACT.Copy).then_inc(S("mv_hi_done"), 1)

        def dve_moving(dve, b, src, i=None, downs=0):
            dve.wait_ge(S("mv_hi_done"), at(i, downs, b + 1))
            tt(mv_lo[:, b % 2, :, :], src, mv_hi[:, b % 2, :, :].bitcast(f32), ALU.subtract
               ).then_inc(S("mv_ready"), 1)

        def pe_out(pe, stage):
            n = END[stage] - CH0[stage]
            for j in range(n):
                pe_down(pe, CH0[stage] + j, B0[stage] + j, j == 0, j == n - 1)

        def act_lead(ac, stage, pair, ready=lambda j: None):
            for j in range(2):
                ready(j)
                act_moving(ac, B0[stage] + j, pair(j))

        def act_out(ac, stage, pair, ready=lambda j: None, all_ahead=True):
            n = END[stage] - CH0[stage]
            for j in range(n):
                c = CH0[stage] + j
                if j < n - 1 or all_ahead:
                    ahead(act_split, ac, c)
                    done_after(ac, c)
                if j + 2 < n:
                    ready(j + 2)
                    act_moving(ac, B0[stage] + j + 2, pair(j + 2))

        def dve_lead(dve, stage, pair):
            for j in range(2):
                dve_moving(dve, B0[stage] + j, pair(j))

        def dve_out(dve, stage, pair, make=lambda j: None):
            n = END[stage] - CH0[stage]
            for j in range(n):
                if j < n - 1:
                    ahead(dve_split, dve, CH0[stage] + j)
                if j + 2 < n:
                    make(j + 2)
                    dve_moving(dve, B0[stage] + j + 2, pair(j + 2))

        A = carve(keep, [("zs", (16, T)), ("xbc", (24, T)), ("rows", (2, T))])
        A.update(carve(late, [("xdt", (32, 64)), ("xdtd", (32, 64)), ("btok", (4, P)), ("cb", (4, P)),
                              ("e", (8, P)), ("e2", (8, P)), ("st", (32, 64)), ("tok", (5, 32))]))
        A["conv"] = tmp[:, :, :]
        A["rg"] = tmp[:, :, :]
        over = A["xdtd"].rearrange("p a b -> p (a b)")
        A["ecs"] = over[:, 0:512].rearrange("p (a b) -> p a b", b=P)
        A["yo"] = over[:, 512:1024].rearrange("p (a b) -> p a b", b=P)
        xbc, zs = A["xbc"], A["zs"]
        HR = 32
        r_cs, r_a = (A["rows"][0:HR, k, :] for k in range(2))
        r_dt, r_da, r_b, r_ncs, r_dtd, r_one = (zs[0:HR, k, :] for k in range(6))
        tokv = A["tok"]
        E2 = [A["e"], A["e2"]]

        def pe_ssd(pe):
            def group_sum(g):
                pe.wait_ge(S("ssd_sq"), g + 1)
                for k in range(4):
                    ins = mm(bank(g // 2, T * (g % 2), T * (g % 2 + 1)), ones, h[:, 4 * (g % 2) + k, :],
                             start=(k == 0 and g % 2 == 0), stop=(k == 3 and g % 2 == 1))
                ins.then_inc(S("ssd_gsum"), 1)

            def decays(n):
                c, g = n // 4, n % 4
                for half in range(2):
                    m = 2 * n + half
                    if m >= 2:
                        pe.wait_ge(S("ssd_exp"), m - 1)
                    b = unit[m % 2]
                    if m < 2:
                        pe.wait_ge(S("unit_free"), 22)
                    for k in range(4):
                        hd = 8 * g + 4 * half + k
                        mm(b[:, P * k:P * (k + 1)], ident[0:HR, hd:hd + 1].to_broadcast([HR, P]),
                           r_cs[:, P * c:P * (c + 1)], start=(k == 0), stop=False, skip_group_check=True)
                    for k in range(4):
                        ins = mm(b[:, P * k:P * (k + 1)], ident, cn("neg_up"), start=False, stop=(k == 3),
                                 skip_group_check=True)
                    ins.then_inc(S("ssd_decay_ps"), 1)

            for k in range(8):
                pe.wait_ge(S("h_exact"), k // 2 + 1)
                ins = mm(misc[1][0:HR, 0:T], par[:, PAR["dt_w"] + 32 * k:PAR["dt_w"] + 32 * (k + 1)], h[:, k, :],
                         start=(k == 0), stop=(k == 7))
            ins.then_inc(S("dt_raw"), 1)
            pe_unit(pe, CH0["ssd_in"], U0["ssd_in"], h_count=0)
            pe_unit(pe, CH0["ssd_in"] + 1, U0["ssd_in"] + 1)
            pe_units(pe, CH0["ssd_in"] + 2, U0["ssd_in"] + 2, 10)
            pe.wait_ge(S("ssd_rows"), 1)
            for n, (src, c) in enumerate(((r_dt, 0), (r_dt, 1), (r_ncs, 0), (r_ncs, 1), (r_dtd, 0))):
                ins = nc.tensor.transpose(misc[1][:, 32 * n:32 * (n + 1)], src[:, P * c:P * (c + 1)], ident[0:HR, 0:HR])
            ins.then_inc(S("ssd_tok_ps"), 1)
            pe_units(pe, CH0["ssd_in"] + 12, U0["ssd_in"] + 12, 8)
            pe.wait_ge(S("con_rest"), 16)
            pe.wait_ge(S("ssd_conv_done"), 24)
            for g in range(4):
                ins = nc.tensor.transpose(bank(0, P * g, P * (g + 1)), xbc[:, 16 + g, 0:P], ident)
            ins.then_inc(S("ssd_btok_ps"), 1)
            for c in range(2):
                for q in range(4):
                    m = 4 * c + q
                    if m >= 2:
                        pe.wait_ge(S("ssd_x_read"), m - 1)
                    if m == 0:
                        pe.wait_ge(S("ssd_btok"), 1)
                    for k in range(4):
                        ins = nc.tensor.transpose(bank(m % 2, P * k, P * (k + 1)), xbc[:, 4 * q + k, P * c:P * (c + 1)],
                                                  ident)
                    ins.then_inc(S("ssd_x_ps"), 1)
                if c == 1:
                    pe.wait_ge(S("ssd_cb"), 1)
                for g in range(4):
                    ins = mm(bank(2, P * g, P * (g + 1)), xbc[:, 16 + g, P * c:P * (c + 1)],
                             xbc[:, 20 + g, P * c:P * (c + 1)], start=True, stop=True)
                ins.then_inc(S("ssd_cb_ps"), 1)
                if c == 0:
                    for g in range(4):
                        pe.wait_ge(S("ssd_xdtd"), g + 1)
                        if g >= 1:
                            pe.wait_ge(S("ssd_state"), g)
                        mm(bank(3, 0, 512), A["btok"][:, g, :],
                           A["xdtd"].rearrange("p a b -> p (a b)")[:, 512 * g:512 * (g + 1)],
                           start=True, stop=True).then_inc(S("ssd_state_ps"), 1)
                    pe.wait_ge(S("ssd_state"), 4)
                if c == 0:
                    decays(0)
                if c == 1:
                    pe.wait_ge(S("ssd_x_read"), 8)
                for g in range(4):
                    n = 4 * c + g
                    if n + 1 < 8:
                        decays(n + 1)
                    if n >= 1:
                        pe.wait_ge(S("ssd_read"), n)
                    if c == 1:
                        for k in range(4):
                            st = A["st"].rearrange("p a b -> p (a b)")[:, 512 * g + P * k:512 * g + P * (k + 1)]
                            mm(misc[1][:, P * k:P * (k + 1)], st, xbc[:, 20 + g, P:T], start=True, stop=True)
                        if g >= 1:
                            pe.wait_ge(S("ssd_ecs"), g)
                        for k in range(4):
                            for e in range(2):
                                hd = 8 * g + 2 * k + e
                                ins = mm(bank(3, P * k, P * (k + 1))[64 * e:64 * (e + 1), :],
                                         ident[0:HR, hd:hd + 1].to_broadcast([HR, 64]), r_a[:, P:T],
                                         start=True, stop=True, skip_group_check=True)
                        ins.then_inc(S("ssd_off_ps"), 1)
                    pe.wait_ge(S("ssd_scores"), n + 1)
                    if n == 0:
                        pe.wait_ge(S("ssd_tok"), 1)
                    for hd in range(8):
                        lo = 64 * (hd % 2)
                        ins = mm(misc[0][lo:lo + 64, P * (hd // 2):P * (hd // 2) + P], A["xdt"][:, 8 * g + hd, :],
                                 E2[n % 2][:, hd, :], start=True, stop=True, skip_group_check=True)
                    ins.then_inc(S("ssd_y_ps"), 1)
                    if c == 1 and g >= 1:
                        group_sum(g - 1)
            group_sum(3)
            pe_out(pe, "ssd_out")

        def ssd_pair(j):
            return xbc[:, 2 * j:2 * j + 2, :]

        def act_ssd(ac, link):
            ac.preload_act_table_set(LN_EXP)
            ac.wait_ge(S("dt_in"), 1)
            link(act(r_a, r_dt, ACT.Abs))
            link(act(r_b, r_a, ACT.Exp, scale=-1.0))
            link(act(r_b, r_b, ACT.Ln, bias=one("one", HR)))
            act(r_one[:, 0:1], pr("a_log", 0, HR), ACT.Exp).then_inc(S("dt_log"), 1)
            ac.wait_ge(S("dt_cs"), 1)
            link(act(r_dtd, r_cs, ACT.Exp, bias=r_cs[:, P - 1:P], scale=-1.0))
            act(r_ncs, r_cs, ACT.Copy, scale=-1.0)
            act(r_a, r_cs, ACT.Exp).then_inc(S("dt_decays"), 1)
            conv = A["conv"]

            def last_tap(j):
                if j % 2 == 0:
                    ahead(act_split, ac, j // 2)
                    done_after(ac, j // 2)
                if j >= 4:
                    ac.wait_ge(S("ssd_conv_done"), j - 3)
                act(conv[:, j % 4, :], unit[(j // 2) % 2][:, T * (j % 2):T * (j % 2 + 1)], ACT.Identity,
                    bias=pr("ssd_conv", 5 * j + 4), scale=pr("ssd_conv", 5 * j + 3)).then_inc(S("ssd_tap"), 1)

            def silu(j):
                ac.wait_ge(S("ssd_taps"), j + 1)
                act(xbc[:, j, :], conv[:, j % 4, :], ACT.Silu).then_inc(S("ssd_conv_done"), 1)

            for j in range(26):
                if j < 24:
                    last_tap(j)
                if j >= 2:
                    silu(j - 2)
            ac.wait_ge(S("unit_free"), 12 + 2)
            ac.wait_ge(S("ssd_tok_ps"), 1)
            for n in range(8):
                ahead(act_split, ac, 12 + n)
                done_after(ac, 12 + n)
                act(zs[:, 2 * n:2 * n + 2, :], unit[n % 2][:, :], ACT.Silu).then_inc(S("unit_free"), 1)
            ac.wait_ge(S("ssd_btok_ps"), 1)
            act(A["btok"], bank(0, 0, 512), ACT.Copy).then_inc(S("ssd_btok"), 1)
            for g in range(4):
                ac.wait_ge(S("ssd_state_ps"), g + 1)
                act(A["st"].rearrange("p a b -> p (a b)")[:, 512 * g:512 * (g + 1)], bank(3, 0, 512),
                    ACT.Copy).then_inc(S("ssd_state"), 1)
            ac.preload_act_table_set(LN_EXP)
            ac.wait_ge(S("ssd_tok"), 1)

            def exps(n):
                c, g = n // 4, n % 4
                for half in range(2):
                    ac.wait_ge(S("ssd_decay_ps"), 2 * n + half + 1)
                    if half == 0 and n >= 2:
                        ac.wait_ge(S("ssd_y_ps"), n - 1)
                    for k in range(4):
                        hd = 4 * half + k
                        ins = act(E2[n % 2][:, hd, :], unit[half][:, P * k:P * (k + 1)], ACT.Exp,
                                  bias=tokv[:, 2 + c, 8 * g + hd:8 * g + hd + 1])
                    ins.then_inc(S("ssd_exp"), 1)

            def group_squares(g):
                ac.wait_ge(S("ssd_gated"), g + 1)
                if g >= 2:
                    ac.wait_ge(S("ssd_gsum"), g - 1)
                act(h[:, 4 * (g % 2):4 * (g % 2) + 4, :], xbc[:, 4 * g:4 * g + 4, :], ACT.Square
                    ).then_inc(S("ssd_sq"), 1)

            exps(0)
            for n in range(8):
                if n + 1 < 8:
                    exps(n + 1)
                if n >= 5:
                    group_squares(n - 5)
                if n >= 4:
                    ac.wait_ge(S("ssd_off_ps"), n - 3)
                    if n >= 5:
                        ac.wait_ge(S("ssd_read"), n)
                    act(A["ecs"], bank(3, 0, 512), ACT.Copy).then_inc(S("ssd_ecs"), 1)
            group_squares(3)
            ac.wait_ge(S("ssd_y"), 8)
            act_split(ac, CH0["ssd_out"])
            for k in range(2):
                ac.wait_ge(S("ssd_gsum"), 2 * k + 2)
                act(A["rg"][:, 2 * k:2 * k + 2, :], bank(k, 0, 512), ACT.Ln, bias=one("eps"),
                    scale=1.0 / 512).then_inc(S("ssd_glog"), 1)
            for k in range(2):
                ac.wait_ge(S("ssd_glog"), k + 1)
                act(A["rg"][:, 2 * k:2 * k + 2, :], A["rg"][:, 2 * k:2 * k + 2, :], ACT.Exp, scale=-0.5
                    ).then_inc(S("ssd_rg"), 1)
            normed = lambda j: ac.wait_ge(S("ssd_yn"), j + 1)
            act_lead(ac, "ssd_out", ssd_pair, normed)
            act_split(ac, CH0["ssd_out"] + 1)
            act_out(ac, "ssd_out", ssd_pair, normed, all_ahead=False)

        def dve_ssd(dve, link):
            dve.wait_ge(S("dt_raw"), 1)
            ts(r_dt, misc[1][0:HR, 0:T], pr("dt_bias", 0, HR), None, ALU.add).then_inc(S("dt_in"), 1)
            dve.wait_ge(S("dt_log"), 1)
            link(stt(r_dt, r_dt, 0.0, r_b, ALU.max, ALU.add))
            link(ts(r_da, r_dt, r_one[:, 0:1], -1.0, ALU.mult, ALU.mult))
            link(nc.vector.memset(r_one, 1.0))
            for c in range(2):
                s = slice(P * c, P * (c + 1))
                ins = nc.vector.tensor_tensor_scan(r_cs[:, s], r_one[:, s], r_da[:, s], 0.0, ALU.mult, ALU.add)
            ins.then_inc(S("dt_cs"), 1)
            dve.wait_ge(S("dt_decays"), 1)
            tt(r_dtd, r_dtd, r_dt, ALU.mult).then_inc(S("ssd_rows"), 1)
            conv = A["conv"]

            for n in range(12):
                ahead(dve_split, dve, n)
                dve.wait_ge(S("ssd_tap"), 2 * n + 2)
                for tap in (2, 1, 0):
                    for t in (2 * n, 2 * n + 1):
                        src = unit[n % 2][:, T * (t % 2):T * (t % 2 + 1)]
                        dst = conv[:, t % 4, 3 - tap:T]
                        ins = stt(dst, src[:, 0:T - 3 + tap], pr("ssd_conv", 5 * t + tap), dst, ALU.mult, ALU.add)
                        if tap == 0:
                            ins.then_inc(S("ssd_taps"), 1)
                    if tap != 0:
                        link(ins)
                dve.wait_ge(S("ssd_taps"), 2 * n + 2)
                dve.sem_inc(S("unit_free"), 1)
            for n in range(8):
                ahead(dve_split, dve, 12 + n)
            done_after(dve, 19)
            dve.wait_ge(S("ssd_tok_ps"), 1)
            nc.vector.tensor_copy(tokv, misc[1][:, 0:160]).then_inc(S("ssd_tok"), 1)
            dve.wait_ge(S("ssd_tok"), 1)
            for c in range(2):
                for q in range(4):
                    m = 4 * c + q
                    dve.wait_ge(S("ssd_x_ps"), m + 1)
                    if c == 1 and q == 0:
                        dve.wait_ge(S("ssd_y_ps"), 4)
                    src = bank(m % 2, 0, 512).rearrange("p (a b) -> p a b", b=64)
                    hs = slice(8 * q, 8 * q + 8)
                    if c == 0:
                        tt(A["xdtd"][:, hs, :], src, tokv[:, 4, hs].unsqueeze(2).to_broadcast([P, 8, 64]),
                           ALU.mult).then_inc(S("ssd_xdtd"), 1)
                    tt(A["xdt"][:, hs, :], src, tokv[:, c, hs].unsqueeze(2).to_broadcast([P, 8, 64]),
                       ALU.mult).then_inc(S("ssd_x_read"), 1)
                dve.wait_ge(S("ssd_cb_ps"), c + 1)
                link(nc.vector.tensor_copy(A["cb"], bank(2, 0, 512)))
                for g in range(4):
                    n = 4 * c + g
                    dve.wait_ge(S("ssd_exp"), 2 * n + 2)
                    e = E2[n % 2]
                    ins = tt(e, e, A["cb"][:, g, :].unsqueeze(1).to_broadcast([P, 8, P]), ALU.mult)
                    ins.then_inc(S("ssd_scores"), 1)
                    if c == 0 and g == 3:
                        dve.wait_ge(S("ssd_scores"), 4)
                        dve.sem_inc(S("ssd_cb"), 1)
                    s = slice(P * c, P * (c + 1))
                    if c == 1:
                        dve.wait_ge(S("ssd_ecs"), g + 1)
                        link(tt(A["yo"], misc[1][:, :].rearrange("p (a b) -> p a b", b=P), A["ecs"], ALU.mult))
                    dve.wait_ge(S("ssd_y_ps"), n + 1)
                    for k in range(4):
                        ins = stt(xbc[:, 4 * g + k, s], xbc[:, 4 * g + k, s], pr("ssd_d", 4 * g + k),
                                  misc[0][:, P * k:P * (k + 1)], ALU.mult, ALU.add)
                    ins.then_inc(S("ssd_read"), 1)
                    dve.wait_ge(S("ssd_read"), n + 1)
                    if c == 1:
                        link(tt(xbc[:, 4 * g:4 * g + 4, s], xbc[:, 4 * g:4 * g + 4, s], A["yo"], ALU.add))
                    ins = tt(xbc[:, 4 * g:4 * g + 4, s], xbc[:, 4 * g:4 * g + 4, s], zs[:, 4 * g:4 * g + 4, s], ALU.mult)
                    if c == 0:
                        ins.then_inc(S("ssd_y"), 1)
                    else:
                        link(ins)
                        dve.sem_inc(S("ssd_y"), 1)
                        dve.sem_inc(S("ssd_gated"), 1)
            dve_split(dve, CH0["ssd_out"])

            def norm(q):
                dve.wait_ge(S("ssd_rg"), q // 4 + 1)
                for j in (2 * q, 2 * q + 1):
                    ins = stt(xbc[:, j, :], xbc[:, j, :], pr("ssd_norm", j), A["rg"][:, j // 4, :], ALU.mult, ALU.mult)
                ins.then_inc(S("ssd_yn"), 1)

            norm(0)
            norm(1)
            dve.wait_ge(S("ssd_yn"), 2)
            dve_lead(dve, "ssd_out", ssd_pair)
            dve_split(dve, CH0["ssd_out"] + 1)

            def next_norm(q):
                norm(q)
                dve.wait_ge(S("ssd_yn"), q + 1)

            dve_out(dve, "ssd_out", ssd_pair, next_norm)

        F = carve(keep, [("fc", (2, 2 * T)), ("fg", (2, T)), ("hid", (2, T))])

        def pe_ffn(pe, l):
            c0, n0, b0 = CH0[f"ffn{l}"], U0[f"ffn{l}"], B0[f"ffn{l}"]
            pe_unit(pe, c0, n0, h_count=4 * HU[f"ffn_pre{l}"])
            pe_unit(pe, c0 + 1, n0 + 1)
            for j in range(2):
                pe_unit(pe, c0 + 2 + j, n0 + 2 + j)
            pe_down(pe, c0 + 4, b0, True, False)
            with pe.Fori(0, 7) as i:
                for k in range(2):
                    for j in range(2):
                        pe_unit(pe, c0 + 5 + 3 * k + j, n0 + 4 + 2 * k + j, i, 6, 4)
                    pe_down(pe, c0 + 7 + 3 * k, b0 + 1 + k, False, False, i, 6, 2)
            pe_down(pe, c0 + 47, b0 + 15, False, True)

        def act_ffn(ac, l):
            c0, b0, f0 = CH0[f"ffn{l}"], B0[f"ffn{l}"], 32 * l
            off = PAR["ffn_conv"] + l * FT * 8

            def column(u, k, i):
                return par[:, off + 8 * u + k:off + 8 * u + k + 1] if i is None else \
                    par[:, bass.ds(i * 32 + (off + 8 * u + k), 1)]

            def last_tap(u, c, i):
                done_after(ac, c, i, 6)
                if i is not None or u >= 2:
                    ac.wait_ge(S("ffn_product"), at(i, 4, f0 + u - 1))
                fc = F["fc"][:, u % 2, :]
                for side in range(2):
                    s = slice(T * side, T * (side + 1))
                    ins = act(fc[:, s], unit[u % 2][:, s], ACT.Identity, bias=column(u, 4 * side + 3, i),
                              scale=column(u, 4 * side + 2, i))
                ins.then_inc(S("ffn_tap"), 1)

            def gelu(u, i):
                ac.wait_ge(S("ffn_taps"), at(i, 4, f0 + u + 1))
                act(F["fg"][:, u % 2, :], F["fc"][:, u % 2, 0:T], ACT.Gelu_apprx_tanh).then_inc(S("ffn_gelu"), 1)

            def moving(p, i=None):
                ac.wait_ge(S("ffn_product"), at(i, 4, f0 + 2 * p + 2))
                act_moving(ac, b0 + p, F["hid"])

            def pair(p, i=None):
                c = c0 + max(3 * p - 1, 0)
                ahead(act_split, ac, c, i, 6)
                if p >= 1:
                    moving(p - 1, i)
                last_tap(2 * p, c, i)
                ahead(act_split, ac, c + 1, i, 6)
                gelu(2 * p, i)
                last_tap(2 * p + 1, c + 1, i)
                if p >= 1:
                    ahead(act_split, ac, c + 2, i, 6)
                gelu(2 * p + 1, i)

            pair(0)
            pair(1)
            with ac.Fori(0, 7) as i:
                for p in (2, 3):
                    pair(p, i)
            moving(15)

        def dve_ffn(dve, l, link):
            c0, b0, f0 = CH0[f"ffn{l}"], B0[f"ffn{l}"], 32 * l
            off = PAR["ffn_conv"] + l * FT * 8
            dve.wait_ge(S("unit_free"), U0[f"ffn{l}"] + 2)

            def column(u, k, i):
                return par[:, off + 8 * u + k:off + 8 * u + k + 1] if i is None else \
                    par[:, bass.ds(i * 32 + (off + 8 * u + k), 1)]

            def taps(u, i):
                dve.wait_ge(S("ffn_tap"), at(i, 4, f0 + u + 1))
                fc, src = F["fc"][:, u % 2, :], unit[u % 2]
                for side in range(2):
                    o = T * side
                    ins = stt(fc[:, o + 1:o + T], src[:, o:o + T - 1], column(u, 4 * side + 1, i),
                              fc[:, o + 1:o + T], ALU.mult, ALU.add)
                link(ins)
                for side in range(2):
                    o = T * side
                    ins = stt(fc[:, o + 2:o + T], src[:, o:o + T - 2], column(u, 4 * side, i),
                              fc[:, o + 2:o + T], ALU.mult, ALU.add)
                ins.then_inc(S("ffn_taps"), 1)
                dve.wait_ge(S("ffn_taps"), at(i, 4, f0 + u + 1))
                dve.sem_inc(S("unit_free"), 1)

            def product(u, i):
                if i is not None or u >= 2:
                    dve.wait_ge(S("mv_ready"), at(i, 2, b0 + u // 2))
                dve.wait_ge(S("ffn_gelu"), at(i, 4, f0 + u + 1))
                tt(F["hid"][:, u % 2, :], F["fg"][:, u % 2, :], F["fc"][:, u % 2, T:2 * T], ALU.mult
                   ).then_inc(S("ffn_product"), 1)

            def moving(p, i=None):
                dve.wait_ge(S("ffn_product"), at(i, 4, f0 + 2 * p + 2))
                dve_moving(dve, b0 + p, F["hid"], i, 2)

            def pair(p, i=None):
                c = c0 + max(3 * p - 1, 0)
                ahead(dve_split, dve, c, i, 6)
                if p >= 1:
                    moving(p - 1, i)
                taps(2 * p, i)
                ahead(dve_split, dve, c + 1, i, 6)
                taps(2 * p + 1, i)
                product(2 * p, i)
                if p >= 1:
                    ahead(dve_split, dve, c + 2, i, 6)
                product(2 * p + 1, i)

            pair(0)
            pair(1)
            with dve.Fori(0, 7) as i:
                link.enter(i, 4)
                for p in (2, 3):
                    pair(p, i)
                link.leave(7)
            moving(15)

        def pe_mod(pe, l):
            pe.wait_ge(S("ada_step"), 4 * ADA_N * (l + 1))
            for j in range(48):
                ins = mm(misc[1][:, j:j + 1], ada_acc[:, P * j:P * (j + 1)], ones[:, 0:1], start=True, stop=True)
            ins.then_inc(S("mod_ps"), 1)

        def dve_mod(dve, link, l):
            mod, gsc = mod2[:, l, :], gsc2[:, l, :]
            dve.wait_ge(S("mod_ps"), l + 1)
            link(tt(mod, misc[1][:, 0:48], par[:, PAR["ada_b"] + 48 * l:PAR["ada_b"] + 48 * (l + 1)], ALU.add))
            for k, name in enumerate(("n1", "n2")):
                w = par[:, PAR[name] + 8 * l:PAR[name] + 8 * (l + 1)]
                ins = stt(gsc[:, 8 * k:8 * (k + 1)], mod[:, 24 * k + 8:24 * k + 16], 1.0, w, ALU.add, ALU.mult)
            link(ins)
            dve.sem_inc(S("mod_done"), 1)

        R = carve(keep, [("xb", (LT, T)), ("yb", (LT, T)), ("pj", (4, T)), ("cv", (4, LT)),
                         ("gates", (2, LT, P)), ("ga89", (2, T)), ("gx", (3, T))])
        gates_flat = R["gates"].rearrange("p g h n -> p (g h n)")
        lg = gates_flat.rearrange("p (a b) -> p a b", b=T)
        R["m"] = lg[:, 0:8, :]
        cv = [R["cv"][:, k, :] for k in range(4)]
        split_cols = 4 * CW
        w8 = late[:, split_cols:split_cols + 8 * T].rearrange("p (a b) -> p a b", b=T)

        def w_(j, n=1):
            return w8[:, j:j + n, :] if j < 8 else R["pj"][:, j - 8:j - 8 + n, :]

        def ga_(j, n=1):
            return h[:, j:j + n, :] if j < 8 else R["ga89"][:, j - 8:j - 8 + n, :]

        def pe_lru(pe):
            c0, n0 = CH0["lru_in"], U0["lru_in"]

            def gates(j):
                pe.wait_ge(S("lru_conv"), j + 1)
                if j >= 2:
                    pe.wait_ge(S("lru_gate_read"), j - 1)
                for g in range(2):
                    ins = mm(misc[j % 2][:, T * g:T * (g + 1)], R["gates"][:, g, j, :], R["xb"][:, j, :],
                             start=(g == 0), stop=(g == 1))
                ins.then_inc(S("lru_gate_ps"), 1)

            pe_unit(pe, c0, n0, h_count=4 * HU["mix_pre1"])
            for j in range(1, 5):
                pe_unit(pe, c0 + j, n0 + j)
            pe.wait_ge(S("gates_loaded"), 16)
            for k in range(5):
                gates(2 * k)
                gates(2 * k + 1)
                pe_unit(pe, c0 + 5 + k, n0 + 5 + k)
            pe.wait_ge(S("lru_gate_read"), LT)
            pe_mod(pe, 0)
            pe_out(pe, "lru_out")

        def lru_pair(j):
            return R["yb"][:, 2 * j:2 * j + 2, :]

        def act_lru(ac, link):
            ac.dma_start(gates_flat, gates_in).then_inc(S("gates_loaded"), 16)
            ac.preload_act_table_set(LN_EXP)
            lam = par[:, PAR["lam"]:PAR["lam"] + LT]
            link(act(cv[0], lam, ACT.Abs))
            link(act(cv[1], cv[0], ACT.Exp, scale=-1.0))
            act(cv[1], cv[1], ACT.Ln, bias=one("one")).then_inc(S("lam_log"), 1)
            ac.preload_act_table(ACT.Sigmoid)
            c0, n0 = CH0["lru_in"], U0["lru_in"]
            ac.wait_ge(S("unit_free"), n0 + 2)
            for n in range(5):
                done_after(ac, c0 + n)
                for k in range(2):
                    j = 2 * n + k
                    if j >= 4:
                        ac.wait_ge(S("lru_conv"), j - 3)
                    act(R["pj"][:, j % 4, :], unit[n % 2][:, T * k:T * (k + 1)], ACT.Identity,
                        bias=pr("lru_b_in", LT + j)).then_inc(S("lru_proj"), 1)
                ac.wait_ge(S("lru_proj"), 2 * n + 2)
                ac.sem_inc(S("unit_free"), 1)
                ahead(act_split, ac, c0 + n)
            ac.wait_ge(S("lam_done"), 1)
            for k in range(5):
                for j in (2 * k, 2 * k + 1):
                    ac.wait_ge(S("lru_gate_ps"), j + 1)
                    if j >= 3:
                        ac.wait_ge(S("lru_gated"), j - 2)
                    act(R["gx"][:, j % 3, :], misc[j % 2][:, 0:T], ACT.Sigmoid, bias=pr("b_gx", j))
                    act(ga_(j)[:, 0, :], misc[j % 2][:, T:2 * T], ACT.Sigmoid,
                        bias=pr("b_ga", j)).then_inc(S("lru_gate_read"), 1)
                ac.wait_ge(S("lru_gate_read"), 2 * k + 2)
                for j in (2 * k, 2 * k + 1):
                    ins = act(w_(j)[:, 0, :], ga_(j)[:, 0, :], ACT.Tanh, scale=cv[3][:, j:j + 1])
                ins.then_inc(S("lru_tanh"), 1)
                if k < 4:
                    ahead(act_split, ac, c0 + 5 + k)
                    done_after(ac, c0 + 5 + k)
                    for e in range(2):
                        ins = act(R["yb"][:, 2 * k + e, :], unit[(k + 1) % 2][:, T * e:T * (e + 1)], ACT.Identity,
                                  bias=pr("lru_b_in", 2 * k + e))
                    ins.then_inc(S("unit_free"), 1)
            ac.wait_ge(S("unit_free"), n0 + 11)
            act(R["yb"][:, 0:8, :], R["yb"][:, 0:8, :], ACT.Gelu_apprx_tanh).then_inc(S("lru_gelu"), 1)
            ac.preload_act_table_set(LN_EXP)

            def mult(q):
                ac.wait_ge(S("lru_diff"), q + 1)
                act(lg[:, 2 * q:2 * q + 2, :], lg[:, 2 * q:2 * q + 2, :], ACT.Exp, scale=0.5).then_inc(S("lru_mult"), 1)

            for q in range(5):
                w = w_(2 * q, 2)
                ac.wait_ge(S("lru_tanh"), q + 1)
                link(act(lg[:, 2 * q:2 * q + 2, :], w, ACT.Ln, scale=-2.0, bias=one("tiny")))
                act(w, w, ACT.Ln, scale=-1.0, bias=one("one")).then_inc(S("lru_logs"), 1)
                for j in (2 * q, 2 * q + 1):
                    ins = act(ga_(j)[:, 0, :], ga_(j)[:, 0, :], ACT.Exp, scale=cv[3][:, j:j + 1])
                ins.then_inc(S("lru_a"), 1)
                if q >= 1:
                    mult(q - 1)
                if q == 1:
                    ahead(act_split, ac, c0 + 9)
            mult(4)
            done_after(ac, c0 + 9)
            for e in range(2):
                ins = act(R["yb"][:, 8 + e, :], unit[1][:, T * e:T * (e + 1)], ACT.Gelu_apprx_tanh,
                          bias=pr("lru_b_in", 8 + e))
            ins.then_inc(S("unit_free"), 1)
            made = lambda j: ac.wait_ge(S("lru_out_ready"), j + 1)
            act_lead(ac, "lru_out", lru_pair, made)
            act_out(ac, "lru_out", lru_pair, made)

        def dve_lru(dve, link):
            c0, n0 = CH0["lru_in"], U0["lru_in"]
            lam = par[:, PAR["lam"]:PAR["lam"] + LT]
            dve.wait_ge(S("lam_log"), 1)
            link(ts(cv[2], lam, -1.0, 0.0, ALU.mult, ALU.max))
            link(tt(cv[3], cv[2], cv[1], ALU.add))
            ts(cv[3], cv[3], -8.0, None, ALU.mult).then_inc(S("lam_done"), 1)
            for j in range(LT):
                dve.wait_ge(S("lru_proj"), j + 1)
                src, dst = R["pj"][:, j % 4, :], R["xb"][:, j, :]
                w = lambda k: pr("lru_conv", 5 * j + k)
                link(ts(dst, src, w(3), w(4), ALU.mult, ALU.add))
                link(stt(dst[:, 1:T], src[:, 0:T - 1], w(2), dst[:, 1:T], ALU.mult, ALU.add))
                link(stt(dst[:, 2:T], src[:, 0:T - 2], w(1), dst[:, 2:T], ALU.mult, ALU.add))
                stt(dst[:, 3:T], src[:, 0:T - 3], w(0), dst[:, 3:T], ALU.mult, ALU.add).then_inc(S("lru_conv"), 1)
                if j % 2:
                    ahead(dve_split, dve, c0 + j // 2)
            for k in range(5):
                for j in (2 * k, 2 * k + 1):
                    dve.wait_ge(S("lru_gate_read"), j + 1)
                    tt(R["xb"][:, j, :], R["gx"][:, j % 3, :], R["xb"][:, j, :], ALU.mult).then_inc(S("lru_gated"), 1)
                if k < 4:
                    ahead(dve_split, dve, c0 + 5 + k)
            dve.wait_ge(S("lru_gated"), LT)

            def diff(q):
                s = lg[:, 2 * q:2 * q + 2, :]
                dve.wait_ge(S("lru_logs"), q + 1)
                tt(s, s, w_(2 * q, 2), ALU.subtract).then_inc(S("lru_diff"), 1)

            def recur(q):
                s = slice(2 * q, 2 * q + 2)
                dve.wait_ge(S("lru_mult"), q + 1)
                dve.wait_ge(S("lru_a"), q + 1)
                link(tt(R["xb"][:, s, :], lg[:, s, :], R["xb"][:, s, :], ALU.mult))
                for j in (2 * q, 2 * q + 1):
                    ins = nc.vector.tensor_tensor_scan(w_(j)[:, 0, :], ga_(j)[:, 0, :], R["xb"][:, j, :], 0.0,
                                                       ALU.mult, ALU.add)
                link(ins)
                if q < 4:
                    dve.wait_ge(S("lru_gelu"), 1)
                else:
                    dve.wait_ge(S("unit_free"), n0 + 12)
                tt(R["yb"][:, s, :], w_(2 * q, 2), R["yb"][:, s, :], ALU.mult).then_inc(S("lru_out_ready"), 1)
                dve.wait_ge(S("lru_out_ready"), q + 1)

            diff(0)
            diff(1)
            ahead(dve_split, dve, c0 + 9)
            recur(0)
            diff(2)
            recur(1)
            diff(3)
            diff(4)
            dve_lead(dve, "lru_out", lru_pair)
            dve_out(dve, "lru_out", lru_pair, recur)
            done_after(dve, END["lru_out"] - 1)
            for t in range(8):
                ins = ts(R["m"][:, t, :], acc8[:, t, :], pr("b_out", t), None, ALU.add)
                if t % 2:
                    ins.then_inc(S("lru_m"), 1)
            ahead(dve_split, dve, END["lru_out"] - 1)

        def ada_chunk(pool, s, l, i=None):
            a = ada_ring[s]
            base = 4 * ADA_N * l + 4 * s
            i = ADA_N // 2 - 1 if i is None else i
            pool.wait_ge(S(f"ada_loaded{s}"), i * 16 + (16 * (ADA_N // 2) * l + 16))
            nc.gpsimd.tensor_tensor(a[:, :, :], a[:, :, :], cact[:, :].unsqueeze(2).to_broadcast([P, 8, AW]),
                                    ALU.mult).then_inc(S("ada_step"), 1)
            for k, n in enumerate((4, 2)):
                pool.wait_ge(S("ada_step"), i * 8 + (base + k + 1))
                nc.gpsimd.tensor_tensor(a[:, 0:n, :], a[:, 0:n, :], a[:, n:2 * n, :],
                                        ALU.add).then_inc(S("ada_step"), 1)
            pool.wait_ge(S("ada_step"), i * 8 + (base + 3))
            nc.gpsimd.tensor_tensor(ada_acc[:, bass.ds(i * (2 * AW) + AW * s, AW)], a[:, 0, :], a[:, 1, :],
                                    ALU.add).then_inc(S("ada_step"), 1)
            pool.wait_ge(S("ada_step"), i * 8 + (base + 4))

        def ada_load(pool, s, chunk):
            src = ada_in[chunk] if isinstance(chunk, int) else \
                ada_in[bass.ds(chunk, 1)].rearrange("o p k n -> p (o k) n")
            pool.dma_start(ada_ring[s][:, :, :], src).then_inc(S(f"ada_loaded{s}"), 16)

        def pool_ada(pool):
            pool.wait_ge(S("c_act"), 1)
            for s in range(2):
                ada_load(pool, s, s)
            with pool.Fori(0, ADA_N // 2) as i:
                for s in range(2):
                    ada_chunk(pool, s, 0, i)
                    ada_load(pool, s, i * 2 + (2 + s))
            pool.wait_ge(S("mod_ps"), 1)
            with pool.Fori(0, ADA_N // 2 - 1) as i:
                for s in range(2):
                    ada_chunk(pool, s, 1, i)
                    ada_load(pool, s, i * 2 + (ADA_N + 2 + s))
            for s in range(2):
                ada_chunk(pool, s, 1)

        B = carve(keep, [("qk", (8, T)), ("vt", (2, 512)), ("z", (4, T)), ("dn", (12, T)), ("ya", (4, T)),
                         ("rows", (7, T)), ("tok", (8, 36)), ("lam", (8,))])
        HB = (4, P)
        W = carve(late, [("kt", (2, 4, P)), ("vt", (2, 4, P)), ("dt", (2, 4, P)), ("lt", (2, 4, P)),
                         ("t", (2, 4, P)), ("u", (2, 4, P)), ("qk", (2, 4, P)), ("vb", (2, 4, P)),
                         ("kbg", HB), ("kd", HB), ("qd", HB), ("s", HB)])
        W["w"] = W["kbg"]
        rot = late[:, split_cols:split_cols + 8 * T].rearrange("p (a b) -> p a b", b=T)
        W2 = carve(late, [("sq", (4, T)), ("e", (2, 2, T)), ("a", (2, T)), ("at", (2, T)),
                          ("st", (8, 8))])
        lam8 = B["lam"]
        gate = keep[:, 0:16 * T].rearrange("p (a b) -> p a b", b=T)
        merged = B["dn"][:, 4:12, :]
        dconv = tmp
        R36 = 36
        RB, RG, RE, RBG, RNG, RKD, RX = (B["rows"][0:R36, k, :] for k in range(7))
        tokd = B["tok"]
        dn = B["dn"]
        dq, dk, dv = dn[:, 0:4, :], dn[:, 4:8, :], dn[:, 8:12, :]
        l2 = W["t"].rearrange("p c h n -> p (c h n)")
        flat = lambda v: v.rearrange("p a b -> p (a b)")
        oacc = acc8[:, 4:8, :]

        def first_second(d):
            return (0, 1) if d == 0 else (1, 0)

        def pe_b2_in(pe, l):
            pe_norm(pe, f"pre1_{l}")
            c0, n0 = CH0[f"in2_{l}"], U0[f"in2_{l}"]
            pe.wait_ge(S("mod_done"), l + 1)
            for g in range(2):
                for k in range(8):
                    at = PAR["ba_w"] + (8 * l + k) * 72 + 36 * g
                    if g == 0:
                        pe.wait_ge(S("h_exact"), 4 * HU[f"pre1_{l}"] + k // 2 + 1)
                    ins = mm(misc[1][0:R36, T * g:T * (g + 1)], par[:, at:at + 36], h[:, k, :],
                             start=(k == 0), stop=(k == 7))
            ins.then_inc(S("ba_ps"), 1)
            pe_unit(pe, c0, n0, h_count=4 * HU[f"pre1_{l}"])
            pe_unit(pe, c0 + 1, n0 + 1)
            pe_units(pe, c0 + 2, n0 + 2, 6)
            pe.wait_ge(S("dn_sq"), 2 * l + 2)
            for k in range(8):
                ins = mm(acc8[:, k, :], ones, h[:, k, :], start=(k % 2 == 0), stop=(k % 2 == 1))
            ins.then_inc(S("dn_ssum"), 1)
            pe_unit(pe, c0 + 8, n0 + 8)
            pe_unit(pe, c0 + 9, n0 + 9)
            for j in range(10, 14):
                pe_unit(pe, c0 + j, n0 + j, tokens_out=(j < 12))
                if j == 10:
                    pe.wait_ge(S("at_sq"), 2 * l + 2)
                    for k in range(8):
                        ins = mm(acc8[:, k, :], cn("half_ones"), h[:, k, :], start=(k % 2 == 0), stop=(k % 2 == 1))
                    ins.then_inc(S("at_ssum"), 1)
                if j == 11:
                    pe.wait_ge(S("at_lam_in"), l + 1)
                    mm(misc[1][:, 0:2], ones[0:64, :], lam8[0:64, 0:2], start=True, stop=True
                       ).then_inc(S("at_lam_ps"), 1)
                if j == 12:
                    pe.wait_ge(S("at_unit"), l + 1)
                    for k in range(8):
                        ins = mm(acc8[:, k, :], cn("rope"), B["qk"][:, k, :], start=(k % 2 == 0), stop=(k % 2 == 1))
                    ins.then_inc(S("at_rot_ps"), 1)

        def act_unit(ac, link, sums, l, ready, scale):
            ac.wait_ge(S(sums), l + 1)
            for k in range(2):
                link(act(flat(h[:, 4 * k:4 * k + 4, :]), acc[:, 1024 * k:1024 * (k + 1)], ACT.Ln, bias=one("eps"),
                         scale=scale))
            for k in range(2):
                s = h[:, 4 * k:4 * k + 4, :]
                act(s, s, ACT.Exp, scale=-0.5).then_inc(S(ready), 1)

        def act_b2_in(ac, l, link):
            act_norm(ac, f"pre1_{l}", x, x_ready(ac, "ffn_post1" if l == 0 else "res2_0"))
            act_h(ac, f"pre1_{l}")
            c0, n0 = CH0[f"in2_{l}"], U0[f"in2_{l}"]

            def centre(j):
                if j >= 4:
                    ac.wait_ge(S("dn_conv"), 12 * l + j - 3)
                if j % 2 == 0:
                    ahead(act_split, ac, c0 + j // 2)
                    done_after(ac, c0 + j // 2)
                act(dconv[:, j % 4, :], unit[(j // 2) % 2][:, T * (j % 2):T * (j % 2 + 1)], ACT.Identity,
                    bias=one("zero"), scale=pr("dn_conv", 60 * l + 5 * j + 2)).then_inc(S("dn_tap"), 1)

            centre(0)
            centre(1)
            for j in range(12):
                if j + 2 < 12:
                    centre(j + 2)
                ac.wait_ge(S("dn_taps"), 12 * l + j + 1)
                act(dn[:, j, :], dconv[:, j % 4, :], ACT.Silu).then_inc(S("dn_conv"), 1)
            ac.wait_ge(S("unit_free"), n0 + 6 + 2)
            for j in range(6, 14):
                if j == 7:
                    ac.wait_ge(S("ba_ps"), l + 1)
                    ac.wait_ge(S("dn_conv"), 12 * l + 12)
                    for k in range(2):
                        act(h[:, 4 * k:4 * k + 4, :], dn[:, 4 * k:4 * k + 4, :], ACT.Square).then_inc(S("dn_sq"), 1)
                    ac.preload_act_table(ACT.Sigmoid)
                    ac.wait_ge(S("a_in"), l + 1)
                    act(RB, misc[1][0:R36, 0:T], ACT.Sigmoid).then_inc(S("beta"), 1)
                    ac.preload_act_table_set(LN_EXP)
                    link(act(RE, RX, ACT.Abs))
                    link(act(RE, RE, ACT.Exp, scale=-1.0))
                    link(act(RE, RE, ACT.Ln, bias=one("one", R36)))
                    act(RG[:, 0:1], pr("A_log", l, R36), ACT.Exp).then_inc(S("a_log_done"), 1)
                    ac.wait_ge(S("g_sum"), l + 1)
                    act(RE, RG, ACT.Exp)
                    act(RNG, RG, ACT.Copy, scale=-1.0)
                    for c in range(2):
                        s = slice(P * c, P * (c + 1))
                        act(RKD[0:32, s], RG[0:32, s], ACT.Exp, bias=RG[0:32, P * c + P - 1:P * c + P], scale=-1.0)
                        ins = act(RKD[32:R36, s], RG[32:R36, s], ACT.Exp, bias=RG[32:R36, P * c:P * c + 1], scale=-1.0)
                    ins.then_inc(S("g_exps"), 1)
                if j == 8:
                    act_unit(ac, link, "dn_ssum", l, "dn_rnorm", 1.0)
                if j == 10:
                    ac.wait_ge(S("unit_free"), n0 + 10 + 2)
                    ac.wait_ge(S("dn_unit"), l + 1)
                    for k in range(2):
                        act(h[:, 4 * k:4 * k + 4, :], B["qk"][:, 4 * k:4 * k + 4, :], ACT.Square
                            ).then_inc(S("at_sq"), 1)
                if j == 13:
                    ac.wait_ge(S("at_lam_ps"), l + 1)
                    act(lam8[:, 2:4], misc[1][:, 0:2], ACT.Exp).then_inc(S("at_lam_exp"), 1)
                if j == 11:
                    act_unit(ac, link, "at_ssum", l, "at_rnorm", 1.0 / 64)
                ahead(act_split, ac, c0 + j)
                done_after(ac, c0 + j)
                u = unit[(n0 + j) % 2]
                if j < 10:
                    ins = act(B["qk"][:, 2 * (j - 6):2 * (j - 6) + 2, :], u[:, :], ACT.Copy)
                elif j < 12:
                    ins = act(B["vt"][:, :, T * (j - 10):T * (j - 9)], u[:, :].rearrange("p (a b) -> p a b", b=T), ACT.Copy)
                else:
                    ins = act(B["z"][:, 2 * (j - 12):2 * (j - 12) + 2, :], u[:, :], ACT.Silu)
                ins.then_inc(S("unit_free"), 1)

        def dve_b2_in(dve, l, link):
            dve_modulated(dve, link, f"pre1_{l}", l, 0)
            dve.wait_ge(S("unit_free"), U0[f"in2_{l}"] + 2)
            for n in range(6):
                ahead(dve_split, dve, CH0[f"in2_{l}"] + n)
                dve.wait_ge(S("dn_tap"), 12 * l + 2 * n + 2)
                for tap, (a, b), (c, e) in ((1, (0, T - 1), (1, T)), (0, (0, T - 2), (2, T)),
                                            (3, (1, T), (0, T - 1)), (4, (2, T), (0, T - 2))):
                    for t in (2 * n, 2 * n + 1):
                        src = unit[n % 2][:, T * (t % 2):T * (t % 2 + 1)]
                        dst = dconv[:, t % 4, c:e]
                        ins = stt(dst, src[:, a:b], pr("dn_conv", 60 * l + 5 * t + tap), dst, ALU.mult, ALU.add)
                        if tap == 4:
                            ins.then_inc(S("dn_taps"), 1)
                    if tap != 4:
                        link(ins)
                dve.wait_ge(S("dn_taps"), 12 * l + 2 * n + 2)
                dve.sem_inc(S("unit_free"), 1)
            ahead(dve_split, dve, CH0[f"in2_{l}"] + 6)
            dl = par[0:64, PAR["dlam"] + 4 * l:PAR["dlam"] + 4 * l + 4].rearrange("p (a b) -> p a b", b=2)
            tt(lam8[0:64, 0:2], dl[:, :, 0], dl[:, :, 1], ALU.mult).then_inc(S("at_lam_in"), 1)
            dve.wait_ge(S("ba_ps"), l + 1)
            ts(RX, misc[1][0:R36, T:2 * T], pr("dn_dt", l, R36), None, ALU.add).then_inc(S("a_in"), 1)
            dve.wait_ge(S("a_log_done"), l + 1)
            link(stt(RX, RX, 0.0, RE, ALU.max, ALU.add))
            link(ts(RX, RX, RG[:, 0:1], -1.0, ALU.mult, ALU.mult))
            link(nc.vector.memset(RKD, 1.0))
            for c in range(2):
                a, z = P * c, P * (c + 1)
                nc.vector.tensor_tensor_scan(RG[0:32, a:z], RKD[0:32, a:z], RX[0:32, a:z], 0.0, ALU.mult, ALU.add)
                back = lambda v: v[32:R36, a:z][:, ::-1]
                ins = nc.vector.tensor_tensor_scan(back(RG), back(RKD), back(RX), 0.0, ALU.mult, ALU.add)
            ins.then_inc(S("g_sum"), 1)
            dve.wait_ge(S("beta"), l + 1)
            dve.wait_ge(S("g_exps"), l + 1)
            tt(RBG, RB, RE, ALU.mult).then_inc(S("dn_rows"), 1)
            for j in range(7, 14):
                ahead(dve_split, dve, CH0[f"in2_{l}"] + j)
                for at_j, name, v, g in ((8, "dn", dn, lambda k: P ** -0.5 if k == 0 else 1.0),
                                         (11, "at", B["qk"], lambda k: pr("qk_gain", 2 * l + k))):
                    if j == at_j:
                        for k in range(2):
                            s = slice(4 * k, 4 * k + 4)
                            dve.wait_ge(S(f"{name}_rnorm"), 2 * l + k + 1)
                            link(stt(v[:, s, :], v[:, s, :], g(k), h[:, s, :], ALU.mult, ALU.mult))
                        dve.sem_inc(S(f"{name}_unit"), 1)
            dve.wait_ge(S("at_rot_ps"), l + 1)
            wide = lambda name: cn(name, 0, T).unsqueeze(1).to_broadcast([P, 8, T])
            tt(rot, acc8[:, :, :], wide("sin"), ALU.mult)
            link(tt(B["qk"], B["qk"], wide("cos"), ALU.mult))
            tt(B["qk"], B["qk"], rot, ALU.add).then_inc(S("at_rope"), 1)
            dve.wait_ge(S("at_lam_exp"), l + 1)
            link(tt(lam8[:, 4:5], lam8[:, 3:4], lam8[:, 2:3], ALU.subtract))
            ts(lam8[:, 5:6], lam8[:, 4:5], -lambda_init(l), None, ALU.add)
            ts(lam8[:, 6:7], pr("subln", l), 1.0 - lambda_init(l), None, ALU.mult).then_inc(S("at_lam"), 1)

        def dve_modulated(dve, link, name, l, k0):
            mod, gsc = mod2[:, l, :], gsc2[:, l, :]

            def tiles(q):
                s = tmp[:, 2 * (q % 2):2 * (q % 2) + 2, :]
                for k in range(2):
                    t = 2 * q + k
                    ins = stt(s[:, k, :], x[:, t, :], gsc[:, 8 * k0 + t:8 * k0 + t + 1], rstd[:, :], ALU.mult, ALU.mult)
                link(ins)
                for k in range(2):
                    t = 2 * q + k
                    ins = ts(h[:, t, :], s[:, k, :], mod[:, 24 * k0 + t:24 * k0 + t + 1], None, ALU.add)
                return ins
            dve_h(dve, name, tiles)

        def heads(b):
            return b.rearrange("p (h n) -> p h n", n=P)

        def pe_delta(pe, l):
            pe.wait_ge(S("at_lam_exp"), l + 1)
            pe.wait_ge(S("dn_rows"), l + 1)
            for c in range(2):
                for k, r in enumerate((RB, RNG, RBG, RKD)):
                    at = 36 * (4 * c + k)
                    ins = nc.tensor.transpose(misc[1][:, at:at + 36], r[:, P * c:P * (c + 1)], ident[0:R36, 0:R36])
            ins.then_inc(S("dn_tok_ps"), 1)
            pe.wait_ge(S("unit_free"), U0[f"in2_{l}"] + 14 + 2)
            pe.wait_ge(S("dn_unit"), l + 1)
            for c in range(2):
                for hd in range(4):
                    ins = nc.tensor.transpose(unit[c][:, P * hd:P * (hd + 1)], dk[:, hd, P * c:P * (c + 1)], ident)
                ins.then_inc(S("dn_kt_ps"), 1)
            pe.wait_ge(S("dn_tok"), l + 1)
            for c in range(2):
                for hd in range(4):
                    ins = nc.tensor.transpose(misc[c][:, P * hd:P * (hd + 1)], dv[:, hd, P * c:P * (c + 1)], ident)
                ins.then_inc(S("dn_vt_ps"), 1)
            pe.wait_ge(S("dn_kt"), 2 * l + 2)
            pe.wait_ge(S("dn_vt"), 2 * l + 2)
            for d in range(2):
                n = 2 * l + d
                row = lambda r, hd: (ident[0:R36, 32 * d + hd:32 * d + hd + 1].to_broadcast([R36, P]), r)
                if d == 1:
                    pe.wait_ge(S("dn_dir_done"), n)
                for c in range(2):
                    s = slice(P * c, P * (c + 1))
                    for hd in range(4):
                        sel, r = row(RG, hd)
                        mm(unit[c][:, P * hd:P * (hd + 1)], sel, r[:, s], start=(hd == 0), stop=False, skip_group_check=True)
                    for hd in range(4):
                        ins = mm(unit[c][:, P * hd:P * (hd + 1)], ident, cn("neg_up" if d == 0 else "neg_lo"),
                                 start=False, stop=(hd == 3), skip_group_check=True)
                    ins.then_inc(S("dn_decay_ps"), 1)
                    for hd in range(4):
                        mm(misc[c][:, P * hd:P * (hd + 1)], dk[:, hd, s], dk[:, hd, s], start=True, stop=True)
                    for hd in range(4):
                        ins = mm(bank(c, P * hd, P * (hd + 1)), dk[:, hd, s], dq[:, hd, s], start=True, stop=True)
                    ins.then_inc(S("dn_kk_ps"), 1)
                for c in range(2):
                    pe.wait_ge(S("dn_decay"), 2 * n + c + 1)
                    for hd in range(4):
                        sel, r = row(RB, hd)
                        ins = mm(unit[c][:, P * hd:P * (hd + 1)], sel, r[:, P * c:P * (c + 1)], start=True, stop=True)
                    ins.then_inc(S("dn_beta_ps"), 1)
                for c in range(2):
                    pe.wait_ge(S("dn_lt"), 2 * n + c + 1)
                    for hd in range(4):
                        ins = mm(unit[c][:, P * hd:P * (hd + 1)], W["lt"][:, c, hd, :], ident, start=True, stop=True)
                    ins.then_inc(S("dn_a_ps"), 1)
                for v in range(1, 7):
                    m = 7 * n + v
                    for c in range(2):
                        pe.wait_ge(S("dn_t"), 2 * (m - n) - 2 + c + 1)
                        for hd in range(4):
                            ins = mm(unit[c][:, P * hd:P * (hd + 1)], W["lt"][:, c, hd, :], W["t"][:, c, hd, :],
                                     start=True, stop=True)
                        ins.then_inc(S("dn_a_ps"), 1)
                    for c in range(2):
                        pe.wait_ge(S("dn_u"), 2 * m - 2 + c + 1)
                        pe.wait_ge(S("dn_a"), 2 * m + c + 1)
                        for hd in range(4):
                            ins = mm(bank(c, P * hd, P * (hd + 1)), W["dt"][:, c, hd, :], W["u"][:, c, hd, :],
                                     start=True, stop=True)
                        if v < 6:
                            for hd in range(4):
                                ins = mm(misc[c][:, P * hd:P * (hd + 1)], W["u"][:, c, hd, :], W["dt"][:, c, hd, :],
                                         start=True, stop=True)
                        ins.then_inc(S("dn_de_ps"), 1)
                c1, c2 = first_second(d)
                s2 = slice(P * c2, P * (c2 + 1))
                pe.wait_ge(S("dn_u"), 14 * n + 14)
                for hd in range(4):
                    sel, r = row(RE, hd)
                    ins = mm(unit[0][:, P * hd:P * (hd + 1)], sel, r[:, s2], start=True, stop=True)
                ins.then_inc(S("dn_eg_ps"), 1)
                pe.wait_ge(S("dn_vb"), n + 1)
                for hd in range(4):
                    ins = mm(misc[0][:, P * hd:P * (hd + 1)], W["u"][:, c1, hd, :], W["vb"][:, c1, hd, :],
                             start=True, stop=True)
                ins.then_inc(S("dn_v1_ps"), 1)
                for hd in range(4):
                    ins = mm(bank(0, P * hd, P * (hd + 1)), W["kbg"][:, hd, :], W["u"][:, c2, hd, :], start=True, stop=True)
                ins.then_inc(S("dn_w_ps"), 1)
                pe.wait_ge(S("dn_v1"), n + 1)
                for hd in range(4):
                    ins = mm(bank(1, P * hd, P * (hd + 1)), W["kd"][:, hd, :], W["vb"][:, c1, hd, :], start=True, stop=True)
                ins.then_inc(S("dn_s_ps"), 1)
                for hd in range(4):
                    mm(oacc[:, hd, P * c1:P * (c1 + 1)], W["vb"][:, c1, hd, :], W["qk"][:, c1, hd, :],
                       start=(d == 0 and hd % 2 == 0), stop=False)
                for hd in range(4):
                    mm(misc[1][:, P * hd:P * (hd + 1)], W["u"][:, c2, hd, :], W["vb"][:, c2, hd, :],
                       start=(hd == 0), stop=False)
                pe.wait_ge(S("dn_w"), n + 1)
                pe.wait_ge(S("dn_s"), n + 1)
                for hd in range(4):
                    ins = mm(misc[1][:, P * hd:P * (hd + 1)], W["w"][:, hd, :], W["s"][:, hd, :], start=False, stop=(hd == 3))
                ins.then_inc(S("dn_v2_ps"), 1)
                pe.wait_ge(S("dn_qd"), n + 1)
                for hd in range(4):
                    mm(oacc[:, hd, s2], W["s"][:, hd, :], W["qd"][:, hd, :], start=False, stop=False)
                pe.wait_ge(S("dn_v2"), n + 1)
                for hd in range(4):
                    ins = mm(oacc[:, hd, s2], W["vb"][:, c2, hd, :], W["qk"][:, c2, hd, :], start=False,
                             stop=(d == 1 and hd % 2 == 1))
                ins.then_inc(S("dn_o_ps"), 1)

        def act_delta(ac, l, link):
            ac.preload_act_table_set(LN_EXP)
            for c in range(2):
                ac.wait_ge(S("dn_kt_ps"), 2 * l + c + 1)
                act(W["kt"][:, c, :, :], unit[c][:, :], ACT.Copy).then_inc(S("dn_kt"), 1)
            for d in range(2):
                n = 2 * l + d
                for c in range(2):
                    ac.wait_ge(S("dn_decay_ps"), 2 * n + c + 1)
                    for hd in range(4):
                        ins = act(W["dt"][:, c, hd, :], unit[c][:, P * hd:P * (hd + 1)], ACT.Exp,
                                  bias=tokd[:, 4 * c + 1, 32 * d + hd:32 * d + hd + 1])
                    ins.then_inc(S("dn_decay"), 1)
                ac.wait_ge(S("dn_w_ps"), n + 1)
                act(flat(W["w"]), bank(0, 0, 512), ACT.Copy, scale=-1.0).then_inc(S("dn_w"), 1)
                ac.wait_ge(S("dn_s_ps"), n + 1)
                act(flat(W["s"]), bank(1, 0, 512), ACT.Copy).then_inc(S("dn_s"), 1)
            ac.wait_ge(S("dn_o_ps"), 2 * l + 2)
            act_onorm(ac, 2 * l, l2, l2, misc)

        def act_onorm(ac, n, sq, out, sums):
            for k in range(2):
                act(sq[:, 512 * k:512 * (k + 1)], acc[:, 1024 + 512 * k:1536 + 512 * k], ACT.Square
                    ).then_inc(S("o_sq"), 1)
            for k in range(2):
                o = out[:, 512 * k:512 * (k + 1)]
                ac.wait_ge(S("o_ssum"), 2 * n + k + 1)
                act(o, sums[k][:, :], ACT.Ln, bias=one("eps"), scale=1.0 / P).then_inc(S("o_log"), 1)
                ac.wait_ge(S("o_log"), 2 * n + k + 1)
                act(o, o, ACT.Exp, scale=-0.5).then_inc(S("o_rms"), 1)

        def pe_onorm(pe, n, sq, sums):
            for hd in range(4):
                if hd % 2 == 0:
                    pe.wait_ge(S("o_sq"), 2 * n + hd // 2 + 1)
                ins = mm(sums[hd // 2][:, T * (hd % 2):T * (hd % 2 + 1)], ones, sq[:, T * hd:T * (hd + 1)],
                         start=(hd % 2 == 0), stop=(hd % 2 == 1))
                if hd % 2:
                    ins.then_inc(S("o_ssum"), 1)

        def dve_delta(dve, l, link):
            dve.wait_ge(S("dn_tok_ps"), l + 1)
            nc.vector.tensor_copy(tokd, misc[1][:, 0:288].rearrange("p (a b) -> p a b", b=36)).then_inc(S("dn_tok"), 1)
            for c in range(2):
                dve.wait_ge(S("dn_vt_ps"), 2 * l + c + 1)
                nc.vector.tensor_copy(W["vt"][:, c, :, :], heads(misc[c][:, :])).then_inc(S("dn_vt"), 1)
            dve.wait_ge(S("dn_kt"), 2 * l + 2)
            dve.wait_ge(S("dn_vt"), 2 * l + 2)
            dve.wait_ge(S("dn_tok"), l + 1)
            for d in range(2):
                n = 2 * l + d
                c1, c2 = first_second(d)
                col = lambda c, k: tokd[:, 4 * c + k, 32 * d:32 * d + 4].unsqueeze(2).to_broadcast([P, 4, P])
                for c in range(2):
                    tt(W["vb"][:, c, :, :], W["vt"][:, c, :, :], col(c, 0), ALU.mult)
                tt(W["kbg"], W["kt"][:, c2, :, :], col(c2, 2), ALU.mult)
                tt(W["kd"], W["kt"][:, c1, :, :], col(c1, 3), ALU.mult).then_inc(S("dn_vb"), 1)
                for c in range(2):
                    dve.wait_ge(S("dn_decay"), 2 * n + c + 1)
                    dve.wait_ge(S("dn_kk_ps"), 2 * n + c + 1)
                    dt = W["dt"][:, c, :, :]
                    tt(W["qk"][:, c, :, :], heads(bank(c, 0, 512)), dt, ALU.mult)
                    link(tt(W["lt"][:, c, :, :], heads(misc[c][:, :]), dt, ALU.mult))
                    dve.wait_ge(S("dn_beta_ps"), 2 * n + c + 1)
                    tt(W["lt"][:, c, :, :], W["lt"][:, c, :, :], heads(unit[c][:, :]), ALU.mult).then_inc(S("dn_lt"), 1)
                level = lambda v, k: cn("level", P * (2 * v + (k + d) % 2)).unsqueeze(1).to_broadcast([P, 4, P])
                eye = ident.unsqueeze(1).to_broadcast([P, 4, P])
                for v in range(7):
                    m = 7 * n + v
                    for c in range(2):
                        a, tm, um = W["dt"][:, c, :, :], W["t"][:, c, :, :], W["u"][:, c, :, :]
                        dve.wait_ge(S("dn_a_ps"), 2 * m + c + 1)
                        tt(a, heads(unit[c][:, :]), level(v, 0), ALU.mult).then_inc(S("dn_a"), 1)
                        if v == 0:
                            link(tt(um, W["lt"][:, c, :, :], level(0, 1), ALU.mult))
                            tt(um, eye, um, ALU.subtract).then_inc(S("dn_u"), 1)
                            dve.wait_ge(S("dn_a"), 2 * m + c + 1)
                            tt(tm, eye, a, ALU.subtract).then_inc(S("dn_t"), 1)
                    if v > 0:
                        for c in range(2):
                            tm, um = W["t"][:, c, :, :], W["u"][:, c, :, :]
                            dve.wait_ge(S("dn_de_ps"), 2 * (m - n - 1) + c + 1)
                            side = lambda b, odd: b.rearrange("p (k e m) -> p k e m", e=2, m=1 << v)[:, :, odd, :]
                            tm, um = (b.rearrange("p h n -> p (h n)") for b in (tm, um))
                            if v < 6:
                                tt(side(tm, d), side(tm, d), side(misc[c][:, :], d), ALU.subtract).then_inc(S("dn_t"), 1)
                            tt(side(um, 1 - d), side(um, 1 - d), side(bank(c, 0, 512), 1 - d), ALU.subtract
                               ).then_inc(S("dn_u"), 1)
                dve.wait_ge(S("dn_eg_ps"), n + 1)
                tt(W["qd"], dq[:, :, P * c2:P * (c2 + 1)], heads(unit[0][:, :]), ALU.mult).then_inc(S("dn_qd"), 1)
                dve.wait_ge(S("dn_v1_ps"), n + 1)
                nc.vector.tensor_copy(W["vb"][:, c1, :, :], heads(misc[0][:, :])).then_inc(S("dn_v1"), 1)
                dve.wait_ge(S("dn_v2_ps"), n + 1)
                nc.vector.tensor_copy(W["vb"][:, c2, :, :], heads(misc[1][:, :])).then_inc(S("dn_v2"), 1)
                dve.wait_ge(S("dn_o_ps"), n + 1)
                dve.sem_inc(S("dn_dir_done"), 1)

        sq8 = W2["sq"].rearrange("p a b -> p (a b)")

        def sbank(n, t):
            return unit[n % 2][:, 0:T] if t == 0 else bank(n % 2, 0, T)

        def lambda_init(l):
            return 0.8 - 0.6 * math.exp(-0.3 * l)

        def pe_attn(pe, l):
            pe.wait_ge(S("at_rope"), l + 1)
            pe.wait_ge(S("at_lam"), l + 1)

            def scores(n):
                hd, qb = n // 2, n % 2
                if n >= 2:
                    pe.wait_ge(S("at_exp"), 8 * l + n - 1)
                for t in range(2):
                    r = slice(64 * t, 64 * (t + 1))
                    ins = mm(sbank(n, t), B["qk"][r, hd, P * qb:P * (qb + 1)], B["qk"][r, 4 + hd, :],
                             start=True, stop=True)
                ins.then_inc(S("at_s_ps"), 1)

            scores(0)
            scores(1)
            pe_onorm(pe, 2 * l, l2, misc)
            pe.wait_ge(S("yb_done"), l + 1)
            for n in range(8):
                hd, qb = n // 2, n % 2
                if n + 2 < 8:
                    scores(n + 2)
                pe.wait_ge(S("at_a"), 8 * l + n + 1)
                if n >= 2:
                    pe.wait_ge(S("at_at"), 8 * l + n - 1)
                for kb in range(2):
                    ins = nc.tensor.transpose(misc[n % 2][:, P * kb:P * (kb + 1)], W2["a"][:, n % 2, P * kb:P * (kb + 1)],
                                              ident)
                ins.then_inc(S("at_at_ps"), 1)
                pe.wait_ge(S("at_at"), 8 * l + n + 1)
                for kb in range(2):
                    ins = mm(oacc[:, hd, P * qb:P * (qb + 1)], B["vt"][:, kb, P * hd:P * (hd + 1)],
                             W2["at"][:, n % 2, P * kb:P * (kb + 1)], start=(kb == 0), stop=(kb == 1))
                ins.then_inc(S("at_o_ps"), 1)
            pe_onorm(pe, 2 * l + 1, sq8, unit)
            if l == 0:
                pe_mod(pe, 1)

        def act_attn(ac, l, link):

            def exps(n):
                ac.wait_ge(S("at_max"), 8 * l + n + 1)
                if n >= 2:
                    ac.wait_ge(S("at_a"), 8 * l + n - 1)
                for t in range(2):
                    ins = act(W2["e"][:, n % 2, t, :], sbank(n, t), ACT.Exp, scale=0.125,
                              bias=W2["st"][:, n, 2 + t:3 + t], accum_out=W2["st"][:, n, 4 + t:5 + t])
                ins.then_inc(S("at_exp"), 1)

            exps(0)
            for n in range(8):
                if n + 1 < 8:
                    exps(n + 1)
                ac.wait_ge(S("at_at_ps"), 8 * l + n + 1)
                if n >= 2:
                    ac.wait_ge(S("at_o_ps"), 8 * l + n - 1)
                act(W2["at"][:, n % 2, :], misc[n % 2][:, 0:T], ACT.Copy).then_inc(S("at_at"), 1)
            ac.wait_ge(S("at_o_ps"), 8 * l + 8)
            act_onorm(ac, 2 * l + 1, sq8, sq8, unit)

        def dve_attn(dve, l, link):
            lam, st = lam8, W2["st"]

            def maximum(n):
                dve.wait_ge(S("at_s_ps"), 8 * l + n + 1)
                for t in range(2):
                    ins = nc.vector.tensor_reduce(st[:, n, t:t + 1], sbank(n, t), AX.X, ALU.max)
                link(ins)
                ts(st[:, n, 2:4], st[:, n, 0:2], -0.125, None, ALU.mult).then_inc(S("at_max"), 1)

            maximum(0)
            maximum(1)
            dve.wait_ge(S("o_rms"), 4 * l + 2)
            yb = dn[:, 0:4, :].rearrange("p a b -> p (a b)")
            link(stt(yb, acc[:, 1024:2048], pr("dn_gain", l), l2, ALU.mult, ALU.mult))
            tt(yb, yb, flat(B["z"]), ALU.mult).then_inc(S("yb_done"), 1)
            for n in range(8):
                dve.wait_ge(S("at_exp"), 8 * l + n + 1)
                link(nc.vector.reciprocal(st[:, n, 6:8], st[:, n, 4:6]))
                link(tt(st[:, n, 7:8], st[:, n, 7:8], lam[:, 5:6], ALU.mult))
                if n >= 2:
                    dve.wait_ge(S("at_at_ps"), 8 * l + n - 1)
                a = W2["a"][:, n % 2, :]
                link(ts(a, W2["e"][:, n % 2, 0, :], st[:, n, 6:7], None, ALU.mult))
                stt(a, W2["e"][:, n % 2, 1, :], st[:, n, 7:8], a, ALU.mult, ALU.add).then_inc(S("at_a"), 1)
                if n + 2 < 8:
                    maximum(n + 2)
            for k in range(2):
                dve.wait_ge(S("o_rms"), 4 * l + k + 3)
                s = slice(512 * k, 512 * (k + 1))
                stt(flat(B["ya"])[:, s], acc[:, 1024 + 512 * k:1536 + 512 * k], lam[:, 6:7], sq8[:, s],
                    ALU.mult, ALU.mult).then_inc(S("ya_done"), 1)

        def pe_merge(pe, l):
            pe_out(pe, f"bra_{l}")
            pe_units(pe, CH0[f"ga_{l}"], U0[f"ga_{l}"], 4)
            pe.wait_ge(S("merge_a"), 4 * l + 4)
            pe_out(pe, f"brb_{l}")
            pe_units(pe, CH0[f"gb_{l}"], U0[f"gb_{l}"], 4)
            pe.wait_ge(S("merged"), 4 * l + 4)
            pe_out(pe, f"out2_{l}")

        def ya_pair(j):
            return B["ya"][:, 2 * j:2 * j + 2, :]

        def yb_pair(j):
            return dn[:, 2 * j:2 * j + 2, :]

        def merged_pair(j):
            return merged[:, 2 * j:2 * j + 2, :]

        def act_gates(ac, stage, k):
            for j in range(4):
                c, n = CH0[stage] + j, U0[stage] + j
                if j < 3:
                    ahead(act_split, ac, c)
                done_after(ac, c)
                act(gate[:, k + 2 * j:k + 2 * j + 2, :], unit[n % 2][:, :], ACT.Sigmoid).then_inc(S("unit_free"), 1)

        def act_merge(ac, l):
            act_lead(ac, f"bra_{l}", ya_pair, lambda j: ac.wait_ge(S("ya_done"), 2 * l + j + 1))
            epoch(act_split, ac, CH0[f"bra_{l}"])
            ac.preload_act_table(ACT.Sigmoid)
            act_out(ac, f"bra_{l}", ya_pair)
            act_lead(ac, f"brb_{l}", yb_pair)
            act_gates(ac, f"ga_{l}", 0)
            ahead(act_split, ac, END[f"ga_{l}"] - 1)
            act_out(ac, f"brb_{l}", yb_pair)
            act_gates(ac, f"gb_{l}", 8)
            ready = lambda j: ac.wait_ge(S("merged"), 4 * l + j + 1)
            act_lead(ac, f"out2_{l}", merged_pair, ready)
            ahead(act_split, ac, END[f"gb_{l}"] - 1)
            act_out(ac, f"out2_{l}", merged_pair, ready)

        def dve_merge(dve, l, link):
            dve.wait_ge(S("ya_done"), 2 * l + 2)
            dve_lead(dve, f"bra_{l}", ya_pair)
            epoch(dve_split, dve, CH0[f"bra_{l}"])
            dve_out(dve, f"bra_{l}", ya_pair)
            ahead(dve_split, dve, END[f"bra_{l}"] - 1)
            dve_lead(dve, f"brb_{l}", yb_pair)
            for q in range(4):
                s = slice(2 * q, 2 * q + 2)
                if q < 3:
                    ahead(dve_split, dve, CH0[f"ga_{l}"] + q)
                dve.wait_ge(S("unit_free"), U0[f"ga_{l}"] + q + 3)
                tt(merged[:, s, :], acc8[:, s, :], gate[:, s, :], ALU.mult).then_inc(S("merge_a"), 1)
            ahead(dve_split, dve, END[f"ga_{l}"] - 1)
            dve_out(dve, f"brb_{l}", yb_pair)
            ahead(dve_split, dve, END[f"brb_{l}"] - 1)
            for q in range(4):
                s = slice(2 * q, 2 * q + 2)
                m = tmp[:, 2 * (q % 2):2 * (q % 2) + 2, :]
                if q < 3:
                    ahead(dve_split, dve, CH0[f"gb_{l}"] + q)
                dve.wait_ge(S("unit_free"), U0[f"gb_{l}"] + q + 3)
                link(tt(m, acc8[:, s, :], gate[:, 8 + 2 * q:10 + 2 * q, :], ALU.mult))
                tt(merged[:, s, :], merged[:, s, :], m, ALU.add).then_inc(S("merged"), 1)
            dve.wait_ge(S("merged"), 4 * l + 4)
            dve_lead(dve, f"out2_{l}", merged_pair)
            ahead(dve_split, dve, END[f"gb_{l}"] - 1)
            dve_out(dve, f"out2_{l}", merged_pair)

        M = carve(keep, [("r", (2, 2, T)), ("hid", (2, 2, T))])

        def pe_mlp(pe, l):
            c0, n0, b0 = CH0[f"mlp_{l}"], U0[f"mlp_{l}"], B0[f"mlp_{l}"]
            pe_unit(pe, c0, n0, h_count=4 * HU[f"pre2_{l}"])
            pe_unit(pe, c0 + 1, n0 + 1)
            pe_down(pe, c0 + 2, b0, True, False)
            with pe.Fori(0, 2) as i:
                for k in range(6):
                    pe_unit(pe, c0 + 3 + 2 * k, n0 + 2 + k, i, 12, 6)
                    pe_down(pe, c0 + 4 + 2 * k, b0 + 1 + k, False, False, i, 12, 6)
            pe_unit(pe, c0 + 27, n0 + 14)
            pe_down(pe, c0 + 28, b0 + 13, False, False)
            pe_unit(pe, c0 + 29, n0 + 15)
            pe_down(pe, c0 + 30, b0 + 14, False, False)
            pe_down(pe, c0 + 31, b0 + 15, False, True)

        def act_mlp(ac, l):
            c0, n0, b0, f0 = CH0[f"mlp_{l}"], U0[f"mlp_{l}"], B0[f"mlp_{l}"], 16 * l

            def relu(u, i=None):
                c = c0 + max(2 * u - 1, 0)
                ahead(act_split, ac, c, i, 12)
                done_after(ac, c, i, 12)
                if i is not None or u >= 2:
                    ac.wait_ge(S("mlp_square"), at(i, 6, f0 + u - 1))
                act(M["r"][:, u % 2, :, :], unit[(n0 + u) % 2][:, :], ACT.Relu).then_inc(S("unit_free"), 1)

            def moving(u, i=None):
                ac.wait_ge(S("mlp_square"), at(i, 6, f0 + u + 1))
                act_moving(ac, b0 + u, M["hid"][:, u % 2, :, :])

            relu(0)
            moving(0)

            def unit_and_down(u, i=None):
                relu(u, i)
                c = c0 + 2 * u
                if u < 15:
                    ahead(act_split, ac, c, i, 12)
                    done_after(ac, c, i, 12)
                    moving(u, i)
                else:
                    moving(u)
                    ahead(act_split, ac, c)

            with ac.Fori(0, 2) as i:
                for u in range(1, 7):
                    unit_and_down(u, i)
            for u in range(13, 16):
                unit_and_down(u)

        def dve_mlp(dve, l):
            c0, n0, b0, f0 = CH0[f"mlp_{l}"], U0[f"mlp_{l}"], B0[f"mlp_{l}"], 16 * l

            def square(u, i=None):
                ahead(dve_split, dve, c0 + max(2 * u - 1, 0), i, 12)
                dve.wait_ge(S("unit_free"), at(i, 6, n0 + u + 3))
                if i is not None or u >= 2:
                    dve.wait_ge(S("mv_ready"), at(i, 6, b0 + u - 1))
                r = M["r"][:, u % 2, :, :]
                tt(M["hid"][:, u % 2, :, :], r, r, ALU.mult).then_inc(S("mlp_square"), 1)

            def moving(u, i=None):
                dve.wait_ge(S("mlp_square"), at(i, 6, f0 + u + 1))
                dve_moving(dve, b0 + u, M["hid"][:, u % 2, :, :], i, 6)

            square(0)
            moving(0)

            def unit_and_down(u, i=None):
                square(u, i)
                if u < 15:
                    ahead(dve_split, dve, c0 + 2 * u, i, 12)
                    moving(u, i)
                else:
                    moving(u)
                    ahead(dve_split, dve, c0 + 2 * u)

            with dve.Fori(0, 2) as i:
                for u in range(1, 7):
                    unit_and_down(u, i)
            for u in range(13, 16):
                unit_and_down(u)

        block = ctx.enter_context(nc.Block())

        @block.sync
        def _(sp):
            def load(c):
                sp.dma_start(raw[c % RAW][:, :], w_in[c]).then_inc(loaded[c % RAW], 16)
            sp.dma_start(x[:, :, :], x_in).then_inc(S("x_loaded"), 16)
            for c in range(RAW):
                load(c)
            turns = NCHUNK // RAW
            with sp.Fori(1, turns) as i:
                for s in range(RAW):
                    sp.wait_ge(S("chunk_split"), i * (2 * RAW) + (2 * (s - RAW) + 2))
                    sp.dma_start(raw[s][:, :], w_in[bass.ds(i * RAW + s, 1)].rearrange("o p n -> p (o n)")
                                 ).then_inc(loaded[s], 16)
            for c in range(turns * RAW, NCHUNK):
                sp.wait_ge(S("chunk_split"), 2 * (c - RAW) + 2)
                load(c)
            for q in range(4):
                sp.wait_ge(S("x_ready"), 4 * XU["res2_1"] + q + 1)
                sp.dma_start(out[:, 2 * q:2 * q + 2, :], x[:, 2 * q:2 * q + 2, :]).then_inc(S("stored"), 16)
            sp.wait_ge(S("stored"), 64)

        @block.gpsimd
        def _(pool):
            pool_ada(pool)

        @block.tensor
        def _(pe):
            pe.wait_ge(S("con_loaded"), 16)
            pe_norm(pe, "mix_pre0")
            pe.wait_ge(S("par_loaded"), 16)
            pe_ssd(pe)
            pe_norm(pe, "mix_post0")
            pe_norm(pe, "ffn_pre0")
            pe_ffn(pe, 0)
            pe_norm(pe, "ffn_post0")
            pe_norm(pe, "mix_pre1")
            pe_lru(pe)
            pe_norm(pe, "mix_post1")
            pe_norm(pe, "ffn_pre1")
            pe_ffn(pe, 1)
            pe_norm(pe, "ffn_post1")
            for l in range(2):
                pe_b2_in(pe, l)
                pe_delta(pe, l)
                pe_attn(pe, l)
                pe_merge(pe, l)
                pe_norm(pe, f"pre2_{l}")
                pe_mlp(pe, l)

        @block.scalar
        def _(ac):
            ac.dma_start(con[:, 0:CON_FIRST], con_in[:, 0:CON_FIRST]).then_inc(S("con_loaded"), 16)
            ac.dma_start(par[:, :], par_in).then_inc(S("par_loaded"), 16)
            link = Chain(ac, S("act_link"))

            def from_acc(stage):
                return lambda q: done_after(ac, END[stage] - 1)

            def split_after(stage):
                return lambda: ahead(act_split, ac, END[stage] - 1)

            ac.wait_ge(S("con_loaded"), 16)
            act_norm(ac, "mix_pre0", x, lambda q: ac.wait_ge(S("x_loaded"), 16))
            act_h(ac, "mix_pre0")
            epoch(act_split, ac, 0)
            ac.wait_ge(S("par_loaded"), 16)
            ac.dma_start(con[:, CON_FIRST:NCON], con_in[:, CON_FIRST:NCON]).then_inc(S("con_rest"), 16)
            act(cact[:, :], par[:, PAR["c"]:PAR["c"] + 8], ACT.Silu).then_inc(S("c_act"), 1)
            act_ssd(ac, link)
            act_norm(ac, "mix_post0", acc8, from_acc("ssd_out"), split_after("ssd_out"))
            act_norm(ac, "ffn_pre0", x, x_ready(ac, "mix_post0"))
            act_h(ac, "ffn_pre0")
            act_ffn(ac, 0)
            act_norm(ac, "ffn_post0", acc8, from_acc("ffn0"), split_after("ffn0"))
            act_norm(ac, "mix_pre1", x, x_ready(ac, "ffn_post0"))
            act_h(ac, "mix_pre1")
            act_lru(ac, link)
            act_norm(ac, "mix_post1", R["m"], lambda q: ac.wait_ge(S("lru_m"), q + 1))
            act_norm(ac, "ffn_pre1", x, x_ready(ac, "mix_post1"))
            act_h(ac, "ffn_pre1")
            act_ffn(ac, 1)
            act_norm(ac, "ffn_post1", acc8, from_acc("ffn1"), split_after("ffn1"))
            for l in range(2):
                act_b2_in(ac, l, link)
                act_delta(ac, l, link)
                act_attn(ac, l, link)
                act_merge(ac, l)
                act_norm(ac, f"pre2_{l}", x, x_ready(ac, f"res1_{l}"))
                act_h(ac, f"pre2_{l}")
                act_mlp(ac, l)
                ahead(act_split, ac, END[f"mlp_{l}"] - 1)

        @block.vector
        def _(dve):
            link = Chain(dve, S("dve_link"))
            dve.sem_inc(S("unit_free"), 2)
            dve.sem_inc(S("x_ready"), 4)
            dve.wait_ge(S("par_loaded"), 16)
            dve.wait_ge(S("x_loaded"), 16)
            block1 = lambda name, l: (lambda t: pr(name, 8 * l + t))
            dve_pre(dve, "mix_pre0", block1("mix_pre", 0))
            epoch(dve_split, dve, 0)
            dve_ssd(dve, link)
            ahead(dve_split, dve, END["ssd_out"] - 1)
            dve_post(dve, link, "mix_post0", block1("mix_post", 0), acc8)
            dve_pre(dve, "ffn_pre0", block1("ffn_pre", 0))
            dve_ffn(dve, 0, link)
            ahead(dve_split, dve, END["ffn0"] - 1)
            dve_post(dve, link, "ffn_post0", block1("ffn_post", 0), acc8)
            dve_pre(dve, "mix_pre1", block1("mix_pre", 1))
            dve_lru(dve, link)
            dve_post(dve, link, "mix_post1", block1("mix_post", 1), R["m"])
            dve_pre(dve, "ffn_pre1", block1("ffn_pre", 1))
            dve_mod(dve, link, 0)
            dve_ffn(dve, 1, link)
            ahead(dve_split, dve, END["ffn1"] - 1)
            dve_post(dve, link, "ffn_post1", block1("ffn_post", 1), acc8)
            for l in range(2):
                gain = lambda k: (lambda t: mod2[:, l, k + t:k + t + 1])
                dve_b2_in(dve, l, link)
                dve_delta(dve, l, link)
                dve_attn(dve, l, link)
                dve_merge(dve, l, link)
                dve_residual(dve, f"res1_{l}", gain(16), f"out2_{l}")
                ahead(dve_split, dve, END[f"out2_{l}"] - 1)
                dve_modulated(dve, link, f"pre2_{l}", l, 1)
                if l == 0:
                    dve_mod(dve, link, 1)
                dve_mlp(dve, l)
                dve_residual(dve, f"res2_{l}", gain(40), f"mlp_{l}")
                ahead(dve_split, dve, END[f"mlp_{l}"] - 1)


def arrays_of(a):
    ada = np.ascontiguousarray(
        a["ada_w_2"].reshape(2, 8, P, ADA_N, AW).transpose(0, 3, 2, 1, 4)).reshape(2 * ADA_N, P, 8, AW)
    return {
        "x_in": np.ascontiguousarray(a["x"][0].T.reshape(DT_, P, T).transpose(1, 0, 2)),
        "w_in": stream(a),
        "gates_in": lru_gates(a),
        "ada_in": ada,
        "par_in": parameters(a),
        "con_in": constants(),
    }


def kernel(**inputs):
    import concourse.bacc as bacc
    from concourse.bass_utils import run_bass_kernel_spmd

    arrays = arrays_of({k: np.asarray(v) for k, v in inputs.items()})
    nc = bacc.Bacc("TRN2", target_bir_lowering=False, num_devices=1)
    aps = [nc.dram_tensor(n, v.shape, mybir.dt.from_np(v.dtype), kind="ExternalInput").ap() for n, v in arrays.items()]
    out = nc.dram_tensor("out", (P, DT_, T), mybir.dt.float32, kind="ExternalOutput").ap()
    build(nc, *aps, out)
    r = run_bass_kernel_spmd(nc, [arrays], core_ids=[0])
    y = r.results[0]["out"]
    return np.ascontiguousarray(y.transpose(1, 0, 2).reshape(D, T).T)[None]
```
